# Optimizing a Trainium2 kernel written in Bass

```python
import jax, jax.numpy as jnp
from jax import lax
import numpy as np

D_MODEL = 1024
BATCH = 1
SEQ = 256
DEPTH = 1

GRID_W = 64
CTX_LEN = 256
HG_HEADS = 4
HG_DK = 128
HG_DV = 128
GLA_HEADS = 4
GLA_DK = 64
GLA_DV = 128
GLA_GATE_RANK = 16
GLA_GATE_NORM = 16.0
HG_KW = HG_HEADS * HG_DK
HG_VW = HG_HEADS * HG_DV
GLA_KW = GLA_HEADS * GLA_DK
GLA_VW = GLA_HEADS * GLA_DV
D_MIX = HG_VW + GLA_VW
CHUNK = 64
PEER_HEADS = 8
PEER_NKEYS = 128
PEER_EXPERTS = PEER_NKEYS * PEER_NKEYS
PEER_DQ = 256
PEER_TOPK = 16
PEER_BLOCK = 128
ALPHA = (2.0 * DEPTH) ** 0.25
BETA = (8.0 * DEPTH) ** -0.25
EPS = 1e-6
LB_FLOOR = 1e-30
IN_SPLITS = (HG_KW, HG_KW, HG_KW, HG_VW, HG_VW, GLA_KW, GLA_KW, GLA_VW, GLA_VW, GLA_GATE_RANK, GLA_GATE_RANK)
D_IN = sum(IN_SPLITS)
IN_SPLIT_POINTS = [int(p) for p in np.cumsum(IN_SPLITS)[:-1]]


def layer_norm(x, gamma=None, beta=None):
    xf = x.astype(jnp.float32)
    mu = jnp.mean(xf, axis=-1, keepdims=True)
    var = jnp.mean(jnp.square(xf - mu), axis=-1, keepdims=True)
    y = (xf - mu) * lax.rsqrt(var + EPS)
    if gamma is not None:
        y = y * gamma.astype(jnp.float32) + beta.astype(jnp.float32)
    return y.astype(x.dtype)

def modulate(x, shift, scale):
    return layer_norm(x) * (1.0 + scale) + shift

def heads(t, n):
    B, L, _ = t.shape
    return t.reshape(B, L, n, -1).transpose(0, 2, 1, 3).astype(jnp.float32)

def head_rms_merge(o, gain):
    o = o * lax.rsqrt(jnp.mean(o * o, axis=-1, keepdims=True) + EPS) * gain.astype(jnp.float32)
    B, n, L, d = o.shape
    return o.transpose(0, 2, 1, 3).reshape(B, L, n * d)

def to_col_major(t, rows):
    B, L, C = t.shape
    return t.reshape(B, rows, GRID_W, C).transpose(0, 2, 1, 3).reshape(B, L, C)

def from_col_major(t, rows):
    B, L, C = t.shape
    return t.reshape(B, GRID_W, rows, C).transpose(0, 2, 1, 3).reshape(B, L, C)

def chunk_scan(q, k, v, log_a, s0):
    B, H, L, dk = q.shape
    dv = v.shape[-1]
    n = L // CHUNK

    def split(t):
        return jnp.moveaxis(t.reshape(B, H, n, CHUNK, t.shape[-1]), 2, 0)

    incl = jnp.tril(jnp.ones((CHUNK, CHUNK), dtype=bool))[:, :, None]

    def step(s, inp):
        qc, kc, vc, ac = inp
        b = jnp.cumsum(ac, axis=-2)
        rel = b[..., :, None, :] - b[..., None, :, :]
        decay = jnp.where(incl, jnp.exp(jnp.minimum(rel, 0.0)), 0.0)
        scores = jnp.einsum('bhtk,bhsk,bhtsk->bhts', qc, kc, decay)
        o = jnp.einsum('bhts,bhsv->bhtv', scores, vc) + jnp.einsum('bhtk,bhkv->bhtv', qc * jnp.exp(b), s)
        b_end = b[..., -1:, :]
        s_new = jnp.exp(b_end[..., 0, :])[..., None] * s + jnp.einsum('bhsk,bhsv->bhkv', kc * jnp.exp(b_end - b), vc)
        return s_new, o

    s_end, o = lax.scan(step, s0, (split(q), split(k), split(v), split(log_a)))
    return jnp.moveaxis(o, 0, 2).reshape(B, H, L, dv), s_end

def scan_two_way(ctx_parts, lat_parts):
    qc, vc, kcf, acf, kcb, acb = ctx_parts
    ql, vl, klf, alf, klb, alb = lat_parts
    B, H, _, dk = qc.shape
    s0 = jnp.zeros((B, H, dk, vc.shape[-1]), jnp.float32)
    flip = lambda t: jnp.flip(t, axis=2)
    oc_f, sc_f = chunk_scan(qc, kcf, vc, acf, s0)
    ol_f, _ = chunk_scan(ql, klf, vl, alf, sc_f)
    oc_b, sc_b = chunk_scan(flip(qc), flip(kcb), flip(vc), flip(acb), s0)
    ol_b, _ = chunk_scan(flip(ql), flip(klb), flip(vl), flip(alb), sc_b)
    return oc_f + flip(oc_b), ol_f + flip(ol_b)

def hgrn2_inputs(hq, hff, hfb, hi, lb_f, lb_b):
    def gate(z, lb):
        z = z.astype(jnp.float32)
        log_lb = jnp.log(jnp.maximum(lb, LB_FLOOR))
        log_f = jnp.logaddexp(log_lb, jnp.log1p(-lb) + jax.nn.log_sigmoid(z))
        k = (1.0 - lb) * jax.nn.sigmoid(-z)
        return heads(k, HG_HEADS), heads(log_f, HG_HEADS)
    kf, af = gate(hff, lb_f)
    kb, ab = gate(hfb, lb_b)
    return (heads(hq, HG_HEADS), heads(hi, HG_HEADS), kf, af, kb, ab)

def gla_inputs(gq, gk, gv, glf, glb, w_gk2, b_gk):
    def gate(r, w, b):
        la = jax.nn.log_sigmoid((r @ w + b).astype(jnp.float32)) / GLA_GATE_NORM
        return heads(la, GLA_HEADS)
    k = heads(gk, GLA_HEADS)
    q = heads(gq, GLA_HEADS) * (GLA_DK ** -0.5)
    return (q, heads(gv, GLA_HEADS), k, gate(glf, w_gk2[0], b_gk[0]), k, gate(glb, w_gk2[1], b_gk[1]))

def token_mixer(u_c, u_l, rows, lb_f, lb_b, w_gk2, b_gk, hg_gain, gla_gain):
    pc = jnp.split(u_c, IN_SPLIT_POINTS, axis=-1)
    pl = jnp.split(u_l, IN_SPLIT_POINTS, axis=-1)
    a_c, a_l = scan_two_way(hgrn2_inputs(pc[0], pc[1], pc[2], pc[3], lb_f, lb_b),
                            hgrn2_inputs(pl[0], pl[1], pl[2], pl[3], lb_f, lb_b))
    out_a_c = head_rms_merge(a_c, hg_gain).astype(u_c.dtype) * jax.nn.silu(pc[4])
    out_a_l = head_rms_merge(a_l, hg_gain).astype(u_l.dtype) * jax.nn.silu(pl[4])
    gl = [to_col_major(pl[j], rows) for j in (5, 6, 7, 9, 10)]
    b_c, b_l = scan_two_way(gla_inputs(pc[5], pc[6], pc[7], pc[9], pc[10], w_gk2, b_gk),
                            gla_inputs(gl[0], gl[1], gl[2], gl[3], gl[4], w_gk2, b_gk))
    out_b_c = head_rms_merge(b_c, gla_gain).astype(u_c.dtype) * jax.nn.silu(pc[8])
    out_b_l = from_col_major(head_rms_merge(b_l, gla_gain), rows).astype(u_l.dtype) * jax.nn.silu(pl[8])
    return (jnp.concatenate([out_a_c, out_b_c], axis=-1), jnp.concatenate([out_a_l, out_b_l], axis=-1))

def peer(h, w_query, sub_keys, expert_u, expert_v):
    B, L, D = h.shape
    tok = h.reshape(-1, PEER_BLOCK, D)
    k1 = sub_keys[0].astype(jnp.float32)
    k2 = sub_keys[1].astype(jnp.float32)

    def block(t):
        q = (t @ w_query).reshape(PEER_BLOCK, PEER_HEADS, 2, PEER_DQ // 2).astype(jnp.float32)
        s1 = jnp.einsum('thd,nd->thn', q[:, :, 0], k1)
        s2 = jnp.einsum('thd,nd->thn', q[:, :, 1], k2)
        v1, i1 = lax.top_k(s1, PEER_TOPK)
        v2, i2 = lax.top_k(s2, PEER_TOPK)
        cand_s = (v1[..., :, None] + v2[..., None, :]).reshape(PEER_BLOCK, PEER_HEADS, PEER_TOPK * PEER_TOPK)
        cand_i = (i1[..., :, None] * PEER_NKEYS + i2[..., None, :]).reshape(PEER_BLOCK, PEER_HEADS, PEER_TOPK * PEER_TOPK)
        top_s, pos = lax.top_k(cand_s, PEER_TOPK)
        idx = jnp.take_along_axis(cand_i, pos, axis=-1)
        g = jax.nn.softmax(top_s, axis=-1)
        act = jax.nn.gelu(jnp.einsum('thkd,td->thk', expert_u[idx], t).astype(jnp.float32))
        return jnp.einsum('thk,thkd->td', (g * act).astype(t.dtype), expert_v[idx])

    return lax.map(block, tok).reshape(B, L, D)

def first_inputs(seed: int = 0) -> dict:
    key = jax.random.key(seed)
    ks = jax.random.split(key, 20)
    f32 = jnp.float32
    nrm = lambda k, shape, s: jax.random.normal(k, shape, f32) * s
    return {
        'x': nrm(ks[0], (BATCH, SEQ, D_MODEL), 1.0),
        'c': nrm(ks[1], (BATCH, D_MODEL), 1.0),
        'ctx': nrm(ks[2], (BATCH, CTX_LEN, D_MODEL), 1.0),
        'c_ctx': nrm(ks[3], (D_MODEL,), 1.0),
        'w_ada': nrm(ks[4], (DEPTH, D_MODEL, 6 * D_MODEL), 0.5 * D_MODEL ** -0.5),
        'b_ada': nrm(ks[5], (DEPTH, 6 * D_MODEL), 0.01),
        'w_in': nrm(ks[6], (DEPTH, D_MODEL, D_IN), D_MODEL ** -0.5),
        'w_gk2': nrm(ks[7], (DEPTH, 2, GLA_GATE_RANK, GLA_KW), GLA_GATE_RANK ** -0.5),
        'b_gk': nrm(ks[8], (DEPTH, 2, GLA_KW), 0.01),
        'hg_lower_bounds': nrm(ks[9], (2, DEPTH, HG_KW), 0.1),
        'hg_norm': 1.0 + nrm(ks[10], (DEPTH, HG_DV), 0.01),
        'gla_norm': 1.0 + nrm(ks[11], (DEPTH, GLA_DV), 0.01),
        'w_out': nrm(ks[12], (DEPTH, D_MIX, D_MODEL), BETA * D_MIX ** -0.5),
        'ln_gamma': 1.0 + nrm(ks[13], (DEPTH, 2, D_MODEL), 0.01),
        'ln_beta': nrm(ks[14], (DEPTH, 2, D_MODEL), 0.01),
        'peer_w_query': nrm(ks[15], (DEPTH, D_MODEL, PEER_HEADS * PEER_DQ), D_MODEL ** -0.5),
        'peer_sub_keys': nrm(ks[16], (DEPTH, 2, PEER_NKEYS, PEER_DQ // 2), (PEER_DQ // 2) ** -0.5),
        'peer_u': nrm(ks[17], (DEPTH, PEER_EXPERTS, D_MODEL), D_MODEL ** -0.5),
        'peer_v': nrm(ks[18], (DEPTH, PEER_EXPERTS, D_MODEL), BETA),
    }

def first_block(x, c, ctx, c_ctx, w_ada, b_ada, w_in, w_gk2, b_gk, hg_lower_bounds, hg_norm, gla_norm,
              w_out, ln_gamma, ln_beta, peer_w_query, peer_sub_keys, peer_u, peer_v):
    rows = x.shape[1] // GRID_W
    sm = jax.nn.softmax(hg_lower_bounds.astype(jnp.float32), axis=1)
    lb_all = jnp.clip(jnp.cumsum(sm, axis=1) - sm[:, :1], 0.0, 1.0 - 1e-6)
    xc = ctx
    for i in range(DEPTH):
        last = i == DEPTH - 1
        m_l = jax.nn.silu(c) @ w_ada[i] + b_ada[i]
        m_c = jax.nn.silu(c_ctx) @ w_ada[i] + b_ada[i]
        sh1_l, sc1_l, g1_l, sh2_l, sc2_l, g2_l = [t[:, None, :] for t in jnp.split(m_l, 6, axis=-1)]
        sh1_c, sc1_c, g1_c, sh2_c, sc2_c, g2_c = jnp.split(m_c, 6, axis=-1)
        u_l = modulate(x, sh1_l, sc1_l) @ w_in[i]
        u_c = modulate(xc, sh1_c, sc1_c) @ w_in[i]
        mix_c, mix_l = token_mixer(u_c, u_l, rows, lb_all[0, i], lb_all[1, i], w_gk2[i], b_gk[i],
                                   hg_norm[i], gla_norm[i])
        x = layer_norm(ALPHA * x + g1_l * (mix_l @ w_out[i]), ln_gamma[i, 0], ln_beta[i, 0])
        if not last:
            xc = layer_norm(ALPHA * xc + g1_c * (mix_c @ w_out[i]), ln_gamma[i, 0], ln_beta[i, 0])
        y_l = peer(modulate(x, sh2_l, sc2_l), peer_w_query[i], peer_sub_keys[i], peer_u[i], peer_v[i])
        x = layer_norm(ALPHA * x + g2_l * y_l, ln_gamma[i, 1], ln_beta[i, 1])
        if not last:
            y_c = peer(modulate(xc, sh2_c, sc2_c), peer_w_query[i], peer_sub_keys[i], peer_u[i], peer_v[i])
            xc = layer_norm(ALPHA * xc + g2_c * y_c, ln_gamma[i, 1], ln_beta[i, 1])
    return x


DEPTH_2 = 2

N_META = 16
BLOCK = 128
SSD_HEADS = 8
SSD_HEAD_DIM = 64
SSD_D = SSD_HEADS * SSD_HEAD_DIM
SSD_GROUPS = 2
SSD_STATE = 64
SSD_CONV = 4
SSD_CONV_DIM = SSD_D + 2 * SSD_GROUPS * SSD_STATE
FOX_HEADS = 4
FOX_HEAD_DIM = 64
FOX_D = FOX_HEADS * FOX_HEAD_DIM
MLA_HEADS = 4
MLA_Q_LORA = 256
MLA_KV_LORA = 128
MLA_NOPE = 64
MLA_ROPE = 32
MLA_V = 64
MLA_D = MLA_HEADS * MLA_V
ROPE_THETA = 10000.0
D_MIX_2 = SSD_D + FOX_D + MLA_D
IN_SIZES = [SSD_D, SSD_CONV_DIM, SSD_HEADS,
            FOX_D, FOX_D, FOX_D, FOX_HEADS,
            MLA_Q_LORA, MLA_KV_LORA, MLA_ROPE]
N_IN = sum(IN_SIZES)
IN_SPLITS_2 = [int(s) for s in np.cumsum(IN_SIZES)[:-1]]
D_FF = 2816
ALPHA_2 = (2 * DEPTH_2) ** 0.25
BETA_2 = (8 * DEPTH_2) ** -0.25
EPS_2 = 1e-5


def layer_norm_2(x, g, b):
    xf = x.astype(jnp.float32)
    mu = jnp.mean(xf, -1, keepdims=True)
    var = jnp.mean(jnp.square(xf - mu), -1, keepdims=True)
    return ((xf - mu) * lax.rsqrt(var + EPS_2) * g + b).astype(x.dtype)

def rms_norm(x, g):
    xf = x.astype(jnp.float32)
    y = xf * lax.rsqrt(jnp.mean(jnp.square(xf), -1, keepdims=True) + EPS_2)
    return (y * g).astype(x.dtype)

def swiglu(x, w_gate, w_up, w_down):
    return (jax.nn.silu(x @ w_gate) * (x @ w_up)) @ w_down

def rope(x, cos, sin):
    x1, x2 = jnp.split(x.astype(jnp.float32), 2, axis=-1)
    return jnp.concatenate([x1 * cos - x2 * sin, x2 * cos + x1 * sin], -1).astype(x.dtype)

def block_edges(total):
    return sorted(set([0] + list(range(N_META, total, BLOCK)) + [total]))

def blocked_causal_attention(logits_fn, v):
    total = v.shape[1]
    outs = []
    edges = block_edges(total)
    for q0, q1 in zip(edges[:-1], edges[1:]):
        s = logits_fn(q0, q1).astype(jnp.float32)
        causal = jnp.arange(q1)[None, :] <= jnp.arange(q0, q1)[:, None]
        s = jnp.where(causal, s, -jnp.inf)
        p = jax.nn.softmax(s, axis=-1).astype(v.dtype)
        outs.append(jnp.einsum('bhqk,bkhd->bqhd', p, v[:, :q1]))
    return jnp.concatenate(outs, axis=1)

def causal_depthwise_conv(x, w, bias):
    out = lax.conv_general_dilated(
        x, w[:, None, :], window_strides=(1,), padding=[(SSD_CONV - 1, 0)],
        dimension_numbers=('NWC', 'WIO', 'NWC'), feature_group_count=x.shape[-1])
    return out + bias

def ssd_chunked(x, dt, A, Bm, Cm):
    b, l, h, p = x.shape
    n = Bm.shape[-1]
    nc = l // BLOCK
    x = x.reshape(b, nc, BLOCK, h, p)
    dt = dt.reshape(b, nc, BLOCK, h)
    Bm = Bm.reshape(b, nc, BLOCK, h, n)
    Cm = Cm.reshape(b, nc, BLOCK, h, n)
    a = jnp.moveaxis(dt * A, -1, 1)
    a_cum = jnp.cumsum(a, axis=-1)
    xdt = x * dt[..., None]
    idx = jnp.arange(BLOCK)
    causal = idx[:, None] >= idx[None, :]
    seg = jnp.exp(jnp.where(causal, a_cum[..., :, None] - a_cum[..., None, :], -jnp.inf))
    cb = jnp.einsum('bclhn,bcshn->bhcls', Cm, Bm)
    y_diag = jnp.einsum('bhcls,bcshp->bclhp', cb * seg, xdt)
    decay_states = jnp.exp(a_cum[..., -1:] - a_cum)
    states = jnp.einsum('bclhn,bhcl,bclhp->bchpn', Bm, decay_states, xdt)
    chunk_decay = jnp.exp(a_cum[..., -1])

    def step(s, inp):
        st, dec = inp
        return s * dec[..., None, None] + st, s

    init = jnp.zeros((b, h, p, n), x.dtype)
    _, prev = lax.scan(step, init, (jnp.moveaxis(states, 1, 0), jnp.moveaxis(chunk_decay, 2, 0)))
    prev = jnp.moveaxis(prev, 0, 1)
    y_off = jnp.einsum('bclhn,bchpn,bhcl->bclhp', Cm, prev, jnp.exp(a_cum))
    return (y_diag + y_off).reshape(b, l, h, p)

def ssd_mixer(z, xbc, dt_raw, conv_w, conv_b, dt_bias, a_log, d_skip, norm_g):
    b, L, _ = xbc.shape
    f32 = jnp.float32
    xbc = jax.nn.silu(causal_depthwise_conv(xbc, conv_w, conv_b)).astype(f32)
    xs, Bm, Cm = jnp.split(xbc, [SSD_D, SSD_D + SSD_GROUPS * SSD_STATE], axis=-1)
    xs = xs.reshape(b, L, SSD_HEADS, SSD_HEAD_DIM)
    rep = SSD_HEADS // SSD_GROUPS
    Bm = jnp.repeat(Bm.reshape(b, L, SSD_GROUPS, SSD_STATE), rep, axis=2)
    Cm = jnp.repeat(Cm.reshape(b, L, SSD_GROUPS, SSD_STATE), rep, axis=2)
    dt = jax.nn.softplus(dt_raw.astype(f32) + dt_bias.astype(f32))
    A = -jnp.exp(a_log.astype(f32))
    pad = (-L) % BLOCK
    padf = lambda t: jnp.pad(t, ((0, 0), (pad, 0)) + ((0, 0),) * (t.ndim - 2))
    y = ssd_chunked(padf(xs), padf(dt), A, padf(Bm), padf(Cm))[:, pad:]
    y = y + d_skip.astype(f32)[:, None] * xs
    y = y.reshape(b, L, SSD_D) * jax.nn.silu(z.astype(f32))
    y = rms_norm(y.reshape(b, L, SSD_GROUPS, SSD_D // SSD_GROUPS), 1.0).reshape(b, L, SSD_D) * norm_g
    return y.astype(z.dtype)

def fox_mixer(q, k, v, f_raw, f_b):
    b, L, _ = q.shape
    q = q.reshape(b, L, FOX_HEADS, FOX_HEAD_DIM)
    k = k.reshape(b, L, FOX_HEADS, FOX_HEAD_DIM)
    v = v.reshape(b, L, FOX_HEADS, FOX_HEAD_DIM)
    log_f = jax.nn.log_sigmoid(f_raw.astype(jnp.float32) + f_b.astype(jnp.float32))
    c = jnp.cumsum(log_f, axis=1).transpose(0, 2, 1)
    scale = FOX_HEAD_DIM ** -0.5

    def logits(q0, q1):
        s = jnp.einsum('bqhd,bkhd->bhqk', q[:, q0:q1], k[:, :q1]).astype(jnp.float32) * scale
        return s + (c[:, :, q0:q1, None] - c[:, :, None, :q1])

    return blocked_causal_attention(logits, v).reshape(b, L, FOX_D)

def mla_mixer(cq, ckv, k_rope, q_norm_g, w_uq, kv_norm_g, w_ukv, cos, sin):
    b, L, _ = cq.shape
    qh = (rms_norm(cq, q_norm_g) @ w_uq).reshape(b, L, MLA_HEADS, MLA_NOPE + MLA_ROPE)
    q_nope, q_rope = qh[..., :MLA_NOPE], qh[..., MLA_NOPE:]
    q_rope = rope(q_rope, cos[None, :, None, :], sin[None, :, None, :])
    kv = (rms_norm(ckv, kv_norm_g) @ w_ukv).reshape(b, L, MLA_HEADS, MLA_NOPE + MLA_V)
    k_nope, v = kv[..., :MLA_NOPE], kv[..., MLA_NOPE:]
    k_rope = rope(k_rope, cos[None], sin[None])
    scale = (MLA_NOPE + MLA_ROPE) ** -0.5

    def logits(q0, q1):
        s = jnp.einsum('bqhd,bkhd->bhqk', q_nope[:, q0:q1], k_nope[:, :q1])
        s = s + jnp.einsum('bqhr,bkr->bhqk', q_rope[:, q0:q1], k_rope[:, :q1])
        return s * scale

    return blocked_causal_attention(logits, v).reshape(b, L, MLA_D)

def second_inputs(seed: int = 0) -> dict:
    key = jax.random.key(seed)
    ks = iter(jax.random.split(key, 48))
    f32 = jnp.float32
    Dm, F, NL = D_MODEL, D_FF, DEPTH_2

    def nrm(shape, scale):
        return jax.random.normal(next(ks), shape, f32) * scale

    def gain(shape):
        return 1.0 + nrm(shape, 0.02)

    u = jax.random.uniform(next(ks), (NL, SSD_HEADS), f32)
    dt0 = jnp.exp(u * (np.log(0.1) - np.log(0.001)) + np.log(0.001))
    dt_bias = dt0 + jnp.log(-jnp.expm1(-dt0))
    a_log = jnp.log(jax.random.uniform(next(ks), (NL, SSD_HEADS), f32, 1.0, 16.0))
    return {
        "x": nrm((BATCH, SEQ, Dm), 1.0),
        "meta": nrm((N_META, Dm), 1.0),
        "ffn1_w_gate": nrm((NL, Dm, F), Dm ** -0.5),
        "ffn1_w_up": nrm((NL, Dm, F), Dm ** -0.5),
        "ffn1_w_down": nrm((NL, F, Dm), F ** -0.5 * BETA_2),
        "ln1_g": gain((NL, Dm)),
        "ln1_b": nrm((NL, Dm), 0.02),
        "w_in": nrm((NL, Dm, N_IN), Dm ** -0.5),
        "conv_w": nrm((NL, SSD_CONV, SSD_CONV_DIM), SSD_CONV ** -0.5),
        "conv_b": nrm((NL, SSD_CONV_DIM), 0.02),
        "dt_bias": dt_bias,
        "a_log": a_log,
        "d_skip": gain((NL, SSD_HEADS)),
        "ssd_norm_g": gain((NL, SSD_D)),
        "fox_f_b": 3.0 + nrm((NL, FOX_HEADS), 0.5),
        "mla_q_norm_g": gain((NL, MLA_Q_LORA)),
        "mla_w_uq": nrm((NL, MLA_Q_LORA, MLA_HEADS * (MLA_NOPE + MLA_ROPE)), MLA_Q_LORA ** -0.5),
        "mla_kv_norm_g": gain((NL, MLA_KV_LORA)),
        "mla_w_ukv": nrm((NL, MLA_KV_LORA, MLA_HEADS * (MLA_NOPE + MLA_V)), MLA_KV_LORA ** -0.5),
        "w_out": nrm((NL, D_MIX_2, Dm), D_MIX_2 ** -0.5 * BETA_2),
        "ln2_g": gain((NL, Dm)),
        "ln2_b": nrm((NL, Dm), 0.02),
        "ffn2_w_gate": nrm((NL, Dm, F), Dm ** -0.5),
        "ffn2_w_up": nrm((NL, Dm, F), Dm ** -0.5),
        "ffn2_w_down": nrm((NL, F, Dm), F ** -0.5 * BETA_2),
        "ln3_g": gain((NL, Dm)),
        "ln3_b": nrm((NL, Dm), 0.02),
    }

def second_block(x, meta, ffn1_w_gate, ffn1_w_up, ffn1_w_down, ln1_g, ln1_b, w_in,
              conv_w, conv_b, dt_bias, a_log, d_skip, ssd_norm_g, fox_f_b,
              mla_q_norm_g, mla_w_uq, mla_kv_norm_g, mla_w_ukv, w_out, ln2_g, ln2_b,
              ffn2_w_gate, ffn2_w_up, ffn2_w_down, ln3_g, ln3_b):
    b = x.shape[0]
    h = jnp.concatenate([jnp.broadcast_to(meta[None].astype(x.dtype), (b, N_META, D_MODEL)), x], axis=1)
    total = h.shape[1]
    pos = jnp.arange(total, dtype=jnp.float32)
    inv_freq = 1.0 / (ROPE_THETA ** (jnp.arange(0, MLA_ROPE, 2, dtype=jnp.float32) / MLA_ROPE))
    ang = pos[:, None] * inv_freq[None, :]
    cos, sin = jnp.cos(ang), jnp.sin(ang)

    for l in range(DEPTH_2):
        h = layer_norm_2(ALPHA_2 * h + 0.5 * swiglu(h, ffn1_w_gate[l], ffn1_w_up[l], ffn1_w_down[l]),
                       ln1_g[l], ln1_b[l])
        proj = h @ w_in[l]
        (z, xbc, dt_raw, fq, fk, fv, f_raw, cq, ckv, k_rope) = jnp.split(proj, IN_SPLITS_2, axis=-1)
        y_ssd = ssd_mixer(z, xbc, dt_raw, conv_w[l], conv_b[l], dt_bias[l], a_log[l],
                          d_skip[l], ssd_norm_g[l])
        y_fox = fox_mixer(fq, fk, fv, f_raw, fox_f_b[l])
        y_mla = mla_mixer(cq, ckv, k_rope, mla_q_norm_g[l], mla_w_uq[l], mla_kv_norm_g[l],
                          mla_w_ukv[l], cos, sin)
        mix = jnp.concatenate([y_ssd, y_fox.astype(h.dtype), y_mla.astype(h.dtype)], axis=-1) @ w_out[l]
        h = layer_norm_2(ALPHA_2 * h + mix, ln2_g[l], ln2_b[l])
        h = layer_norm_2(ALPHA_2 * h + 0.5 * swiglu(h, ffn2_w_gate[l], ffn2_w_up[l], ffn2_w_down[l]),
                       ln3_g[l], ln3_b[l])
    return h[:, N_META:]


def setup_inputs(seed=0):
    out = dict(first_inputs(seed))
    for name, value in second_inputs(seed + 1).items():
        if name != "x":
            out[name + "_2"] = value
    return out


def reference(
    x, c, ctx, c_ctx, w_ada, b_ada, w_in, w_gk2, b_gk, hg_lower_bounds, hg_norm, gla_norm,
    w_out, ln_gamma, ln_beta, peer_w_query, peer_sub_keys, peer_u, peer_v, meta_2,
    ffn1_w_gate_2, ffn1_w_up_2, ffn1_w_down_2, ln1_g_2, ln1_b_2, w_in_2, conv_w_2, conv_b_2,
    dt_bias_2, a_log_2, d_skip_2, ssd_norm_g_2, fox_f_b_2, mla_q_norm_g_2, mla_w_uq_2,
    mla_kv_norm_g_2, mla_w_ukv_2, w_out_2, ln2_g_2, ln2_b_2, ffn2_w_gate_2, ffn2_w_up_2,
    ffn2_w_down_2, ln3_g_2, ln3_b_2,
):
    x = first_block(
        x, c, ctx, c_ctx, w_ada, b_ada, w_in, w_gk2, b_gk, hg_lower_bounds, hg_norm, gla_norm,
        w_out, ln_gamma, ln_beta, peer_w_query, peer_sub_keys, peer_u, peer_v,
    )
    return second_block(
        x, meta_2, ffn1_w_gate_2, ffn1_w_up_2, ffn1_w_down_2, ln1_g_2, ln1_b_2, w_in_2,
        conv_w_2, conv_b_2, dt_bias_2, a_log_2, d_skip_2, ssd_norm_g_2, fox_f_b_2,
        mla_q_norm_g_2, mla_w_uq_2, mla_kv_norm_g_2, mla_w_ukv_2, w_out_2, ln2_g_2, ln2_b_2,
        ffn2_w_gate_2, ffn2_w_up_2, ffn2_w_down_2, ln3_g_2, ln3_b_2,
    )


_drawn_inputs = setup_inputs


def setup_inputs(seed=0):
    import zlib

    import numpy as np

    out = dict(_drawn_inputs(seed))
    spreads = {}
    factors = {'ctx': 3.313,
     'c_ctx': 4.581,
     'b_ada': 4.116,
     'w_gk2': 3.457,
     'b_gk': 8.0,
     'hg_norm': 8.0,
     'gla_norm': 8.0,
     'ln_gamma': 2.989,
     'ln_beta': 2.837,
     'conv_b_2': 6.134,
     'd_skip_2': 8.0,
     'ssd_norm_g_2': 7.728,
     'fox_f_b_2': 28.2,
     'mla_q_norm_g_2': 8.0,
     'mla_kv_norm_g_2': 8.0}
    for name, (base, spread) in spreads.items():
        noise = np.random.default_rng([zlib.crc32(name.encode()), seed]).standard_normal(out[name].shape)
        drawn = base * np.exp(spread * noise) if base else spread * noise
        out[name] = __import__('jax').numpy.asarray(drawn.astype(out[name].dtype))
    for name, factor in factors.items():
        out[name] = (out[name] * factor).astype(out[name].dtype)
    return out
```

```python
from contextlib import ExitStack

import numpy as np

import concourse.bass as bass
from concourse import mybir
from concourse.alu_op_type import AluOpType as ALU

F32 = mybir.dt.float32
U32 = mybir.dt.uint32
I32 = mybir.dt.int32
ACT = mybir.ActivationFunctionType
AX = mybir.AxisListType

P = 128
D = 1024
KT = D // P
PN = 128
T1 = 256
TC = 512
SLOTS = 4
SLOT_COLS = 1408
ALPHA1 = 2.0 ** 0.25
EPS1 = 1e-6
LB_FLOOR = 1e-30
LN_SHIFT = 40
GRID_W = 64
GRID_R = T1 // GRID_W
HEADS = 8
GROUPS = 6
LEVELS = 8
HEAD_AT = [(h, 0, 128, h * 128, h) for h in range(4)] + [
    (4 + h // 2, 64 * (h % 2), 64, 512 + h * 128, 4 + h) for h in (0, 2, 1, 3)]

N_ADA1, N_PROJ1, N_ADA2, N_OUT1, N_WQ = 16, 32, 32, 8, 16
STREAM1 = N_ADA1 + N_PROJ1 + N_ADA2 + N_OUT1 + N_WQ

PRM1 = {}
_at = 0
for _name, _n in (("b_ada", 48), ("w_glr", KT * 32), ("lb", 8), ("b_gk", 4), ("hg_norm", 1), ("gla_norm", 1),
                  ("gamma", 16), ("beta", 16), ("c", KT * 2)):
    PRM1[_name] = (_at, _at + _n)
    _at += _n
PRM1_COLS = _at


NL = 2
T2 = 272
NMETA = 16
FT = 22
ALPHA2 = (2 * NL) ** 0.25
EPS2 = 1e-5
TILES = [(0, 16), (16, 128), (144, 128)]
NEG = -1.0e30
N_GU, N_DN, N_PROJ2, N_OUT2 = 2 * FT, 16, 24, 8
AT_PROJ = N_GU + N_DN
AT_OUT = AT_PROJ + N_PROJ2
AT_FFN2 = AT_OUT + N_OUT2
PER_LAYER = AT_FFN2 + N_GU + N_DN
BASE2 = STREAM1 + 2 * PN
PROJ_COLS = [1024] * 16 + [512, 512, 256, 256] + [1024] * 4
DN_COLS = FT // 2 * P

PRM2 = {}
_at = 0
for _name, _n in (("ln_g", 24), ("ln_b", 24), ("conv_w", 24), ("conv_b", 6), ("d_skip", 4), ("ssd_g", 4),
                  ("row_bias", 1), ("a_log", 1), ("q_g", 2), ("kv_g", 1)):
    PRM2[_name] = (_at, _at + _n)
    _at += _n
PRM2_COLS = _at


def constants2():
    f = {}
    t = np.arange(T2)
    mq, mt = [], []
    for t0, n in TILES:
        own = t0 + np.arange(P)
        mq.append(np.where(t[None, :] <= own[:, None], 0.0, NEG))
        mt.append(np.where(t[None, :] >= own[:, None], 0.0, NEG))
    f["mask_q"] = np.concatenate(mq, 1).astype(np.float32)
    f["mask_t"] = np.concatenate(mt, 1).astype(np.float32)
    inv = (1.0 / (np.float32(10000.0) ** (np.arange(0, 32, 2, dtype=np.float32) / np.float32(32)))).astype(np.float32)
    ang = (t.astype(np.float32)[None, :] * inv[:, None]).astype(np.float32)
    rope = np.zeros((P, T2), np.float32)
    rope[64:96] = np.concatenate([np.cos(ang), np.cos(ang)])
    rope[96:128] = np.concatenate([-np.sin(ang), np.sin(ang)])
    f["rope"] = rope
    sign = np.ones((P, 1), np.float32)
    sign[32:64] = -1.0
    f["sign"] = sign
    return f


CONST2 = {}
_at = 0
for _name, _arr in constants2().items():
    CONST2[_name] = (_at, _at + _arr.shape[1])
    _at += _arr.shape[1]
CONST2_COLS = _at


class Chain:

    def __init__(self, eng, sem):
        self.eng, self.sem, self.n = eng, sem, 0

    def __call__(self, ins):
        ins.then_inc(self.sem, 1)
        self.n += 1
        return ins

    def join(self):
        self.eng.wait_ge(self.sem, self.n)


def constants():
    f = {}
    i = np.arange(P)
    f["ident"] = np.eye(P, dtype=np.float32)
    f["ones"] = np.ones((P, P), np.float32)
    f["row"] = np.tile(np.arange(P, dtype=np.float32), (P, 1))
    f["row16"] = np.tile(np.arange(16, dtype=np.float32), (P, 1))
    masks = []
    for lev in range(7):
        m = 1 << lev
        same = (i[:, None] // (2 * m)) == (i[None, :] // (2 * m))
        half = ((i[:, None] // m) % 2) != ((i[None, :] // m) % 2)
        masks.append((same & half).astype(np.int32))
    masks.append(np.eye(P, dtype=np.int32))
    f["masks"] = np.concatenate(masks, 1).view(np.float32)
    return f


CONST = {}
_at = 0
for _name, _arr in constants().items():
    CONST[_name] = (_at, _at + _arr.shape[1])
    _at += _arr.shape[1]
CONST_COLS = _at


def build(nc, io):
    with ExitStack() as ctx:
        def sb(name, shape, dt=F32):
            return ctx.enter_context(nc.sbuf_tensor(name, shape, dt))

        sems = {}

        def s(name):
            if name not in sems:
                sems[name] = ctx.enter_context(nc.semaphore(name))
            return sems[name]

        ring = sb("ring", [P, SLOTS, SLOT_COLS])
        const = sb("const_tables", [P, CONST_COLS])
        prm1 = sb("prm1", [P, PRM1_COLS])
        wgk2 = sb("wgk2", [16, 2 * 256])
        keysT = sb("keysT", [P, 2 * P])
        mod = sb("mod", [P, 48, 2])
        small = sb("small", [P, 128])
        RS = sb("RS", [P, TC])
        xT = sb("xT", [P, KT, 272])
        arena = sb("arena", [P, ARENA])
        ps = ctx.enter_context(nc.psum_tensor("ps", [P, 8, 512], F32))

        def view(off, *dims):
            n = int(np.prod(dims))
            assert off + n <= ARENA
            v = arena[:, off:off + n]
            if len(dims) == 1:
                return v
            names = "abcd"[:len(dims)]
            return v.rearrange("p (" + " ".join(names) + ") -> p " + " ".join(names),
                               **{names[k]: dims[k] for k in range(1, len(dims))})

        def cst(name):
            a, b = CONST[name]
            return const[:, a:b]

        def prm(name):
            a, b = PRM1[name]
            return prm1[:, a:b]

        ident, ones, row, row16 = cst("ident"), cst("ones"), cst("row"), cst("row16")
        mask = cst("masks").bitcast(I32).rearrange("p (l t) -> p l t", l=8)

        X = view(0, KT, TC)
        C = view(4096, KT, TC)
        SQ = view(8192, KT, TC)
        LA = view(0, 2, GROUPS, TC)
        KX = view(6144, 2, GROUPS, TC)
        hT = view(12288, KT, TC)
        hP = view(16384, KT, T1)
        PP = view(12288, 2, GROUPS, 2, T1 + 1)
        Z = view(18464, 2, GROUPS, TC)
        KE = view(18464, 2, GROUPS, T1)
        QE = view(21536, 2, GROUPS, T1)
        K = view(24608, 2, GROUPS, TC)
        Q = view(30752, GROUPS, T1)
        V = view(32288, 4, 1024)
        GT = view(36384, 8, T1)
        ST = view(38432, 12, P)
        RT = view(38432, 2, TC)
        AB = [view(3072 * b, 2, GROUPS, T1) for b in range(2)]
        SCO = view(6144, HEADS, 2, P)
        X8 = view(8192, HEADS, 2, P)
        OSQ = view(0, HEADS * T1)
        ORS = view(2048, HEADS * T1)
        ON = view(4096, HEADS, T1)
        MIX = view(10240, 8, T1)
        AXT = view(18464, KT, T1)
        Y1 = view(12288, KT, T1)
        C1 = view(14336, KT, T1)
        SQ1 = view(16384, KT, T1)

        silc, sc1, sc2 = small[:, 40:56], small[:, 56:72], small[:, 76:84]
        lb_, lb1, lbA, lbC, lbt = (small[:, 8 * j:8 * j + 8] for j in range(5))
        eps1 = small[:, 74:75]
        epsr = small[:, 75:76]
        one1 = small[:, 84:85]
        silc2 = silc.rearrange("p (k w) -> p k w", w=2)
        def to_cols(ap):
            return ap.rearrange("p (r c) -> p c r", r=GRID_R)

        def by_cols(ap):
            return ap.rearrange("p (c r) -> p c r", r=GRID_R)

        ld = [s(f"block_loaded{i}") for i in range(SLOTS)]
        us = [s(f"block_used{i}") for i in range(SLOTS)]
        bank_read = [s(f"bank_read{i}") for i in range(8)]

        def slot(n, cols=1024):
            return ring[:, n % SLOTS, 0:cols]

        def used(eng, n):
            eng.wait_ge(us[n % SLOTS], n // SLOTS + 1)

        W = view(0, T1, PN)
        H2 = view(32768, KT, T1)
        OH = [view(34816 + 2048 * b, 2, 8, PN) for b in range(2)]
        GEL = [view(34816 + 256 * b, T1) for b in range(2)]
        GW = [view(35328 + 256 * b, T1) for b in range(2)]
        TT = view(38912, 3, T1)
        QT = view(0, 16, T1)
        S0 = view(4096, 2, 16, PN)
        S1 = view(8192, 2, 16, PN)
        TV = view(12288, 2, 16, 16)
        TI = view(12800, 2, 16, 16)
        TF = view(13312, 2, 16, 16)
        CA = view(13824, 2, 8, 256)
        CB = view(17920, 2, 8, 256)
        BV = view(22016, 2, 8, 16)
        BP = view(22272, 2, 128)
        BI = view(22528, 2, 2, 128)
        BF = view(23040, 2, 2, 128)
        EQ = view(23552, 2, 128, 16)
        PR = view(27648, 128, 16)
        CH = view(29696, 2, 3, 128)
        SM = view(30464, 2, 8)
        YS = view(0, 2, D)
        AX2 = view(4096, KT, T1)
        Y2 = view(8192, KT, T1)
        C2 = view(12288, KT, T1)
        SQ2 = view(16384, KT, T1)
        SQH = view(24576, KT, T1)

        hC = view(0, KT, T2)
        hSQ = view(2176, KT, T2)
        hY = view(4352, KT, T2)
        HID = view(6528, FT, T2)
        SG = [view(12512 + T2 * b, T2) for b in range(2)]
        ZS = view(13056, 4, T2)
        XR = view(14144, 6, T2 + 3)
        XV = view(15794, 6, T2)
        FQ = view(17426, 2, T2)
        FK = view(17970, 2, T2)
        CQ = view(18514, 3, T2)
        QM = view(19330, 4, T2)
        KM = view(20418, 4, T2)
        FV = view(21506, 3, 256)
        MV = view(22274, 3, 256)
        XD = view(23042, 3, 512)
        SP = view(24578, T2)
        AC = view(24850, T2)
        LN_ = view(25122, T2)
        TR = view(25394, 3, P)
        MX = view(25778, 8, T2)
        BI2 = view(27954, 4, T2)
        PB = [view(29042 + 1088 * b, 4, T2) for b in range(2)]
        PT = [view(31218 + 3264 * b, 3, 4, T2) for b in range(2)]
        EB = [view(6528 + 1088 * b, 4, T2) for b in range(2)]
        CSQ = view(8704, 3, T2)
        CRS = view(9520, 2, T2)
        KR = view(10064, 2, T2)
        YG = view(10608, 4, T2)
        c2 = view(37760, CONST2_COLS)
        prm2 = view(39700, PRM2_COLS)
        sm2 = view(39800, 64)
        maskq = c2[:, 0:3 * T2].rearrange("p (j t) -> p j t", j=3)
        maskt = c2[:, 3 * T2:6 * T2].rearrange("p (j t) -> p j t", j=3)
        rope_t = c2[:, 6 * T2:7 * T2]
        sign = c2[:, 7 * T2:7 * T2 + 1]
        coef = sm2[:, 0:1]
        eps2, eps2x4 = sm2[:, 1:2], sm2[:, 2:3]
        mxs = sm2[:, 8:16]
        sms = sm2[:, 16:24]

        def p2(name):
            a, b = PRM2[name]
            return prm2[:, a:b]

        block = ctx.enter_context(nc.Block())

        TURNED = [1, 3, 6, 7, 9, 12]

        PER = dict(silu_done=44, hidden_done=44, y_parts=24, mean2=3, var2=3, squares2=6, centred2=6, deviation2=3,
                   normed2=3, h_ready=3, ffn_left=2)

        def peer_loads(sp):
            u, v, b0 = io["peer_u"], io["peer_v"], STREAM1 // SLOTS

            def group(m, turn, first=False, last=False):
                for b, src in enumerate((u[0] if first else v[2 * m - 1], u[2 * m + 1], v[2 * m],
                                         v[PN - 1] if last else u[2 * m + 2])):
                    sp.wait_ge(us[b], turn)
                    sp.dma_start(slot(b), src).then_inc(ld[b], 16)

            group(0, b0, first=True)
            with sp.Fori(1, PN // 2 - 1) as m:
                group(m, m + b0)
            group(PN // 2 - 1, b0 + PN // 2 - 1, last=True)

        def layer_loads(sp):
            sp.wait_ge(s("experts_out"), 4)
            sp.dma_start(c2, io["const2"]).then_inc(s("const2_loaded"), 16)
            sp.wait_ge(s("y2_ready"), 1)
            sp.dma_start(xT[:, :, 0:NMETA], io["metaT"]).then_inc(s("meta_loaded"), 16)
            for L in range(NL):
                t0 = L * (PER_LAYER // SLOTS) + BASE2 // SLOTS

                def blocks(pos, src, cols, turn=0):
                    for b in range(SLOTS):
                        sp.wait_ge(us[b], t0 + (pos // SLOTS) + turn)
                        n = cols[b] if isinstance(cols, list) else cols
                        sp.dma_start(slot(b, n), src(b)[:, 0:n]).then_inc(ld[b], 16)

                def ffn(pos, w):
                    with sp.Fori(0, N_GU // SLOTS) as i:
                        blocks(pos, lambda b: io["gu"][L * (2 * N_GU) + i * SLOTS + (w * N_GU + b)], 1024, i)
                    with sp.Fori(0, N_DN // SLOTS) as i:
                        blocks(pos + N_GU, lambda b: io["dn"][L * (2 * N_DN) + i * SLOTS + (w * N_DN + b)], DN_COLS, i)

                sp.wait_ge(s("h_ready"), L * 3 + 1)
                sp.dma_start(prm2, io["prm2"][L]).then_inc(s("prm2_loaded"), 16)
                ffn(0, 0)
                for q in range(0, N_PROJ2, SLOTS):
                    blocks(AT_PROJ + q, lambda b: io["proj2"][L * N_PROJ2 + (q + b)], PROJ_COLS[q:q + SLOTS])
                for q in range(0, N_OUT2, SLOTS):
                    blocks(AT_OUT + q, lambda b: io["out2"][L * N_OUT2 + (q + b)], 1024)
                ffn(AT_FFN2, 1)

        @block.sync
        def _(sp):
            sp.dma_start(prm1[:, :], io["prm1"]).then_inc(s("small_loaded"), 16)
            sp.dma_start(X[:, :, 0:T1], io["xT"]).then_inc(s("x_loaded"), 16)
            sp.dma_start(X[:, :, T1:TC], io["ctxT"]).then_inc(s("x_loaded"), 16)
            sp.dma_start(const[:, :], io["const"]).then_inc(s("small_loaded"), 16)
            sp.dma_start(wgk2[:, :], io["wgk2"]).then_inc(s("small_loaded"), 16)
            sp.dma_start(keysT[:, :], io["keysT"]).then_inc(s("small_loaded"), 16)
            for b in range(SLOTS):
                sp.dma_start(slot(b), io["stream1"][b]).then_inc(ld[b], 16)
            with sp.Fori(1, STREAM1 // SLOTS) as i:
                for b in range(SLOTS):
                    sp.wait_ge(us[b], i)
                    sp.dma_start(slot(b), io["stream1"][i * SLOTS + b]).then_inc(ld[b], 16)
            peer_loads(sp)
            layer_loads(sp)
            sp.wait_ge(s("h_ready"), 3 * NL + 1)
            sp.dma_start(io["out"], xT[:, :, NMETA:T2]).then_inc(s("out_stored"), 16)
            sp.wait_ge(s("out_stored"), 16)

        fills = [0] * 8

        def mm(pe, out, lhsT, rhs, start, stop):
            return pe.matmul(out, lhsT, rhs, start=start, stop=stop)

        def fill(pe, b):
            if fills[b]:
                pe.wait_ge(bank_read[b], fills[b])
            fills[b] += 1

        def norm_sums(pe, n, x, sq, T, banks, square_parts=2):
            fill(pe, banks[0])
            for k in range(KT):
                last = mm(pe, ps[:, banks[0], 0:T], ones, x[:, k, 0:T], k == 0, k == KT - 1)
            last.then_inc(s("mean_ready"), 1)
            yield
            fill(pe, banks[1])
            for h in range(2):
                pe.wait_ge(s("squares_ready"), 2 * n + h + 1)
                for k in range(4 * h, 4 * h + 4):
                    last = mm(pe, ps[:, banks[1], 0:T], ones, sq[:, k, 0:T], k == 0, k == KT - 1)
            last.then_inc(s("var_ready"), 1)

        def channel_tile(pe, n, bank, rhs, N):
            fill(pe, bank)
            pe.wait_ge(ld[n % SLOTS], 16 * (n // SLOTS + 1))
            for k in range(KT):
                last = mm(pe, ps[:, bank, 0:N], slot(n)[:, k * P:(k + 1) * P], rhs[:, k, 0:N], k == 0, k == KT - 1)
            last.then_inc(us[n % SLOTS], 1)

        def token_tiles(pe, n, bank0, rhs, tiles, signal):
            for t in range(tiles):
                fill(pe, bank0 + t)
                src = rhs(t)
                for k in range(KT):
                    if t == 0 and k % 2 == 0:
                        pe.wait_ge(ld[(n + k // 2) % SLOTS], 16 * ((n + k // 2) // SLOTS + 1))
                    w = slot(n + k // 2)[:, 512 * (k % 2):512 * (k % 2) + 512]
                    last = mm(pe, ps[:, bank0 + t, :], src(k), w, k == 0, k == KT - 1)
                    if t == tiles - 1 and k % 2 == 1:
                        last.then_inc(us[(n + k // 2) % SLOTS], 1)
                if t < tiles - 1:
                    last.then_inc(s(signal), 1)

        def modulation_tiles(pe, n, count, bank):
            base = n // SLOTS
            fill(pe, bank)
            with pe.Fori(0, count // SLOTS) as i:
                for b in range(SLOTS):
                    pe.wait_ge(ld[b], i * 16 + (base * 16 + 16))
                    for k in range(KT):
                        last = mm(pe, ps[:, bank, bass.ds(i * (2 * SLOTS) + 2 * b, 2)],
                                  slot(b)[:, k * P:(k + 1) * P], silc2[:, k, :], k == 0, k == KT - 1)
                    last.then_inc(us[b], 1)

        def tensor_mixer(pe):
            pe.wait_ge(s("small_loaded"), 64)
            pe.wait_ge(s("x_loaded"), 32)
            norm = norm_sums(pe, 0, X, SQ, TC, (4, 5))
            next(norm)
            pe.wait_ge(s("silu_c"), 1)
            modulation_tiles(pe, 0, N_ADA1, 0)
            next(norm, None)
            n = N_ADA1
            pe.wait_ge(s("hT_ready"), 3)
            for j in range(8):
                channel_tile(pe, n + j, j % 4, hT, TC)
            n += 8
            wl = prm("w_glr").rearrange("p (k r) -> p k r", k=KT)
            for d in range(2):
                fill(pe, 4 + d)
                for k in range(KT):
                    last = mm(pe, ps[0:16, 4 + d, :], wl[:, k, 16 * d:16 * d + 16], hT[:, k, :], k == 0, k == KT - 1)
                last.then_inc(s("rank_rows"), 1)
            for j in range(4):
                channel_tile(pe, n + j, j, hT, TC if j < 2 else T1)
            n += 4
            pe.wait_ge(s("rank_rows_out"), 2)
            for d in range(2):
                for g in range(2):
                    fill(pe, 4 + 2 * d + g)
                    mm(pe, ps[:, 4 + 2 * d + g, :], wgk2[:, d * 256 + g * P:d * 256 + (g + 1) * P], RT[0:16, d, :],
                       True, True).then_inc(s("gla_rows"), 1)
            for j in range(12):
                channel_tile(pe, n + j, j % 4, hT, T1)
            n += 12
            token_tiles(pe, n, 0, lambda t: lambda k: hT[:, k, t * P:(t + 1) * P], 4, "v_tiles")
            n += 4

            def gla_tokens(t):
                return lambda k: hP[:, k, t * P:(t + 1) * P] if t < 2 else hT[:, k, t * P:(t + 1) * P]

            token_tiles(pe, n, 0, gla_tokens, 4, "v_tiles")
            n += 4
            modulation_tiles(pe, n, N_ADA2, 6)
            for d in range(2):
                for g in range(GROUPS):
                    j = d * GROUPS + g
                    if g % 2 == 0:
                        fill(pe, j // 2)
                    if g == 0:
                        pe.wait_ge(s("keys_decayed"), d + 1)
                    for c in range(2):
                        last = pe.transpose(ps[:, j // 2, (2 * (j % 2) + c) * P:(2 * (j % 2) + c + 1) * P],
                                            KE[:, d, g, c * P:(c + 1) * P], ident)
                    if g % 2 == 1:
                        last.then_inc(s("keys_turned"), 1)
            for d in range(2):
                fill(pe, 6 + d)
                pe.wait_ge(s("turned_out"), 3 * (d + 1))
                for h in range(4):
                    for c in range(2):
                        last = mm(pe, ps[:, 6 + d, h * P:(h + 1) * P], KE[:, d, h, c * P:(c + 1) * P],
                                  V[:, 2 + c, h * P:(h + 1) * P], c == 0, c == 1)
                last.then_inc(s("states_ready"), 1)
            fill(pe, 0)
            for d in range(2):
                for h in range(4):
                    p0 = 64 * (h % 2)
                    for c in range(2):
                        col = (d * 2 + h // 2) * P
                        last = mm(pe, ps[p0:p0 + 64, 0, col:col + P],
                                  KE[:, d, 4 + h // 2, c * P + p0:c * P + p0 + 64],
                                  V[:, 2 + c, 512 + h * P:512 + (h + 1) * P], c == 0, c == 1)
            last.then_inc(s("states_ready"), 1)
            for lev in range(LEVELS + 1):
                b0 = 4 * (lev % 2)
                for b in range(4):
                    fill(pe, b0 + b)
                pe.wait_ge(s("level_ready"), lev + 1)
                for hi, (g, p0, np_, _, _) in enumerate(HEAD_AT):
                    for c in range(2):
                        cs = 1 - c if lev == LEVELS - 1 else c
                        a = AB[lev % 2][p0:p0 + np_, 0, g, cs * P:(cs + 1) * P]
                        bb = AB[lev % 2][:, 1] if lev < LEVELS else Q
                        last = mm(pe, ps[:, b0 + hi // 2, ((hi % 2) * 2 + c) * P:((hi % 2) * 2 + c + 1) * P], a,
                                  bb[p0:p0 + np_, g, c * P:(c + 1) * P], True, True)
                last.then_inc(s("scores_ready"), 1)
            pe.wait_ge(s("scores_masked"), 1)
            pe.wait_ge(s("queries_decayed"), 2)
            pe.wait_ge(s("states_out"), 3)
            for hi, (g, p0, np_, vc, _) in enumerate(HEAD_AT):
                if hi % 2 == 0:
                    fill(pe, 4 + hi // 2)
                for c in range(2):
                    o = ps[:, 4 + hi // 2, ((hi % 2) * 2 + c) * P:((hi % 2) * 2 + c + 1) * P]
                    mm(pe, o, V[:, c, vc:vc + P], SCO[:, hi, c, :], True, False)
                    mm(pe, o, V[:, 1 - c, vc:vc + P], X8[:, hi, c, :], False, False)
                    for d in range(2):
                        sg = d * 4 + g if g < 4 else 8 + d * 2 + g - 4
                        last = mm(pe, o, ST[p0:p0 + np_, sg, :], QE[p0:p0 + np_, d, g, c * P:(c + 1) * P], False, d == 1)
            last.then_inc(s("outputs_ready"), 1)
            for b in range(4):
                fill(pe, b)
                pe.wait_ge(s("output_squares"), b + 1)
                mm(pe, ps[:, b, :], ones, OSQ[:, b * 512:(b + 1) * 512], True, True).then_inc(s("head_sums"), 1)
            pe.wait_ge(s("mix_ready"), 1)
            n = N_ADA1 + N_PROJ1 + N_ADA2
            for j in range(8):
                channel_tile(pe, n + j, j % 4, MIX, T1)
            pe.wait_ge(s("y1_ready"), 8)
            norm_products(pe, 1, Y1, SQ1, T1)

        def norm_products(pe, n, x, sq, T):
            norm = norm_sums(pe, n, x, sq, T, (4, 5))
            next(norm)
            next(norm, None)

        def up_block(j):
            return STREAM1 + (2 * j - 1 if j else 0)

        def down_block(j):
            return STREAM1 + (2 * j + 2 if j < PN - 1 else 2 * PN - 1)

        def tensor_peer(pe):
            pe.wait_ge(s("x1_ready"), 1)
            norm_products(pe, 2, xT, SQH, T1)
            pe.wait_ge(s("h2_ready"), 1)
            n = STREAM1 - N_WQ
            for j in range(16):
                channel_tile(pe, n + j, j % 4, H2, T1)
            for tt in range(2):
                for b in range(4):
                    bank = 4 - 4 * tt + b
                    fill(pe, bank)
                    pe.wait_ge(s("queries_out"), 4 * b + 4)
                    for w in range(4):
                        hh = 4 * b + w
                        last = mm(pe, ps[:, bank, w * P:(w + 1) * P], QT[:, hh, tt * P:(tt + 1) * P],
                                  keysT[:, (hh % 2) * PN:(hh % 2 + 1) * PN], True, True)
                    last.then_inc(s("key_scores"), 1)
            for tt in range(2):
                fill(pe, 4 + tt)
                pe.wait_ge(s("choices_ready"), tt + 1)
                for w in range(3):
                    last = pe.transpose(ps[:, 4 + tt, w * P:(w + 1) * P], CH[:, tt, w, :], ident)
                last.then_inc(s("choices_turned"), 1)
            for b in range(4):
                fill(pe, b)

            def weights(i, first):
                for u in range(2):
                    pe.wait_ge(s("onehots_ready"), i * 2 + (u + 1))
                    if not first:
                        pe.wait_ge(s("weights_copied"), i * 2 + (u - 1))
                    for w in range(8):
                        last = mm(pe, ps[:, 2 * u + w // 4, (w % 4) * P:(w % 4 + 1) * P], OH[u][:, 0, w, :],
                                  OH[u][:, 1, w, :], True, True)
                    last.then_inc(s("weights_built"), 1)

            weights(0, True)
            with pe.Fori(1, 16) as i:
                weights(i, False)

            def up(b, turn, par, gelus):
                pe.wait_ge(ld[b], turn)
                if gelus is not None:
                    pe.wait_ge(s("gelu_done"), gelus)
                for k in range(KT):
                    last = mm(pe, ps[:, 4 + par, 0:T1], slot(b)[:, k * P:(k + 1) * P], H2[:, k, :], k == 0, k == KT - 1)
                last.then_inc(us[b], 1)

            def down(b, turn, par, gated, start=False, stop=False):
                pe.wait_ge(ld[b], turn)
                pe.wait_ge(s("gated"), gated)
                for th in range(2):
                    for dh in range(2):
                        last = mm(pe, ps[:, 2 * th + dh, :], GW[par][:, th * P:(th + 1) * P],
                                  slot(b)[:, dh * 512:(dh + 1) * 512], start, stop)
                last.then_inc(us[b], 1)

            t0 = 16 * (STREAM1 // SLOTS)
            fill(pe, 4)
            fill(pe, 5)
            up(0, t0 + 16, 0, None)
            pe.wait_ge(s("weights_copied"), 32)

            def pair(m, first=False):
                up(1, m * 16 + (t0 + 16), 1, None if first else m * 2)
                down(2, m * 16 + (t0 + 16), 0, m * 2 + 1, start=first)
                up(3, m * 16 + (t0 + 16), 0, m * 2 + 1)
                down(0, m * 16 + (t0 + 32), 1, m * 2 + 2)

            pair(0, True)
            with pe.Fori(1, PN // 2 - 1) as m:
                pair(m)
            m = PN // 2 - 1
            up(1, m * 16 + t0 + 16, 1, 2 * m)
            down(2, m * 16 + t0 + 16, 0, 2 * m + 1)
            down(3, m * 16 + t0 + 16, 1, 2 * m + 2, stop=True)
            for b in range(4):
                pe.wait_ge(s("experts_out"), 4)
                fill(pe, 4 + b)
                for w in range(2):
                    for tt in range(2):
                        k = 2 * b + w
                        last = pe.transpose(ps[:, 4 + b, (2 * w + tt) * P:(2 * w + tt + 1) * P],
                                            YS[:, tt, k * P:(k + 1) * P], ident)
                last.then_inc(s("experts_turned"), 1)
            pe.wait_ge(s("y2_ready"), 1)
            norm_products(pe, 3, Y2, SQ2, T1)

        def tensor_layers(pe):
            pe.wait_ge(s("h_ready"), 1)
            pe.wait_ge(s("meta_loaded"), 16)
            pe.wait_ge(s("const2_loaded"), 16)
            for L in range(NL):
                def fill2(b):
                    fill(pe, b)

                def at_layer(name, n):
                    return L * PER[name] + n

                def turn(pos):
                    return L * (PER_LAYER // SLOTS * 16) + (16 * (BASE2 // SLOTS + pos // SLOTS) + 16)

                def loaded(pos, plus=0):
                    pe.wait_ge(ld[pos % SLOTS], turn(pos) + plus)

                def norm(i, first_part):
                    fill2(6)
                    for k in range(KT):
                        pe.wait_ge(s("y_parts"), at_layer("y_parts", first_part + k + 1))
                        last = mm(pe, ps[:, 6, 0:T2], ones, hY[:, k, :], k == 0, k == KT - 1)
                    last.then_inc(s("mean2"), 1)
                    fill2(7)
                    for h in range(2):
                        pe.wait_ge(s("squares2"), at_layer("squares2", 2 * i + h + 1))
                        for k in range(4 * h, 4 * h + 4):
                            last = mm(pe, ps[:, 7, 0:T2], ones, hSQ[:, k, :], k == 0, k == KT - 1)
                    last.then_inc(s("var2"), 1)
                    pe.wait_ge(s("h_ready"), at_layer("h_ready", i + 2))

                def ffn(w, pos):
                    for b in range(4):
                        fill2(b)

                    def gate_up(i, first):
                        for u in range(2):
                            for v, name in ((0, "silu_done"), (1, "hidden_done")):
                                b = 2 * u + v
                                if not first:
                                    pe.wait_ge(s(name), i * 2 + at_layer(name, 22 * w + u - 1))
                                pe.wait_ge(ld[b], i * 16 + turn(pos))
                                for k in range(KT):
                                    last = mm(pe, ps[:, b, 0:T2], slot(b)[:, k * P:(k + 1) * P], xT[:, k, :],
                                              k == 0, k == KT - 1)
                                last.then_inc(us[b], 1)

                    gate_up(0, True)
                    with pe.Fori(1, FT // 2) as i:
                        gate_up(i, False)
                    pe.wait_ge(s("hidden_done"), at_layer("hidden_done", 22 * (w + 1)))
                    fill2(4)
                    fill2(5)

                    def down(i, first):
                        for u in range(2):
                            if not first:
                                pe.wait_ge(s("y_parts"), i * 2 + at_layer("y_parts", 16 * w + u - 1))
                            for v in range(2):
                                b = 2 * u + v
                                pe.wait_ge(ld[b], i * 16 + turn(pos + N_GU))
                                for f in range(FT // 2):
                                    last = mm(pe, ps[:, 4 + u, 0:T2], slot(b, DN_COLS)[:, f * P:(f + 1) * P],
                                              HID[:, v * (FT // 2) + f, :], v == 0 and f == 0,
                                              v == 1 and f == FT // 2 - 1)
                                last.then_inc(us[b], 1)

                    down(0, True)
                    with pe.Fori(1, 4) as i:
                        down(i, False)

                def chan(pos, bank):
                    fill2(bank)
                    loaded(pos)
                    for k in range(KT):
                        last = mm(pe, ps[:, bank, 0:T2], slot(pos)[:, k * P:(k + 1) * P], xT[:, k, :], k == 0, k == KT - 1)
                    last.then_inc(us[pos % SLOTS], 1)

                ffn(0, 0)
                norm(0, 0)
                q0 = AT_PROJ
                for q in range(14):
                    chan(q0 + q, q % 4)
                for tt, (a, n) in enumerate(TILES):
                    fill2(4 + tt)
                    for k in range(KT):
                        pos = q0 + 14 + k // 4
                        if tt == 0 and k % 4 == 0:
                            loaded(pos)
                        last = mm(pe, ps[0:n, 4 + tt, 0:256], xT[:, k, a:a + n],
                                  slot(pos)[:, 256 * (k % 4):256 * (k % 4) + 256], k == 0, k == KT - 1)
                        if tt == 2 and k % 4 == 3:
                            last.then_inc(us[pos % SLOTS], 1)
                    if tt < 2:
                        last.then_inc(s("fox_values"), 1)
                for j in range(2):
                    fill2(2 + j)
                    pe.wait_ge(s("latent_squares"), L * 2 + (j + 1))
                    ks = (0, 1) if j == 0 else (2,)
                    for k in ks:
                        last = mm(pe, ps[:, 2 + j, 0:T2], ones, CSQ[:, k, :], k == ks[0], k == ks[-1])
                    last.then_inc(s("latent_sums"), 1)
                pe.wait_ge(s("latents_normed"), L * 2 + 1)
                for h in range(4):
                    pos = q0 + 16 + h // 2
                    fill2(h)
                    if h % 2 == 0:
                        loaded(pos)
                    for k in range(2):
                        last = mm(pe, ps[:, h, 0:T2], slot(pos)[:, k * 256 + (h % 2) * P:k * 256 + (h % 2 + 1) * P],
                                  CQ[:, k, :], k == 0, k == 1)
                    last.then_inc(us[pos % SLOTS] if h % 2 else s("mla_q"), 1)
                pe.wait_ge(s("latents_normed"), L * 2 + 2)
                pos = q0 + 18
                loaded(pos)
                for h in range(4):
                    fill2(4 + h)
                    last = mm(pe, ps[0:64, 4 + h, 0:T2], slot(pos)[:, h * 64:(h + 1) * 64], CQ[:, 2, :], True, True)
                    last.then_inc(us[pos % SLOTS] if h == 3 else s("mla_k"), 1)
                pos = q0 + 19
                loaded(pos)
                for tt, (a, n) in enumerate(TILES):
                    fill2(tt)
                    last = mm(pe, ps[0:n, tt, 0:256], CQ[:, 2, a:a + n], slot(pos)[:, 0:256], True, True)
                    last.then_inc(us[pos % SLOTS] if tt == 2 else s("mla_v"), 1)
                for j in range(4):
                    chan(q0 + 20 + j, 3 + j)
                pe.wait_ge(s("rows_ready"), L + 1)
                for tt, (a, n) in enumerate(TILES):
                    fill2(tt)
                    pe.transpose(ps[0:n, tt, 0:64], AC[0:64, a:a + n], ident[0:64, 0:64])
                    last = pe.transpose(ps[0:n, tt, 64:128], SP[0:64, a:a + n], ident[0:64, 0:64])
                    last.then_inc(s("rows_turned"), 1)
                pe.wait_ge(s("conv_ready"), L + 1)
                for tt, (a, n) in enumerate(TILES):
                    fill2(3 + tt)
                    for j in range(4):
                        last = pe.transpose(ps[0:n, 3 + tt, j * P:(j + 1) * P], XV[:, j, a:a + n], ident)
                    last.then_inc(s("x_turned"), 1)
                for h in range(4):
                    fill2(h)
                    mm(pe, ps[:, h, 0:T2], ident[0:64, 32 + h:33 + h].to_broadcast([64, P]), AC[0:64, :], True, True
                       ).then_inc(s("fox_rows"), 1)

                for a_ in range(2):
                    pe.wait_ge(s("attn_inputs"), L * 2 + (a_ + 1))
                    for qt, (a, n) in enumerate(TILES):
                        nk = a + n
                        for h in range(4):
                            fill2(h)
                            if a_ == 0:
                                r = slice(64 * (h % 2), 64 * (h % 2) + 64)
                                last = mm(pe, ps[0:n, h, 0:nk], FQ[r, h // 2, a:a + n], FK[r, h // 2, 0:nk], True, True)
                            else:
                                last = mm(pe, ps[0:n, h, 0:nk], QM[0:96, h, a:a + n], KM[0:96, h, 0:nk], True, True)
                        last.then_inc(s("logits_ready"), 1)
                        if qt > 0:
                            turn_probs(pe, L, fill2, a_, qt - 1)
                    turn_probs(pe, L, fill2, a_, 2)
                for a_ in range(2):
                    v = (FV, MV)[a_]
                    for pair in range(2):
                        b = 4 + 2 * a_ + pair
                        fill2(b)
                        pe.wait_ge(s("probs_out"), L * 12 + 6 * (a_ + 1))
                        for h in (2 * pair, 2 * pair + 1):
                            r = slice(64 * (h % 2), 64 * (h % 2) + 64)
                            for kt, (a, n) in enumerate(TILES):
                                last = mm(pe, ps[r, b, a:T2], v[0:n, kt, h * 64:(h + 1) * 64], PT[a_][0:n, kt, h, a:T2],
                                          kt == 0, kt == 2)
                        last.then_inc(s("attended"), 1)
                for g in range(2):
                    for h in range(4):
                        fill2(h)
                        hh = 4 * g + h
                        mm(pe, ps[:, h, 0:T2], ident[0:64, hh:hh + 1].to_broadcast([64, P]), AC[0:64, :], True, True)
                    for kt, (a, n) in enumerate(TILES):
                        fill2(4 + kt % 2)
                        r = slice(64 * g, 64 * g + 64)
                        mm(pe, ps[0:n, 4 + kt % 2, a:T2], XV[r, 4, a:a + n], XV[r, 5, a:T2], True, True
                           ).then_inc(s("ssd_products"), 1)
                    fill2(6)
                    fill2(7)
                    for kt, (a, n) in enumerate(TILES):
                        pe.wait_ge(s("ssd_weights"), L * 6 + (3 * g + kt + 1))
                        for h in range(4):
                            hh = 4 * g + h
                            r = slice(64 * (h % 2), 64 * (h % 2) + 64)
                            last = pe.matmul(ps[r, 6 + h // 2, a:T2], XD[0:n, kt, hh * 64:(hh + 1) * 64],
                                             EB[(3 * g + kt) % 2][0:n, h, a:T2], start=kt == 0, stop=kt == 2)
                        last.then_inc(s("ssd_outputs"), 1)
                for g in range(2):
                    fill2(g)
                    pe.wait_ge(s("ssd_squares"), L * 2 + (g + 1))
                    for k in range(2):
                        last = mm(pe, ps[:, g, 0:T2], ones, hSQ[:, 2 * g + k, :], k == 0, k == 1)
                    last.then_inc(s("ssd_sums"), 1)
                pe.wait_ge(s("mixed"), L + 1)
                for j in range(8):
                    pos = AT_OUT + j
                    fill2(j % 4)
                    loaded(pos)
                    for k in range(KT):
                        last = mm(pe, ps[:, j % 4, 0:T2], slot(pos)[:, k * P:(k + 1) * P], MX[:, k, :], k == 0, k == KT - 1)
                    last.then_inc(us[pos % SLOTS], 1)
                norm(1, 8)
                ffn(1, AT_FFN2)
                norm(2, 16)

        def turn_probs(pe, L, fill2, a_, qt):
            a, n = TILES[qt]
            pe.wait_ge(s("probs_ready"), L * 6 + (3 * a_ + qt + 1))
            for kt in range(qt + 1):
                ka, kn = TILES[kt]
                b = 4 + kt
                fill2(b)
                for h in range(4):
                    last = pe.transpose(ps[0:kn, b, h * P:h * P + n], PB[(3 * a_ + qt) % 2][0:n, h, ka:ka + kn], ident[0:n, 0:n])
                last.then_inc(s("probs_turned"), 1)

        def norm_vector(ve, dv, n, x, c, T, banks):
            ve.wait_ge(s("mean_ready"), n + 1)
            for h in range(2):
                k = slice(4 * h, 4 * h + 4)
                m = ps[:, banks[0], 0:T].unsqueeze(1).to_broadcast([P, 4, T])
                last = ve.scalar_tensor_tensor(out=c[:, k, 0:T], in0=m, scalar=-1.0 / D, in1=x[:, k, 0:T],
                                               op0=ALU.mult, op1=ALU.add)
                last.then_inc(s("centred"), 1)
            ve.wait_ge(s("centred"), 2 * n + 2)
            ve.wait_ge(s("deviation_ready"), n + 1)
            dv(ve.reciprocal(RS[:, 0:T], RS[:, 0:T]))
            dv.join()
            ve.tensor_tensor(c[:, :, 0:T], c[:, :, 0:T], RS[:, 0:T].unsqueeze(1).to_broadcast([P, KT, T]), ALU.mult
                             ).then_inc(s("normed"), 1)
            ve.wait_ge(s("normed"), n + 1)

        def vector_mixer(ve, dv):
            def bc(ap, n):
                return ap.unsqueeze(len(ap.shape)).to_broadcast([*ap.shape, n])

            dv(ve.memset(eps1, EPS1))
            dv(ve.memset(one1, 1.0))
            dv.join()
            ve.nop().then_inc(s("eps_ready"), 1)
            ve.wait_ge(s("small_loaded"), 64)
            ve.wait_ge(s("x_loaded"), 32)
            lbp = prm("lb")
            ve.tensor_tensor(lbt, lbp, lbp, ALU.subtract).then_inc(s("lb_steps"), 1)
            ve.wait_ge(s("lb_steps"), 2)
            dv(ve.reciprocal(lb1, lbt))
            dv.join()
            dv(ve.tensor_tensor(lbt, lbt, lb1, ALU.mult))
            dv.join()
            dv(ve.tensor_tensor(lb_, lbt, lbt, ALU.subtract))
            dv.join()
            dv(ve.tensor_scalar(lb_, lb_, 0.0, 1.0 - 1e-6, ALU.max, ALU.min))
            dv.join()
            dv(ve.tensor_scalar(lb1, lb_, -1.0, 1.0, ALU.mult, ALU.add))
            ve.tensor_scalar(lbA, lb_, LB_FLOOR, None, ALU.max).then_inc(s("lb_steps"), 1)
            norm_vector(ve, dv, 0, X, C, TC, (4, 5))
            used(ve, N_ADA1 - 1)
            ve.tensor_tensor(mod[:, 0:16, :], ps[:, 0, 0:32].rearrange("p (j w) -> p j w", w=2),
                             bc(prm("b_ada")[:, 0:16], 2), ALU.add).then_inc(bank_read[0], 1)
            ve.wait_ge(bank_read[0], 1)
            ve.tensor_scalar(sc1, mod[:, 8:16, :].rearrange("p k w -> p (k w)"), 1.0, None,
                             ALU.add).then_inc(s("scale_ready"), 1)
            ve.wait_ge(s("scale_ready"), 1)
            scw = sc1.rearrange("p (k w) -> p k w", w=2)
            for k in range(KT):
                last = ve.tensor_scalar(hT[:, k, 0:T1], C[:, k, 0:T1], scw[:, k, 0:1], mod[:, k, 0:1],
                                        ALU.mult, ALU.add)
            last.then_inc(s("hT_ready"), 1)
            for d in range(2):
                ve.wait_ge(s("rank_rows"), d + 1)
                ve.tensor_copy(RT[0:16, d, :], ps[0:16, 4 + d, :]).then_inc(s("rank_rows_out"), 1)
            ve.wait_ge(s("rank_rows_out"), 2)
            ve.nop().then_inc(bank_read[4], 1)
            ve.nop().then_inc(bank_read[5], 1)
            for j in range(4):
                d, g = j // 2, j % 2
                ve.wait_ge(s("gla_rows"), j + 1)
                b = prm("b_gk")[:, j:j + 1]
                ve.tensor_scalar(by_cols(Z[:, d, 4 + g, 0:T1]), to_cols(ps[:, 4 + j, 0:T1]), b, None, ALU.add)
                ve.tensor_scalar(Z[:, d, 4 + g, T1:TC], ps[:, 4 + j, T1:TC], b, None, ALU.add
                                 ).then_inc(bank_read[4 + j], 1)
            n0 = N_ADA1 + 8

            def flat(t, d, g0, g1):
                return t[:, d, g0:g1, :].rearrange("p g t -> p (g t)")

            def gate_logs(d):
                ve.wait_ge(s("gate_ln1p"), 2 * d + 1)
                ve.wait_ge(bank_read[5 + 2 * d], 1 + 2 * (d == 0))
                dv(ve.scalar_tensor_tensor(out=flat(LA, d, 0, 6), in0=flat(Z, d, 0, 6), scalar=0.0,
                                           in1=flat(LA, d, 0, 6), op0=ALU.min, op1=ALU.subtract))
                dv.join()
                dv(ve.tensor_tensor(KX[:, d, 0:4, :], LA[:, d, 0:4, :], Z[:, d, 0:4, :], ALU.subtract))
                dv(ve.tensor_tensor(LA[:, d, 0:4, :], LA[:, d, 0:4, :], bc(lbC[:, 4 * d:4 * d + 4], TC), ALU.add))
                dv(ve.tensor_scalar(flat(LA, d, 4, 6), flat(LA, d, 4, 6), 1.0 / 16.0, None, ALU.mult))
                dv.join()
                ve.tensor_tensor(Z[:, d, 0:4, :], LA[:, d, 0:4, :], bc(lbA[:, 4 * d:4 * d + 4], TC),
                                 ALU.subtract).then_inc(s("gate_diff"), 1)

            def gate_finish(d):
                ve.wait_ge(s("gate_ln1p"), 2 * d + 2)
                dv(ve.tensor_tensor(K[:, d, 0:4, :], K[:, d, 0:4, :], bc(lb1[:, 4 * d:4 * d + 4], TC), ALU.mult))
                dv(ve.tensor_tensor(LA[:, d, 0:4, :], LA[:, d, 0:4, :], bc(lbA[:, 4 * d:4 * d + 4], TC), ALU.max))
                dv.join()
                dv(ve.tensor_tensor(LA[:, d, 0:4, :], LA[:, d, 0:4, :], Z[:, d, 0:4, :], ALU.add))
                dv.join()

            ve.wait_ge(s("lb_steps"), 5)
            dv(ve.tensor_scalar(lbA, lbA, -LN_SHIFT * float(np.log(2.0)), None, ALU.add))
            dv.join()
            gate_logs(0)
            for g in range(2):
                used(ve, n0 + g)
                for d in range(2):
                    ve.tensor_copy(by_cols(K[:, d, 4 + g, 0:T1]), to_cols(ps[:, g, 0:T1]))
                    last = ve.tensor_copy(K[:, d, 4 + g, T1:TC], ps[:, g, T1:TC])
                last.then_inc(bank_read[g], 1)
            for g in range(2):
                used(ve, n0 + 2 + g)
                ve.tensor_scalar(by_cols(Q[:, 4 + g, :]), to_cols(ps[:, 2 + g, 0:T1]), 0.125, None, ALU.mult
                                 ).then_inc(bank_read[2 + g], 1)
            gate_logs(1)
            for g in range(4):
                used(ve, n0 + 4 + g)
                ve.tensor_copy(Q[:, g, :], ps[:, g, 0:T1]).then_inc(bank_read[g], 1)
            for g in range(8):
                used(ve, n0 + 8 + g)
                ve.tensor_copy(GT[:, g, :], ps[:, g % 4, 0:T1]).then_inc(bank_read[g % 4], 1)
            gate_finish(0)
            gate_finish(1)
            n1 = n0 + 16
            for w in range(2):
                for t in range(4):
                    if t < 3:
                        ve.wait_ge(s("v_tiles"), 3 * w + t + 1)
                    else:
                        used(ve, n1 + 4 * w + 3)
                    ve.tensor_copy(V[:, t, 512 * w:512 * (w + 1)], ps[:, t, :]).then_inc(bank_read[t], 1)
            dv(ve.memset(PP[:, :, :, :, 0:1].rearrange("p d g w o -> p (d g w) o"), 0.0))
            one_b = one1.to_broadcast([P, T1])
            for d in range(2):
                for g in range(GROUPS):
                    for w in range(2):
                        last = dv(ve.tensor_tensor_scan(PP[:, d, g, w, 1:T1 + 1], one_b, LA[:, d, g, w * T1:(w + 1) * T1],
                                                        0.0, ALU.mult, ALU.add))
            dv.join()
            ve.nop().then_inc(s("prefix_ready"), 1)

            end = [bc(PP[:, 0, :, 1, T1], T1), bc(PP[:, 1, :, 0, T1], T1)]
            ve.tensor_tensor(KE[:, 0], end[0], PP[:, 0, :, 1, 1:T1 + 1], ALU.subtract).then_inc(s("end_exponents"), 1)
            ve.tensor_tensor(QE[:, 1], end[1], PP[:, 1, :, 0, 0:T1], ALU.subtract).then_inc(s("end_exponents"), 1)
            for d in range(2):
                ve.wait_ge(s("end_decays"), d + 1)
                ve.tensor_tensor(KE[:, d], KE[:, d], K[:, d, :, T1:TC], ALU.mult).then_inc(s("keys_decayed"), 1)
            for d in range(2):
                ve.wait_ge(s("end_decays"), 4)
                ve.tensor_tensor(QE[:, d], QE[:, d], Q, ALU.mult).then_inc(s("queries_decayed"), 1)

            def split(ap, m):
                v = ap.rearrange("p g (b m) -> p g b m", m=2 * m)
                return v[:, :, :, 0:m], v[:, :, :, m:2 * m]

            Pf, Pb = PP[:, 0, :, 0, :], PP[:, 1, :, 0, :]

            def exponents(lev):
                m = 1 << lev
                buf = AB[lev % 2]
                if lev >= 2:
                    ve.wait_ge(s("scores_ready"), lev - 1)
                Pf1, Pb0 = split(Pf[:, :, 1:T1 + 1], m), split(Pb[:, :, 0:T1], m)

                def mid(p):
                    v = p[:, :, 0:T1].rearrange("p g (b m) -> p g b m", m=2 * m)[:, :, :, m:m + 1]
                    return v.to_broadcast([P, GROUPS, T1 // (2 * m), m])

                (k1, k2), (q1, q2) = split(buf[:, 0], m), split(buf[:, 1], m)
                ve.tensor_tensor(k1, mid(Pf), Pf1[0], ALU.subtract)
                ve.tensor_tensor(k2, Pb0[1], mid(Pb), ALU.subtract)
                ve.tensor_tensor(q1, mid(Pb), Pb0[0], ALU.subtract)
                ve.tensor_tensor(q2, Pf1[1], mid(Pf), ALU.subtract).then_inc(s("level_exponents"), 1)

            def decayed(lev):
                m = 1 << lev
                buf = AB[lev % 2]
                ve.wait_ge(s("level_decays"), lev + 1)
                (a1, a2) = split(buf[:, 0], m)
                ve.tensor_tensor(a1, a1, split(K[:, 0, :, 0:T1], m)[0], ALU.mult)
                ve.tensor_tensor(a2, a2, split(K[:, 1, :, 0:T1], m)[1], ALU.mult)
                ve.tensor_tensor(buf[:, 1], buf[:, 1], Q, ALU.mult).then_inc(s("level_ready"), 1)

            def masked(lev):
                ve.wait_ge(s("scores_ready"), lev + 1)
                b0 = 4 * (lev % 2)
                if lev == LEVELS - 1:
                    last = dv(ve.tensor_copy(X8.rearrange("p h c t -> p (h c t)"),
                                             ps[:, b0:b0 + 4, :].rearrange("p b n -> p (b n)")))
                else:
                    last = dv(ve.copy_predicated(SCO.rearrange("p h c t -> p (h c) t"),
                                                 mask[:, min(lev, 7), :].unsqueeze(1).to_broadcast([P, 16, P]),
                                                 ps[:, b0:b0 + 4, :].rearrange("p b (j t) -> p (b j) t", t=P)))
                dv.join()
                for b in range(4):
                    ve.nop().then_inc(bank_read[b0 + b], 1)

            exponents(0)
            exponents(1)
            for j in range(6):
                ve.wait_ge(s("keys_turned"), j + 1)
                d, g = j // 3, 2 * (j % 3)
                dv(ve.tensor_copy(KE[:, d, g:g + 2, :].rearrange("p g t -> p (g t)"), ps[:, j, :]))
                dv.join()
                ve.nop().then_inc(s("turned_out"), 1)
                ve.nop().then_inc(bank_read[j], 1)
            used(ve, N_ADA1 + N_PROJ1 + N_ADA2 - 1)
            ve.tensor_tensor(mod[:, 16:48, :], ps[:, 6, 0:64].rearrange("p (j w) -> p j w", w=2),
                             bc(prm("b_ada")[:, 16:48], 2), ALU.add).then_inc(bank_read[6], 1)
            for j, b in enumerate((6, 7, 0)):
                ve.wait_ge(s("states_ready"), j + 1)
                dv(ve.tensor_copy(ST[:, 4 * j:4 * j + 4, :].rearrange("p g v -> p (g v)"), ps[:, b, :]))
                dv.join()
                ve.nop().then_inc(s("states_out"), 1)
                ve.nop().then_inc(bank_read[b], 1)
            decayed(0)
            for lev in range(LEVELS):
                if lev + 1 < LEVELS:
                    decayed(lev + 1)
                masked(lev)
                if lev + 2 < LEVELS:
                    exponents(lev + 2)
            ve.wait_ge(s("scores_ready"), LEVELS - 1)
            ve.tensor_tensor(AB[0][:, 0], K[:, 0, :, 0:T1], K[:, 1, :, 0:T1], ALU.add).then_inc(s("level_ready"), 1)
            masked(LEVELS)
            ve.nop().then_inc(s("scores_masked"), 1)
            ve.wait_ge(s("keys_turned"), 6)
            for b in range(4):
                ve.wait_ge(s("head_deviation"), b + 1)
                r = ORS[:, b * 512:(b + 1) * 512]
                dv(ve.reciprocal(r, r))
                dv.join()
                dv(ve.tensor_tensor(ON[:, 2 * b:2 * b + 2, :].rearrange("p h t -> p (h t)"), ps[:, 4 + b, :], r, ALU.mult))
                dv.join()
                ve.nop().then_inc(bank_read[4 + b], 1)
            ve.wait_ge(s("gates_ready"), 1)
            for hi, (g, _, _, _, kt) in enumerate(HEAD_AT):
                o, src, gate = MIX[:, kt, :], ON[:, hi, :], GT[:, kt, :]
                gain = prm("hg_norm" if g < 4 else "gla_norm")
                if g >= 4:
                    o, gate = to_cols(o), to_cols(gate)
                    src = by_cols(src)
                last = ve.scalar_tensor_tensor(out=o, in0=src, scalar=gain, in1=gate, op0=ALU.mult, op1=ALU.mult)
            last.then_inc(s("mix_ready"), 1)
            n = N_ADA1 + N_PROJ1 + N_ADA2
            ve.wait_ge(s("ax_loaded"), 16)
            dv(ve.tensor_scalar(AXT, AXT, ALPHA1, None, ALU.mult))
            dv.join()
            for j in range(8):
                used(ve, n + j)
                dv(ve.scalar_tensor_tensor(out=Y1[:, j, :], in0=ps[:, j % 4, 0:T1], scalar=mod[:, 16 + j, 0:1],
                                           in1=AXT[:, j, :], op0=ALU.mult, op1=ALU.add))
                dv.join()
                ve.nop().then_inc(bank_read[j % 4], 1)
                ve.nop().then_inc(s("y1_ready"), 1)
            norm_vector(ve, dv, 1, Y1, C1, T1, (4, 5))
            for k in range(KT):
                last = ve.tensor_scalar(xT[:, k, 0:T1], C1[:, k, :], prm("gamma")[:, k:k + 1], prm("beta")[:, k:k + 1],
                                        ALU.mult, ALU.add)
            last.then_inc(s("x1_ready"), 1)

        def vector_peer(ve, dv):
            def bc(ap, n):
                return ap.unsqueeze(len(ap.shape)).to_broadcast([*ap.shape, n])

            dv(ve.tensor_scalar(sc2, mod[:, 32:40, 0], 1.0, None, ALU.add))
            norm_vector(ve, dv, 2, xT, H2, T1, (4, 5))
            dv.join()
            for k in range(KT):
                last = ve.tensor_scalar(H2[:, k, :], H2[:, k, :], sc2[:, k:k + 1], mod[:, 24 + k, 0:1], ALU.mult, ALU.add)
            last.then_inc(s("h2_ready"), 1)

            def best16(tt, n, src, alt, vals, idx):
                for j in range(n):
                    dv(ve.max(vals[:, tt, j, 0:8], src[:, tt, j, :]))
                dv.join()
                for j in range(n):
                    dv(ve.match_replace(alt[:, tt, j, :], vals[:, tt, j, 0:8], src[:, tt, j, :], -3.0e38))
                for j in range(n):
                    dv(ve.max_index(idx[:, tt, j, 0:8], vals[:, tt, j, 0:8], src[:, tt, j, :]))
                dv.join()
                for j in range(n):
                    dv(ve.max(vals[:, tt, j, 8:16], alt[:, tt, j, :]))
                dv.join()
                for j in range(n):
                    dv(ve.max_index(idx[:, tt, j, 8:16], vals[:, tt, j, 8:16], alt[:, tt, j, :]))
                dv.join()

            for tt in range(2):
                ve.wait_ge(s("key_scores_out"), 4 * tt + 4)
                best16(tt, 16, S0, S1, TV, TI.bitcast(U32))
                dv(ve.tensor_copy(TF[:, tt], TI[:, tt].bitcast(U32)))
                tv = TV[:, tt].rearrange("p (h w) k -> p h w k", w=2)
                dv(ve.tensor_tensor(CA[:, tt].rearrange("p h (i j) -> p h i j", i=16), bc(tv[:, :, 0, :], 16),
                                    tv[:, :, 1, :].unsqueeze(2).to_broadcast([P, 8, 16, 16]), ALU.add))
                dv.join()
                best16(tt, 8, CA, CB, BV, BP.rearrange("p a (h k) -> p a h k", h=8).bitcast(U32))
                bp = BP[:, tt].bitcast(U32)
                dv(ve.tensor_scalar(BI[:, tt, 0].bitcast(U32), bp, 4, None, ALU.logical_shift_right))
                dv(ve.tensor_scalar(BI[:, tt, 1].bitcast(U32), bp, 15, None, ALU.bitwise_and))
                dv.join()
                dv(ve.tensor_copy(BF[:, tt], BI[:, tt].bitcast(U32)))
                dv.join()
                tf = TF[:, tt].rearrange("p (h w) k -> p h w k", w=2)
                for w in range(2):
                    dv(ve.tensor_tensor(EQ[:, w], bc(BF[:, tt, w], 16),
                                        row16.unsqueeze(1).to_broadcast([P, 128, 16]), ALU.is_equal))
                for w in range(2):
                    dv.join()
                    dv(ve.tensor_tensor(PR.rearrange("p (h k) i -> p h k i", h=8),
                                        EQ[:, w].rearrange("p (h k) i -> p h k i", h=8),
                                        tf[:, :, w, :].unsqueeze(2).to_broadcast([P, 8, 16, 16]), ALU.mult))
                    dv.join()
                    dv(ve.tensor_reduce(CH[:, tt, w], PR, AX.X, ALU.add))
                g = CH[:, tt, 2].rearrange("p (h k) -> p h k", h=8)
                ve.tensor_tensor(g, BV[:, tt], BV[:, tt, :, 0:1].to_broadcast([P, 8, 16]), ALU.subtract
                                 ).then_inc(s("pair_exponents"), 1)
                ve.wait_ge(s("pair_exps"), tt + 1)
                dv(ve.tensor_reduce(SM[:, tt], g, AX.X, ALU.add))
                dv.join()
                dv(ve.reciprocal(SM[:, tt], SM[:, tt]))
                dv.join()
                ve.tensor_tensor(g, g, bc(SM[:, tt], 16), ALU.mult).then_inc(s("choices_ready"), 1)
            for tt in range(2):
                ve.wait_ge(s("choices_turned"), tt + 1)
                ve.tensor_copy(TT[:, :, tt * P:(tt + 1) * P], ps[:, 4 + tt, 0:384].rearrange("p (w t) -> p w t", w=3)
                               ).then_inc(s("choices_out"), 1)
            ve.wait_ge(s("choices_out"), 2)
            for tt in range(2):
                ve.nop().then_inc(bank_read[4 + tt], 1)

            def onehots(i, first):
                for u in range(2):
                    if not first:
                        ve.wait_ge(s("weights_built"), i * 2 + (u - 1))
                    for w in range(8):
                        t = i * 16 + (8 * u + w)
                        ve.tensor_scalar(OH[u][:, 0, w, :], row, TT[:, 0, bass.ds(t, 1)], None, ALU.is_equal)
                        last = ve.tensor_scalar(OH[u][:, 1, w, :], row, TT[:, 1, bass.ds(t, 1)], TT[:, 2, bass.ds(t, 1)],
                                                ALU.is_equal, ALU.mult)
                    last.then_inc(s("onehots_ready"), 1)

            onehots(0, True)
            with ve.Fori(1, 16) as i:
                onehots(i, False)

            def gate(j, par, gelus, downs):
                ve.wait_ge(s("gelu_done"), gelus)
                if downs is not None:
                    ve.wait_ge(us[downs[0]], downs[1])
                ve.tensor_tensor(GW[par], GEL[par], W[:, :, bass.ds(j, 1)].rearrange("p t o -> p (t o)"), ALU.mult
                                 ).then_inc(s("gated"), 1)

            t0 = STREAM1 // SLOTS
            ve.wait_ge(s("weights_copied"), 32)
            gate(0, 0, 1, None)
            gate(1, 1, 2, None)
            with ve.Fori(1, PN // 2) as m:
                gate(m * 2, 0, m * 2 + 1, (2, m + t0))
                gate(m * 2 + 1, 1, m * 2 + 2, (0, m + (t0 + 1)))
            used(ve, down_block(PN - 1))
            dv(ve.tensor_scalar(AX2, xT[:, :, 0:T1], ALPHA1, None, ALU.mult))
            for b in range(2):
                ve.tensor_copy(YS[:, b, :].rearrange("p (h n) -> p h n", h=2)[:, 0, :], ps[:, 2 * b, :]
                               ).then_inc(s("experts_out"), 1)
            dv.join()
            for b in range(4):
                ve.wait_ge(s("experts_turned"), b + 1)
                for w in range(2):
                    k = 2 * b + w
                    dv(ve.scalar_tensor_tensor(out=Y2[:, k, :], in0=ps[:, 4 + b, w * T1:(w + 1) * T1],
                                               scalar=mod[:, 40 + k, 0:1], in1=AX2[:, k, :], op0=ALU.mult, op1=ALU.add))
                dv.join()
                ve.nop().then_inc(bank_read[4 + b], 1)
            ve.nop().then_inc(s("y2_ready"), 1)
            norm_vector(ve, dv, 3, Y2, C2, T1, (4, 5))
            for k in range(KT):
                last = ve.tensor_scalar(xT[:, k, 16:16 + T1], C2[:, k, :], prm("gamma")[:, 8 + k:9 + k],
                                        prm("beta")[:, 8 + k:9 + k], ALU.mult, ALU.add)
            last.then_inc(s("h_ready"), 1)

        def vector_layers(ve, dv):
            def bc(ap, n):
                return ap.unsqueeze(len(ap.shape)).to_broadcast([*ap.shape, n])

            ve.wait_ge(s("h_ready"), 1)
            dv(ve.memset(XR[:, :, 0:3], 0.0))
            dv(ve.memset(coef, -1.0))
            dv(ve.memset(eps2, EPS2))
            dv(ve.memset(eps2x4, 4 * EPS2))
            dv.join()
            ve.nop().then_inc(s("eps2_ready"), 1)
            ve.wait_ge(s("const2_loaded"), 16)
            for L in range(NL):
                def read(*banks):
                    dv.join()
                    for b in banks:
                        ve.nop().then_inc(bank_read[b], 1)

                def at_layer(name, n):
                    return L * PER[name] + n

                def turn(pos):
                    return L * (PER_LAYER // SLOTS) + (BASE2 // SLOTS + pos // SLOTS + 1)

                def done(pos):
                    ve.wait_ge(us[pos % SLOTS], turn(pos))

                def norm(i):
                    ve.wait_ge(s("mean2"), L * 3 + (i + 1))
                    for h in range(2):
                        k = slice(4 * h, 4 * h + 4)
                        ve.scalar_tensor_tensor(out=hC[:, k, :], in0=ps[:, 6, 0:T2].unsqueeze(1).to_broadcast([P, 4, T2]),
                                                scalar=-1.0 / D, in1=hY[:, k, :], op0=ALU.mult, op1=ALU.add
                                                ).then_inc(s("centred2"), 1)
                    ve.wait_ge(s("centred2"), L * 6 + (2 * i + 2))
                    ve.nop().then_inc(bank_read[6], 1)
                    ve.wait_ge(s("deviation2"), L * 3 + (i + 1))
                    dv(ve.reciprocal(RS[:, 0:T2], RS[:, 0:T2]))
                    dv.join()
                    ve.tensor_tensor(hC, hC, RS[:, 0:T2].unsqueeze(1).to_broadcast([P, KT, T2]), ALU.mult
                                     ).then_inc(s("normed2"), 1)
                    ve.wait_ge(s("normed2"), L * 3 + (i + 1))
                    for k in range(KT):
                        last = ve.tensor_scalar(xT[:, k, :], hC[:, k, :], p2("ln_g")[:, 8 * i + k:8 * i + k + 1],
                                                p2("ln_b")[:, 8 * i + k:8 * i + k + 1], ALU.mult, ALU.add)
                    last.then_inc(s("h_ready"), 1)

                def ffn(w, pos):
                    def hidden(i):
                        for u in range(2):
                            ve.wait_ge(s("silu_done"), i * 2 + at_layer("silu_done", 22 * w + u + 1))
                            ve.wait_ge(us[2 * u + 1], i + turn(pos))
                            ve.tensor_tensor(HID[:, bass.ds(i * 2 + u, 1), :].rearrange("p o t -> p (o t)"), SG[u],
                                             ps[:, 2 * u + 1, 0:T2], ALU.mult).then_inc(s("hidden_done"), 1)

                    with ve.Fori(0, FT // 2) as i:
                        hidden(i)
                    ve.wait_ge(s("hidden_done"), at_layer("hidden_done", 22 * (w + 1)))
                    for b in (1, 3):
                        ve.nop().then_inc(bank_read[b], 1)

                    with ve.Fori(0, 4) as i:
                        for u in range(2):
                            ve.wait_ge(us[2 * u + 1], i + turn(pos + N_GU))
                            ve.scalar_tensor_tensor(out=hY[:, bass.ds(i * 2 + u, 1), :].rearrange("p o t -> p (o t)"),
                                                    in0=xT[:, bass.ds(i * 2 + u, 1), :].rearrange("p o t -> p (o t)"),
                                                    scalar=2.0 * ALPHA2, in1=ps[:, 4 + u, 0:T2], op0=ALU.mult, op1=ALU.add
                                                    ).then_inc(s("y_parts"), 1)
                    ve.wait_ge(s("y_parts"), at_layer("y_parts", 16 * w + 8))
                    for b in (4, 5):
                        ve.nop().then_inc(bank_read[b], 1)

                ffn(0, 0)
                ve.wait_ge(s("prm2_loaded"), L * 16 + 16)
                norm(0)
                q0 = AT_PROJ
                done(q0)
                dv(ve.tensor_scalar(SP[0:64, :], ps[0:64, 0, 0:T2], p2("row_bias")[0:64, :], sign[0:64, :], ALU.add, ALU.mult))
                dv(ve.tensor_tensor(KR[64:96, 0, :], ps[64:96, 0, 0:T2], rope_t[64:96, :], ALU.mult))
                dv(ve.tensor_tensor(KR[64:96, 1, :], ps[96:128, 0, 0:T2], rope_t[96:128, :], ALU.mult))
                read(0)
                ve.nop().then_inc(s("rows_in"), 1)
                dv(ve.tensor_tensor(KM[64:96, :, :], KR[64:96, 0:1, :].to_broadcast([32, 4, T2]),
                                    KR[64:96, 1:2, :].to_broadcast([32, 4, T2]), ALU.add))
                for j in range(2):
                    ve.wait_ge(s("latent_deviation"), L * 2 + (j + 1))
                    dv(ve.reciprocal(CRS[:, j, :], CRS[:, j, :]))
                    dv.join()
                    for k in ((0, 1) if j == 0 else (2,)):
                        g = p2("q_g")[:, k:k + 1] if j == 0 else p2("kv_g")
                        last = ve.scalar_tensor_tensor(out=CQ[:, k, :], in0=CQ[:, k, :], scalar=g, in1=CRS[:, j, :],
                                                       op0=ALU.mult, op1=ALU.mult)
                    last.then_inc(s("latents_normed"), 1)
                ve.wait_ge(s("rows_ln"), L + 1)
                dv(ve.scalar_tensor_tensor(out=SP[0:64, :], in0=SP[0:64, :], scalar=0.0, in1=LN_[0:64, :],
                                           op0=ALU.max, op1=ALU.add))
                dv(ve.tensor_scalar(coef[0:8, :], coef[0:8, :], -1.0, None, ALU.mult))
                dv.join()
                dv(ve.tensor_scalar(LN_[0:64, :], SP[0:64, :], coef[0:64, :], None, ALU.mult))
                dv.join()
                ve.tensor_tensor_scan(AC[0:64, :], one1[0:64, :].to_broadcast([64, T2]), LN_[0:64, :], 0.0,
                                      ALU.mult, ALU.add).then_inc(s("rows_ready"), 1)
                for tt, (a, n) in enumerate(TILES):
                    if tt < 2:
                        ve.wait_ge(s("fox_values"), L * 2 + (tt + 1))
                    else:
                        done(q0 + 15)
                    dv(ve.tensor_copy(FV[0:n, tt, :], ps[0:n, 4 + tt, 0:256]))
                read(4, 5, 6)
                for j in range(6):
                    ve.wait_ge(s("conv_rows"), L * 6 + (j + 1))
                    w = p2("conv_w")
                    dv(ve.tensor_scalar(XV[:, j, :], XR[:, j, 3:3 + T2], w[:, 18 + j:19 + j], p2("conv_b")[:, j:j + 1],
                                        ALU.mult, ALU.add))
                for i in range(3):
                    dv.join()
                    for j in range(6):
                        dv(ve.scalar_tensor_tensor(out=XV[:, j, :], in0=XR[:, j, i:i + T2],
                                                   scalar=p2("conv_w")[:, 6 * i + j:6 * i + j + 1],
                                                   in1=XV[:, j, :], op0=ALU.mult, op1=ALU.add))
                dv.join()
                ve.nop().then_inc(s("conv_sums"), 1)
                for h in range(4):
                    if h % 2 == 0:
                        ve.wait_ge(s("mla_q"), L * 2 + (h // 2 + 1))
                    else:
                        done(q0 + 16 + h // 2)
                    dv(ve.tensor_copy(QM[0:64, h, :], ps[0:64, h, 0:T2]))
                    dv(ve.tensor_tensor(QM[64:96, h, :], ps[64:96, h, 0:T2], rope_t[64:96, :], ALU.mult))
                    dv(ve.tensor_tensor(KR[64:96, h % 2, :], ps[96:128, h, 0:T2], rope_t[96:128, :], ALU.mult))
                    read(h)
                    dv(ve.tensor_tensor(QM[64:96, h, :], QM[64:96, h, :], KR[64:96, h % 2, :], ALU.add))
                for h in range(4):
                    if h < 3:
                        ve.wait_ge(s("mla_k"), L * 3 + (h + 1))
                    else:
                        done(q0 + 18)
                    dv(ve.tensor_copy(KM[0:64, h, :], ps[0:64, 4 + h, 0:T2]))
                read(4, 5, 6, 7)
                for tt, (a, n) in enumerate(TILES):
                    if tt < 2:
                        ve.wait_ge(s("mla_v"), L * 2 + (tt + 1))
                    else:
                        done(q0 + 19)
                    dv(ve.tensor_copy(MV[0:n, tt, :], ps[0:n, tt, 0:256]))
                read(0, 1, 2)
                for tt, (a, n) in enumerate(TILES):
                    ve.wait_ge(s("rows_turned"), L * 3 + (tt + 1))
                    dv(ve.tensor_copy(TR[0:n, tt, :], ps[0:n, tt, 0:P]))
                read(0, 1, 2)
                for tt, (a, n) in enumerate(TILES):
                    ve.wait_ge(s("x_turned"), L * 3 + (tt + 1))
                    dv(ve.tensor_tensor(XD[0:n, tt, :].rearrange("p (h d) -> p h d", h=8),
                                        ps[0:n, 3 + tt, :].rearrange("p (h d) -> p h d", h=8),
                                        bc(TR[0:n, tt, 64:72], 64), ALU.mult))
                read(3, 4, 5)
                for a_ in range(2):
                    if a_ == 0:
                        ve.wait_ge(s("fox_rows"), L * 4 + 4)
                        dv(ve.tensor_copy(BI2[:, :, :], ps[:, 0:4, 0:T2]))
                        read(0, 1, 2, 3)
                    ve.nop().then_inc(s("attn_inputs"), 1)
                    for qt, (a, n) in enumerate(TILES):
                        nk, pb = a + n, PB[(3 * a_ + qt) % 2]
                        b3 = [n, 4, nk]
                        m_ = maskq[0:n, qt, 0:nk].unsqueeze(1).to_broadcast(b3)
                        if a_ == 0:
                            dv(ve.tensor_tensor(EB[1][0:n, :, 0:nk], m_, BI2[0:n, :, 0:nk], ALU.subtract))
                            dv.join()
                            dv(ve.tensor_tensor(EB[0][0:n, :, 0:nk], EB[1][0:n, :, 0:nk], bc(TR[0:n, qt, 32:36], nk), ALU.add))
                            m_, scale = EB[0][0:n, :, 0:nk], 64.0 ** -0.5
                        else:
                            scale = 96.0 ** -0.5
                        dv.join()
                        ve.wait_ge(s("logits_ready"), L * 6 + (3 * a_ + qt + 1))
                        if 3 * a_ + qt >= 2:
                            ve.wait_ge(s("probs_turned"), L * 12 + TURNED[3 * a_ + qt - 2])
                        dv(ve.scalar_tensor_tensor(out=pb[0:n, :, 0:nk], in0=ps[0:n, 0:4, 0:nk], scalar=scale,
                                                   in1=m_, op0=ALU.mult, op1=ALU.add))
                        read(0, 1, 2, 3)
                        dv(ve.tensor_reduce(mxs[0:n, 0:4], pb[0:n, :, 0:nk], AX.X, ALU.max))
                        dv.join()
                        ve.tensor_tensor(pb[0:n, :, 0:nk], pb[0:n, :, 0:nk], bc(mxs[0:n, 0:4], nk), ALU.subtract
                                         ).then_inc(s("attn_exponents"), 1)
                        ve.wait_ge(s("attn_exps"), L * 6 + (3 * a_ + qt + 1))
                        dv(ve.tensor_reduce(sms[0:n, 0:4], pb[0:n, :, 0:nk], AX.X, ALU.add))
                        dv.join()
                        dv(ve.reciprocal(sms[0:n, 0:4], sms[0:n, 0:4]))
                        dv.join()
                        ve.tensor_tensor(pb[0:n, :, 0:nk], pb[0:n, :, 0:nk], bc(sms[0:n, 0:4], nk), ALU.mult
                                         ).then_inc(s("probs_ready"), 1)
                for g in range(2):
                    for kt, (a, n) in enumerate(TILES):
                        e = EB[(3 * g + kt) % 2]
                        ve.wait_ge(s("ssd_products"), L * 6 + (3 * g + kt + 1))
                        if 3 * g + kt >= 2:
                            ve.wait_ge(s("ssd_outputs"), L * 6 + (3 * g + kt - 1))
                        else:
                            ve.wait_ge(s("probs_ready"), L * 6 + 6)
                        for h in range(4):
                            dv(ve.scalar_tensor_tensor(out=e[0:n, h, a:T2], in0=ps[0:n, h, a:T2],
                                                       scalar=TR[0:n, kt, 4 * g + h:4 * g + h + 1],
                                                       in1=maskt[0:n, kt, a:T2], op0=ALU.subtract, op1=ALU.add))
                        dv.join()
                        ve.nop().then_inc(s("ssd_exponents"), 1)
                        if kt == 2:
                            read(0, 1, 2, 3)
                        ve.wait_ge(s("ssd_exps"), L * 6 + (3 * g + kt + 1))
                        dv(ve.tensor_tensor(e[0:n, :, a:T2], e[0:n, :, a:T2],
                                            ps[0:n, 4 + kt % 2, a:T2].unsqueeze(1).to_broadcast([n, 4, T2 - a]), ALU.mult))
                        read(4 + kt % 2)
                        ve.nop().then_inc(s("ssd_weights"), 1)
                    ve.wait_ge(s("ssd_outputs"), L * 6 + (3 * g + 3))
                    for j in range(2):
                        k = 2 * g + j
                        dv(ve.scalar_tensor_tensor(out=YG[:, k, :], in0=XV[:, k, :], scalar=p2("d_skip")[:, k:k + 1],
                                                   in1=ps[:, 6 + j, 0:T2], op0=ALU.mult, op1=ALU.add))
                    read(6, 7)
                    ve.wait_ge(s("z_gates"), L + 1)
                    ve.tensor_tensor(YG[:, 2 * g:2 * g + 2, :], YG[:, 2 * g:2 * g + 2, :], ZS[:, 2 * g:2 * g + 2, :],
                                     ALU.mult).then_inc(s("ssd_gated"), 1)
                for g in range(2):
                    ve.wait_ge(s("ssd_deviation"), L * 2 + (g + 1))
                    dv(ve.reciprocal(CRS[:, g, :], CRS[:, g, :]))
                    dv.join()
                    for j in range(2):
                        k = 2 * g + j
                        dv(ve.scalar_tensor_tensor(out=MX[:, k, :], in0=YG[:, k, :], scalar=p2("ssd_g")[:, k:k + 1],
                                                   in1=CRS[:, g, :], op0=ALU.mult, op1=ALU.mult))
                dv.join()
                ve.wait_ge(s("attended_out"), L * 4 + 4)
                ve.nop().then_inc(s("mixed"), 1)
                for j in range(8):
                    done(AT_OUT + j)
                    dv(ve.scalar_tensor_tensor(out=hY[:, j, :], in0=xT[:, j, :], scalar=ALPHA2, in1=ps[:, j % 4, 0:T2],
                                               op0=ALU.mult, op1=ALU.add))
                    read(j % 4)
                    ve.nop().then_inc(s("y_parts"), 1)
                norm(1)
                ffn(1, AT_FFN2)
                norm(2)

        def norm_scalar(act, n, c, sq, T, banks, eps, scale=1.0 / D):
            for h in range(2):
                act.wait_ge(s("centred"), 2 * n + h + 1)
                if n:
                    act.wait_ge(s("var_ready"), n)
                act.activation(sq[:, 4 * h:4 * h + 4, 0:T], c[:, 4 * h:4 * h + 4, 0:T], ACT.Square
                               ).then_inc(s("squares_ready"), 1)
            act.wait_ge(s("var_ready"), n + 1)
            act.activation(RS[:, 0:T], ps[:, banks[1], 0:T], ACT.Sqrt, bias=eps, scale=scale
                           ).then_inc(s("deviation_ready"), 1)
            act.wait_ge(s("deviation_ready"), n + 1)
            act.nop().then_inc(bank_read[banks[0]], 1)
            act.nop().then_inc(bank_read[banks[1]], 1)

        def scalar_mixer(act, ac):
            act.wait_ge(s("small_loaded"), 64)
            act.wait_ge(s("x_loaded"), 32)
            act.wait_ge(s("eps_ready"), 1)
            act.activation(silc, prm("c"), ACT.Silu).then_inc(s("silu_c"), 1)
            act.wait_ge(s("lb_steps"), 1)
            act.activation(lbt, lbt, ACT.Exp).then_inc(s("lb_steps"), 1)
            act.wait_ge(s("lb_steps"), 3)
            act.activation(lbA, lbA, ACT.Ln, scale=2.0 ** LN_SHIFT).then_inc(s("lb_steps"), 1)
            act.activation(lbC, lb1, ACT.Ln).then_inc(s("lb_steps"), 1)
            norm_scalar(act, 0, C, SQ, TC, (4, 5), eps1)
            act.wait_ge(s("scale_ready"), 1)
            act.wait_ge(s("normed"), 1)
            scw = sc1.rearrange("p (k w) -> p k w", w=2)
            for k in range(KT):
                last = act.activation(hT[:, k, T1:TC], C[:, k, T1:TC], ACT.Identity, bias=mod[:, k, 1:2],
                                      scale=scw[:, k, 1:2])
            last.then_inc(s("hT_ready"), 1)
            for j in range(8):
                used(act, N_ADA1 + j)
                act.copy(Z[:, j // 4, j % 4, :], ps[:, j % 4, :]).then_inc(bank_read[j % 4], 1)
            act.wait_ge(bank_read[3], 2)

            def flat(t, d, g0, g1):
                return t[:, d, g0:g1, :].rearrange("p g t -> p (g t)")

            def step(*a, **k):
                ac(act.activation(*a, **k))
                ac.join()

            for d in range(2):
                act.wait_ge(bank_read[5 + 2 * d], 1 + 2 * (d == 0))
                step(flat(LA, d, 0, 6), flat(Z, d, 0, 6), ACT.Abs)
                step(flat(LA, d, 0, 6), flat(LA, d, 0, 6), ACT.Exp, scale=-1.0)
                act.activation(flat(LA, d, 0, 6), flat(LA, d, 0, 6), ACT.Ln, bias=1.0).then_inc(s("gate_ln1p"), 1)
                act.wait_ge(s("gate_diff"), d + 1)
                step(flat(K, d, 0, 4), flat(KX, d, 0, 4), ACT.Exp)
                step(flat(Z, d, 0, 4), flat(Z, d, 0, 4), ACT.Abs)
                step(flat(Z, d, 0, 4), flat(Z, d, 0, 4), ACT.Exp, scale=-1.0)
                act.activation(flat(Z, d, 0, 4), flat(Z, d, 0, 4), ACT.Ln, bias=1.0).then_inc(s("gate_ln1p"), 1)
            act.wait_ge(s("prefix_ready"), 1)
            act.wait_ge(s("end_exponents"), 1)
            ef = s("end_decays")
            act.activation(KE[:, 0], KE[:, 0], ACT.Exp).then_inc(ef, 1)
            act.activation(KE[:, 1], PP[:, 1, :, 1, 0:T1], ACT.Exp).then_inc(ef, 1)
            act.activation(QE[:, 0], PP[:, 0, :, 0, 1:T1 + 1], ACT.Exp).then_inc(ef, 1)
            act.wait_ge(s("end_exponents"), 2)
            act.activation(QE[:, 1], QE[:, 1], ACT.Exp).then_inc(ef, 1)
            for lev in range(LEVELS):
                act.wait_ge(s("level_exponents"), lev + 1)
                buf = AB[lev % 2].rearrange("p a g t -> p (a g t)")
                act.activation(buf, buf, ACT.Exp).then_inc(s("level_decays"), 1)
            gt = GT.rearrange("p k t -> p (k t)")
            act.wait_ge(s("prefix_ready"), 1)
            act.activation(gt, gt, ACT.Silu).then_inc(s("gates_ready"), 1)
            act.wait_ge(s("outputs_ready"), 1)
            for b in range(4):
                act.activation(OSQ[:, b * 512:(b + 1) * 512], ps[:, 4 + b, :], ACT.Square).then_inc(s("output_squares"), 1)
            for b in range(4):
                act.wait_ge(s("head_sums"), b + 1)
                act.activation(ORS[:, b * 512:(b + 1) * 512], ps[:, b, :], ACT.Sqrt, bias=eps1, scale=1.0 / P
                               ).then_inc(s("head_deviation"), 1)
                act.wait_ge(s("head_deviation"), b + 1)
                act.nop().then_inc(bank_read[b], 1)
            norm_scalar(act, 1, C1, SQ1, T1, (4, 5), eps1)

        def scalar_peer(act, ac):
            norm_scalar(act, 2, H2, SQH, T1, (4, 5), eps1)
            n = STREAM1 - N_WQ
            for j in range(16):
                used(act, n + j)
                act.copy(QT[:, j, :], ps[:, j % 4, 0:T1]).then_inc(s("queries_out"), 1)
                act.wait_ge(s("queries_out"), j + 1)
                act.nop().then_inc(bank_read[j % 4], 1)
            for tt in range(2):
                for b in range(4):
                    act.wait_ge(s("key_scores"), 4 * tt + b + 1)
                    act.copy(S0[:, tt, 4 * b:4 * b + 4, :].rearrange("p a n -> p (a n)"), ps[:, 4 - 4 * tt + b, :]
                             ).then_inc(s("key_scores_out"), 1)
            act.wait_ge(s("key_scores_out"), 8)
            for b in range(8):
                act.nop().then_inc(bank_read[b], 1)
            for tt in range(2):
                act.wait_ge(s("pair_exponents"), tt + 1)
                act.activation(CH[:, tt, 2], CH[:, tt, 2], ACT.Exp).then_inc(s("pair_exps"), 1)
            act.wait_ge(s("choices_turned"), 2)

            def copies(i):
                for u in range(2):
                    act.wait_ge(s("weights_built"), i * 2 + (u + 1))
                    act.copy(W[:, bass.ds(i * 16 + 8 * u, 8), :].rearrange("p t n -> p (t n)"),
                             ps[:, 2 * u:2 * u + 2, :].rearrange("p b n -> p (b n)")).then_inc(s("weights_copied"), 1)

            with act.Fori(0, 16) as i:
                copies(i)

            def gelu(par, b, turn, gated):
                act.wait_ge(us[b], turn)
                if gated is not None:
                    act.wait_ge(s("gated"), gated)
                act.activation(GEL[par], ps[:, 4 + par, 0:T1], ACT.Gelu_apprx_tanh).then_inc(s("gelu_done"), 1)

            t0 = STREAM1 // SLOTS
            gelu(0, 0, t0 + 1, None)
            gelu(1, 1, t0 + 1, None)
            with act.Fori(1, PN // 2) as m:
                gelu(0, 3, m + t0, m * 2 - 1)
                gelu(1, 1, m + (t0 + 1), m * 2)
            used(act, down_block(PN - 1))
            for b in range(2):
                act.copy(YS[:, b, :].rearrange("p (h n) -> p h n", h=2)[:, 1, :], ps[:, 2 * b + 1, :]
                         ).then_inc(s("experts_out"), 1)
            act.wait_ge(s("experts_out"), 4)
            for b in range(6):
                act.nop().then_inc(bank_read[b], 1)
            norm_scalar(act, 3, C2, SQ2, T1, (4, 5), eps1)

        def scalar_layers(act, ac):
            act.wait_ge(s("eps2_ready"), 1)
            for L in range(NL):
                def read(*banks):
                    ac.join()
                    for b in banks:
                        act.nop().then_inc(bank_read[b], 1)

                def at_layer(name, n):
                    return L * PER[name] + n

                def turn(pos):
                    return L * (PER_LAYER // SLOTS) + (BASE2 // SLOTS + pos // SLOTS + 1)

                def done(pos):
                    act.wait_ge(us[pos % SLOTS], turn(pos))

                def norm(i):
                    for h in range(2):
                        act.wait_ge(s("centred2"), L * 6 + (2 * i + h + 1))
                        act.activation(hSQ[:, 4 * h:4 * h + 4, :], hC[:, 4 * h:4 * h + 4, :], ACT.Square
                                       ).then_inc(s("squares2"), 1)
                    act.wait_ge(s("var2"), L * 3 + (i + 1))
                    act.activation(RS[:, 0:T2], ps[:, 7, 0:T2], ACT.Sqrt, bias=eps2 if i == 1 else eps2x4, scale=1.0 / D
                                   ).then_inc(s("deviation2"), 1)
                    act.wait_ge(s("deviation2"), L * 3 + (i + 1))
                    act.nop().then_inc(bank_read[7], 1)

                def ffn(w, pos):
                    def silu(i, first):
                        for u in range(2):
                            act.wait_ge(us[2 * u], i + turn(pos))
                            if not first:
                                act.wait_ge(s("hidden_done"), i * 2 + at_layer("hidden_done", 22 * w + u - 1))
                            act.activation(SG[u], ps[:, 2 * u, 0:T2], ACT.Silu).then_inc(s("silu_done"), 1)

                    silu(0, True)
                    with act.Fori(1, FT // 2) as i:
                        silu(i, False)
                    act.wait_ge(s("silu_done"), at_layer("silu_done", 22 * (w + 1)))
                    for b in (0, 2):
                        act.nop().then_inc(bank_read[b], 1)

                ffn(0, 0)
                norm(0)
                act.wait_ge(s("prm2_loaded"), L * 16 + 16)
                q0 = AT_PROJ
                for j in range(3):
                    done(q0 + 1 + j)
                    ac(act.copy(CQ[:, j, :], ps[:, 1 + j, 0:T2]))
                    last = act.activation(CSQ[:, j, :], ps[:, 1 + j, 0:T2], ACT.Square)
                    if j:
                        last.then_inc(s("latent_squares"), 1)
                        act.wait_ge(s("latent_squares"), L * 2 + j)
                    else:
                        ac(last)
                    read(1 + j)
                for j in range(6):
                    done(q0 + 4 + j)
                    act.copy(XR[:, j, 3:3 + T2], ps[:, j % 4, 0:T2]).then_inc(s("conv_rows"), 1)
                    act.wait_ge(s("conv_rows"), L * 6 + (j + 1))
                    read(j % 4)
                for j in range(4):
                    done(q0 + 10 + j)
                    ac(act.copy((FQ, FK)[j // 2][:, j % 2, :], ps[:, (10 + j) % 4, 0:T2]))
                    read((10 + j) % 4)
                for j in range(2):
                    act.wait_ge(s("latent_sums"), L * 2 + (j + 1))
                    act.activation(CRS[:, j, :], ps[:, 2 + j, 0:T2], ACT.Sqrt, bias=eps2, scale=1.0 / (256 - 128 * j)
                                   ).then_inc(s("latent_deviation"), 1)
                    act.wait_ge(s("latent_deviation"), L * 2 + (j + 1))
                    read(2 + j)
                act.wait_ge(s("rows_in"), L + 1)
                ac(act.activation(LN_[0:64, :], SP[0:64, :], ACT.Abs))
                ac.join()
                ac(act.activation(LN_[0:64, :], LN_[0:64, :], ACT.Exp, scale=-1.0))
                ac(act.activation(coef[0:8, :], p2("a_log")[0:8, :], ACT.Exp))
                ac.join()
                act.activation(LN_[0:64, :], LN_[0:64, :], ACT.Ln, bias=1.0).then_inc(s("rows_ln"), 1)
                act.wait_ge(s("conv_sums"), L + 1)
                act.activation(XV.rearrange("p j t -> p (j t)"), XV.rearrange("p j t -> p (j t)"), ACT.Silu
                               ).then_inc(s("conv_ready"), 1)
                for j in range(4):
                    done(q0 + 20 + j)
                    last = ac(act.activation(ZS[:, j, :], ps[:, 3 + j, 0:T2], ACT.Silu))
                    read(3 + j)
                act.nop().then_inc(s("z_gates"), 1)
                n_out = 0
                for a_ in range(2):
                    for qt, (a, n) in enumerate(TILES):
                        nk, pb = a + n, PB[(3 * a_ + qt) % 2]
                        act.wait_ge(s("attn_exponents"), L * 6 + (3 * a_ + qt + 1))
                        act.activation(pb[0:n, :, 0:nk], pb[0:n, :, 0:nk], ACT.Exp).then_inc(s("attn_exps"), 1)
                        if qt or a_:
                            n_out = probs_out(act, L, a_ if qt else 0, qt - 1 if qt else 2, n_out)
                n_out = probs_out(act, L, 1, 2, n_out)
                for j in range(4):
                    act.wait_ge(s("attended"), L * 4 + (j + 1))
                    act.copy(MX[:, 4 + j, :], ps[:, 4 + j, 0:T2]).then_inc(s("attended_out"), 1)
                    act.wait_ge(s("attended_out"), L * 4 + (j + 1))
                    read(4 + j)
                for g in range(2):
                    for kt, (a, n) in enumerate(TILES):
                        act.wait_ge(s("ssd_exponents"), L * 6 + (3 * g + kt + 1))
                        e = EB[(3 * g + kt) % 2][0:n, :, a:T2]
                        act.activation(e, e, ACT.Exp).then_inc(s("ssd_exps"), 1)
                    act.wait_ge(s("ssd_gated"), L * 2 + (g + 1))
                    act.activation(hSQ[:, 2 * g:2 * g + 2, :], YG[:, 2 * g:2 * g + 2, :], ACT.Square
                                   ).then_inc(s("ssd_squares"), 1)
                for g in range(2):
                    act.wait_ge(s("ssd_sums"), L * 2 + (g + 1))
                    act.activation(CRS[:, g, :], ps[:, g, 0:T2], ACT.Sqrt, bias=eps2, scale=1.0 / 256
                                   ).then_inc(s("ssd_deviation"), 1)
                    act.wait_ge(s("ssd_deviation"), L * 2 + (g + 1))
                    read(g)
                norm(1)
                ffn(1, AT_FFN2)
                norm(2)

        def probs_out(act, L, a_, qt, n_out):
            a, n = TILES[qt]
            for kt in range(qt + 1):
                kn = TILES[kt][1]
                n_out += 1
                act.wait_ge(s("probs_turned"), L * 12 + n_out)
                act.copy(PT[a_][0:kn, kt, :, a:a + n], ps[0:kn, 4 + kt, :].rearrange("p (h q) -> p h q", h=4)[:, :, 0:n]
                         ).then_inc(s("probs_out"), 1)
                act.wait_ge(s("probs_out"), L * 12 + n_out)
                act.nop().then_inc(bank_read[4 + kt], 1)
            return n_out

        def pool_mixer(pool):
            pool.wait_ge(s("hT_ready"), 2)
            for k in range(KT):
                last = pool.tensor_copy(by_cols(hP[:, k, :]), to_cols(hT[:, k, 0:T1]))
            last.then_inc(s("hT_ready"), 1)
            pool.wait_ge(s("queries_decayed"), 2)
            pool.wait_ge(s("states_ready"), 3)
            pool.wait_ge(s("outputs_ready"), 1)
            pool.dma_start(AXT, io["xT"]).then_inc(s("ax_loaded"), 16)
            pool.wait_ge(s("ax_loaded"), 16)

        @block.tensor
        def _(pe):
            tensor_mixer(pe)
            tensor_peer(pe)
            tensor_layers(pe)

        @block.vector
        def _(ve):
            dv = Chain(ve, s("vector_steps"))
            vector_mixer(ve, dv)
            vector_peer(ve, dv)
            vector_layers(ve, dv)

        @block.scalar
        def _(act):
            ac = Chain(act, s("scalar_steps"))
            scalar_mixer(act, ac)
            scalar_peer(act, ac)
            scalar_layers(act, ac)

        @block.gpsimd
        def _(pool):
            pool_mixer(pool)


ARENA = 41216


def host_layout(i):
    def chan(a):
        a = np.asarray(a).reshape(-1, a.shape[-1] // P, P)
        return np.ascontiguousarray(a.transpose(2, 1, 0))

    def tiles(w):
        k, n = w.shape
        return w.reshape(k // P, P, n // P, P).transpose(2, 1, 0, 3).reshape(n // P, P, k)

    def moving(w):
        k = w.shape[0]
        return w.reshape(k // (2 * P), 2, P, 512).transpose(0, 2, 1, 3).reshape(k // (2 * P), P, 1024)

    w_in, ada = i["w_in"][0], i["w_ada"][0]
    parts = [tiles(ada[:, 0:2048])]
    for kind, a, b in (("t", 512, 1536), ("t", 2816, 3072), ("t", 2560, 2816), ("t", 0, 512), ("t", 2048, 2560),
                       ("t", 3584, 4096), ("m", 1536, 2048), ("m", 3072, 3584)):
        parts.append((tiles if kind == "t" else moving)(w_in[:, a:b]))
    parts += [tiles(ada[:, 2048:]), tiles(i["w_out"][0]), tiles(i["peer_w_query"][0])]
    out = {"stream1": np.concatenate(parts, 0), "xT": chan(i["x"][0]), "ctxT": chan(i["ctx"][0])}
    assert out["stream1"].shape[0] == STREAM1

    prm = np.zeros((P, PRM1_COLS), np.float32)

    def put(name, a):
        lo, hi = PRM1[name]
        prm[:, lo:hi] = np.asarray(a).reshape(P, hi - lo)

    put("b_ada", i["b_ada"][0].reshape(48, P).T)
    put("w_glr", w_in[:, 4096:4128].reshape(KT, P, 32).transpose(1, 0, 2))
    put("lb", i["hg_lower_bounds"][:, 0].reshape(8, P).T)
    put("b_gk", i["b_gk"][0].reshape(4, P).T)
    put("hg_norm", i["hg_norm"][0])
    put("gla_norm", i["gla_norm"][0])
    put("gamma", i["ln_gamma"][0].reshape(16, P).T)
    put("beta", i["ln_beta"][0].reshape(16, P).T)
    put("c", np.stack([i["c"][0], i["c_ctx"]], -1).reshape(KT, P, 2).transpose(1, 0, 2))
    out["prm1"] = prm
    out["wgk2"] = i["w_gk2"][0].transpose(1, 0, 2).reshape(16, 512)
    out["keysT"] = i["peer_sub_keys"][0].transpose(2, 0, 1).reshape(P, 2 * P)
    u, v = i["peer_u"][0].reshape(PN, PN, KT, P), i["peer_v"][0].reshape(PN, PN, D)
    out["peer_u"] = u.transpose(1, 3, 2, 0).reshape(PN, P, KT * PN)
    out["peer_v"] = v.transpose(1, 0, 2)
    def gate_up(g, u):
        return np.stack([tiles(g), tiles(u)], 1).reshape(N_GU, P, D)

    def down(w):
        return w.reshape(2, FT // 2, P, KT, P).transpose(3, 0, 2, 1, 4).reshape(N_DN, P, DN_COLS)

    gu, dn, proj, w_o, prms = [], [], [], [], []
    for l in range(NL):
        for w in ("ffn1", "ffn2"):
            gu.append(gate_up(i[w + "_w_gate_2"][l], i[w + "_w_up_2"][l]))
            dn.append(down(i[w + "_w_down_2"][l]))
        w = i["w_in_2"][l]
        at_ = np.cumsum([0, 512, 768, 8, 256, 256, 256, 4, 256, 128, 32])
        z, xbc, dt, fq, fk, fv, fr, cq, ckv, kr = (w[:, at_[j]:at_[j + 1]] for j in range(10))
        swap = np.r_[16:32, 0:16]
        rows = np.zeros((D, P), np.float32)
        rows[:, 0:8], rows[:, 32:36], rows[:, 64:96], rows[:, 96:128] = dt, fr, kr, kr[:, swap]
        b = np.zeros((N_PROJ2, P, 1024), np.float32)
        b[0:14] = np.concatenate([tiles(a) for a in (rows, cq, ckv, xbc, fq, fk)])
        b[14:16] = fv.reshape(2, 4, P, 256).transpose(0, 2, 1, 3).reshape(2, P, 1024)
        uq = i["mla_w_uq_2"][l].reshape(256, 4, 96)
        uq = np.concatenate([uq, uq[:, :, 64:][:, :, swap]], 2)
        b[16:18, :, 0:512] = uq.reshape(2, P, 2, 256).transpose(2, 1, 0, 3).reshape(2, P, 512)
        ukv = i["mla_w_ukv_2"][l].reshape(P, 4, 128)
        b[18, :, 0:256] = ukv[:, :, 0:64].reshape(P, 256)
        b[19, :, 0:256] = ukv[:, :, 64:].reshape(P, 256)
        b[20:24] = tiles(z)
        proj.append(b)
        w_o.append(tiles(i["w_out_2"][l]))
        pr = np.zeros((P, PRM2_COLS), np.float32)

        def put2(name, a, rows=slice(0, P)):
            lo, hi = PRM2[name]
            pr[rows, lo:hi] = a

        for nm, part in (("ln_g", "g"), ("ln_b", "b")):
            put2(nm, np.concatenate([i[f"ln{j}_{part}_2"][l].reshape(KT, P).T for j in (1, 2, 3)], 1))
        put2("conv_w", i["conv_w_2"][l].reshape(24, P).T)
        put2("conv_b", i["conv_b_2"][l].reshape(6, P).T)
        put2("d_skip", np.repeat(i["d_skip_2"][l], 64).reshape(4, P).T)
        put2("ssd_g", i["ssd_norm_g_2"][l].reshape(4, P).T)
        put2("row_bias", i["dt_bias_2"][l][:, None], slice(0, 8))
        put2("row_bias", i["fox_f_b_2"][l][:, None], slice(32, 36))
        put2("a_log", i["a_log_2"][l][:, None], slice(0, 8))
        put2("q_g", i["mla_q_norm_g_2"][l].reshape(2, P).T)
        put2("kv_g", i["mla_kv_norm_g_2"][l][:, None])
        prms.append(pr)
    out.update(gu=np.concatenate(gu), dn=np.concatenate(dn), proj2=np.concatenate(proj), out2=np.concatenate(w_o),
               prm2=np.stack(prms), metaT=chan(i["meta_2"]), const2=np.concatenate(list(constants2().values()), 1))
    out["const"] = np.concatenate(list(constants().values()), 1)
    return {k: np.ascontiguousarray(v) for k, v in out.items()}


def kernel(**inputs):
    import concourse.bacc as bacc
    from concourse.bass_utils import run_bass_kernel_spmd

    nc = bacc.Bacc("TRN2", target_bir_lowering=False, num_devices=1)
    arrays = host_layout({k: np.asarray(v) for k, v in inputs.items()})
    io = {name: nc.dram_tensor("in_" + name, a.shape, mybir.dt.from_np(a.dtype), kind="ExternalInput").ap()
          for name, a in arrays.items()}
    io["out"] = nc.dram_tensor("out", (P, KT, T1), F32, kind="ExternalOutput").ap()
    build(nc, io)
    r = run_bass_kernel_spmd(nc, [{"in_" + k: v for k, v in arrays.items()}], core_ids=[0])
    return r.results[0]["out"].transpose(2, 1, 0).reshape(1, T1, D)
```

```python
from contextlib import ExitStack

import numpy as np

import concourse.bass as bass
from concourse import mybir
from concourse.alu_op_type import AluOpType as ALU

F32 = mybir.dt.float32
F32R = mybir.dt.float32r
U32 = mybir.dt.uint32
I32 = mybir.dt.int32
ACT = mybir.ActivationFunctionType
AX = mybir.AxisListType

P = 128
D = 1024
KT = D // P
PN = 128
T1 = 256
TC = 512
SLOTS = 4
SLOT_COLS = 1408
PARTS1_AT, PARTS2_AT = 32768, 11264
PARTS2 = 2 * 8 * 272 + 2 * 22 * 272 + 4 * SLOT_COLS
ALPHA1 = 2.0 ** 0.25
EPS1 = 1e-6
LB_FLOOR = 1e-30
LN_SHIFT = 40
GRID_W = 64
GRID_R = T1 // GRID_W
HEADS = 8
GROUPS = 6
LEVELS = 8
HEAD_AT = [(h, 0, 128, h * 128, h) for h in range(4)] + [
    (4 + h // 2, 64 * (h % 2), 64, 512 + h * 128, 4 + h) for h in (0, 2, 1, 3)]

N_ADA1, N_PROJ1, N_ADA2, N_OUT1, N_WQ = 16, 32, 32, 8, 16
STREAM1 = N_ADA1 + N_PROJ1 + N_ADA2 + N_OUT1 + N_WQ

PRM1 = {}
_at = 0
for _name, _n in (("b_ada", 48), ("w_glr", KT * 32), ("lb", 8), ("b_gk", 4), ("hg_norm", 1), ("gla_norm", 1),
                  ("gamma", 16), ("beta", 16), ("c", KT * 2)):
    PRM1[_name] = (_at, _at + _n)
    _at += _n
PRM1_COLS = _at


NL = 2
T2 = 272
NMETA = 16
FT = 22
ALPHA2 = (2 * NL) ** 0.25
EPS2 = 1e-5
TILES = [(0, 16), (16, 128), (144, 128)]
NEG = -1.0e30
N_GU, N_DN, N_PROJ2, N_OUT2 = 2 * FT, 16, 24, 8
AT_PROJ = N_GU + N_DN
AT_OUT = AT_PROJ + N_PROJ2
AT_FFN2 = AT_OUT + N_OUT2
PER_LAYER = AT_FFN2 + N_GU + N_DN
BASE2 = STREAM1 + 2 * PN
PROJ_COLS = [1024] * 16 + [512, 512, 256, 256] + [1024] * 4
DN_COLS = FT // 2 * P

PRM2 = {}
_at = 0
for _name, _n in (("ln_g", 24), ("ln_b", 24), ("conv_w", 24), ("conv_b", 6), ("d_skip", 4), ("ssd_g", 4),
                  ("row_bias", 1), ("a_log", 1), ("q_g", 2), ("kv_g", 1)):
    PRM2[_name] = (_at, _at + _n)
    _at += _n
PRM2_COLS = _at


def constants2():
    f = {}
    t = np.arange(T2)
    mq, mt = [], []
    for t0, n in TILES:
        own = t0 + np.arange(P)
        mq.append(np.where(t[None, :] <= own[:, None], 0.0, NEG))
        mt.append(np.where(t[None, :] >= own[:, None], 0.0, NEG))
    f["mask_q"] = np.concatenate(mq, 1).astype(np.float32)
    f["mask_t"] = np.concatenate(mt, 1).astype(np.float32)
    inv = (1.0 / (np.float32(10000.0) ** (np.arange(0, 32, 2, dtype=np.float32) / np.float32(32)))).astype(np.float32)
    ang = (t.astype(np.float32)[None, :] * inv[:, None]).astype(np.float32)
    rope = np.zeros((P, T2), np.float32)
    rope[64:96] = np.concatenate([np.cos(ang), np.cos(ang)])
    rope[96:128] = np.concatenate([-np.sin(ang), np.sin(ang)])
    f["rope"] = rope
    sign = np.ones((P, 1), np.float32)
    sign[32:64] = -1.0
    f["sign"] = sign
    return f


CONST2 = {}
_at = 0
for _name, _arr in constants2().items():
    CONST2[_name] = (_at, _at + _arr.shape[1])
    _at += _arr.shape[1]
CONST2_COLS = _at


class Chain:

    def __init__(self, eng, sem):
        self.eng, self.sem, self.n = eng, sem, 0

    def __call__(self, ins):
        ins.then_inc(self.sem, 1)
        self.n += 1
        return ins

    def join(self):
        self.eng.wait_ge(self.sem, self.n)


def constants():
    f = {}
    i = np.arange(P)
    f["ident"] = np.eye(P, dtype=np.float32)
    f["ones"] = np.ones((P, P), np.float32)
    f["row"] = np.tile(np.arange(P, dtype=np.float32), (P, 1))
    f["row16"] = np.tile(np.arange(16, dtype=np.float32), (P, 1))
    masks = []
    for lev in range(7):
        m = 1 << lev
        same = (i[:, None] // (2 * m)) == (i[None, :] // (2 * m))
        half = ((i[:, None] // m) % 2) != ((i[None, :] // m) % 2)
        masks.append((same & half).astype(np.int32))
    masks.append(np.eye(P, dtype=np.int32))
    return f, np.concatenate(masks, 1).view(np.float32)


CONST = {}
_at = 0
for _name, _arr in constants()[0].items():
    CONST[_name] = (_at, _at + _arr.shape[1])
    _at += _arr.shape[1]
CONST_COLS = _at


def build(nc, io):
    with ExitStack() as ctx:
        def sb(name, shape, dt=F32):
            return ctx.enter_context(nc.sbuf_tensor(name, shape, dt))

        sems = {}

        def s(name):
            if name not in sems:
                sems[name] = ctx.enter_context(nc.semaphore(name))
            return sems[name]

        const = sb("const_tables", [P, CONST_COLS])
        prm1 = sb("prm1", [P, PRM1_COLS])
        keysT = sb("keysT", [P, 2 * P])
        mod = sb("mod", [P, 48, 2])
        small = sb("small", [P, 128])
        RS = sb("RS", [P, TC])
        xT = sb("xT", [P, KT, 272])
        map0 = -(-nc.sbuf_base // 64) * 64
        ring_at, arena_at = map0, map0 + 4 * SLOTS * D
        arena = nc.alloc_sbuf_tensor_at("arena", [P, ARENA], F32, offset=arena_at)

        def in_arena(name, off, shape, dt):
            return nc.alloc_sbuf_tensor_at(name, shape, dt, offset=arena_at + 4 * off)

        ring = nc.alloc_sbuf_tensor_at("ring", [P, SLOTS, D], F32, offset=ring_at)
        ring2 = nc.alloc_sbuf_tensor_at("ring2", [P, SLOTS, SLOT_COLS], F32, offset=ring_at)
        wgk2 = in_arena("wgk2", 40448, [16, 2 * 256], F32)
        masks = in_arena("masks", 40960, [P, 8 * P], F32)
        R1 = in_arena("parts1", PARTS1_AT, [P, 9216], F32R)
        R2 = in_arena("parts2", PARTS2_AT, [P, PARTS2], F32R)
        ps = ctx.enter_context(nc.psum_tensor("ps", [P, 8, 512], F32))

        def view(off, *dims):
            n = int(np.prod(dims))
            assert off + n <= ARENA
            v = arena[:, off:off + n]
            if len(dims) == 1:
                return v
            names = "abcd"[:len(dims)]
            return v.rearrange("p (" + " ".join(names) + ") -> p " + " ".join(names),
                               **{names[k]: dims[k] for k in range(1, len(dims))})

        def cst(name):
            a, b = CONST[name]
            return const[:, a:b]

        def prm(name):
            a, b = PRM1[name]
            return prm1[:, a:b]

        ident, ones, row, row16 = cst("ident"), cst("ones"), cst("row"), cst("row16")
        mask = masks[:, :].bitcast(I32).rearrange("p (l t) -> p l t", l=8)

        X = view(0, KT, TC)
        C = view(4096, KT, TC)
        SQ = view(8192, KT, TC)
        LA = view(0, 2, GROUPS, TC)
        KX = view(6144, 2, GROUPS, TC)
        hT = view(12288, KT, TC)
        hP = view(16384, KT, T1)
        PP = view(12288, 2, GROUPS, 2, T1 + 1)
        Z = view(18464, 2, GROUPS, TC)
        KE = view(18464, 2, GROUPS, T1)
        QE = view(21536, 2, GROUPS, T1)
        K = view(24608, 2, GROUPS, TC)
        Q = view(30752, GROUPS, T1)
        V = view(32288, 4, 1024)
        GT = view(36384, 8, T1)
        ST = view(38432, 12, P)
        RT = view(38432, 2, TC)
        AB = [view(3072 * b, 2, GROUPS, T1) for b in range(2)]
        SCO = view(6144, HEADS, 2, P)
        X8 = view(8192, HEADS, 2, P)
        OSQ = view(0, HEADS * T1)
        ORS = view(2048, HEADS * T1)
        ON = view(4096, HEADS, T1)
        MIX = view(10240, 8, T1)
        AXT = view(18464, KT, T1)
        MR = view(41984, 2, 4 * P)
        Y1 = view(12288, KT, T1)
        C1 = view(14336, KT, T1)
        SQ1 = view(16384, KT, T1)

        silc, sc1, sc2 = small[:, 40:56], small[:, 56:72], small[:, 76:84]
        lb_, lb1, lbA, lbC, lbt = (small[:, 8 * j:8 * j + 8] for j in range(5))
        eps1 = small[:, 74:75]
        one1 = small[:, 84:85]
        silc2 = silc.rearrange("p (k w) -> p k w", w=2)
        def to_cols(ap):
            return ap.rearrange("p (r c) -> p c r", r=GRID_R)

        def by_cols(ap):
            return ap.rearrange("p (c r) -> p c r", r=GRID_R)

        ld = [s(f"block_loaded{i}") for i in range(SLOTS)]
        us = [s(f"block_used{i}") for i in range(SLOTS)]
        bank_read = [s(f"bank_read{i}") for i in range(8)]

        def slot(n, cols=None):
            return ring[:, n % SLOTS, :] if cols is None else ring2[:, n % SLOTS, 0:cols]

        def used(eng, n):
            eng.wait_ge(us[n % SLOTS], n // SLOTS + 1)

        W = view(0, T1, PN)
        H2 = in_arena("h2", 30720, [P, KT, T1], F32)[:, :, :]
        OH = [view(41984 + 1024 * b, 2, 4, PN) for b in range(2)]
        DIF = [view(37888 + 512 * b, 4, PN) for b in range(2)]
        GEL = [view(41984 + 256 * b, T1) for b in range(2)]
        gated32 = in_arena("gated32", 42496, [P, 2, T1], F32)
        G32 = [gated32[:, b, :] for b in range(2)]

        def parts(r, off, *dims):
            n = int(np.prod(dims))
            names = "abc"[:len(dims)]
            kw = {names[k]: dims[k] for k in range(1, len(dims))}
            return [r[:, off + v * n:off + (v + 1) * n].rearrange(
                "p (" + " ".join(names) + ") -> p " + " ".join(names), **kw) for v in range(2)]

        HX = parts(R1, 0, KT, T1)
        GX = parts(R1, 4096, 2, T1)
        WX1 = parts(R1, 5120, 2, D)
        TT = view(44032, 3, T1)
        QT = view(0, 16, T1)
        S0 = view(4096, 2, 16, PN)
        S1 = view(8192, 2, 16, PN)
        TV = view(12288, 2, 16, 16)
        TI = view(12800, 2, 16, 16)
        TF = view(13312, 2, 16, 16)
        CA = view(13824, 2, 8, 256)
        CB = view(17920, 2, 8, 256)
        BV = view(22016, 2, 8, 16)
        BP = view(22272, 2, 128)
        BI = view(22528, 2, 2, 128)
        BF = view(23040, 2, 2, 128)
        EQ = view(23552, 2, 128, 16)
        PR = view(27648, 128, 16)
        CH = view(29696, 2, 3, 128)
        SM = view(30464, 2, 8)
        YS = view(0, 2, D)
        AX2 = view(4096, KT, T1)
        Y2 = view(14336, KT, T1)
        C2 = view(12288, KT, T1)
        SQ2 = view(16384, KT, T1)
        SQH = view(24576, KT, T1)

        hC = view(1536, KT, T2)
        hSQ = view(3712, KT, T2)
        hY = view(5888, KT, T2)
        SG = [view(8064 + T2 * b, T2) for b in range(2)]
        inner32 = in_arena("inner32", 8608, [P, 2, T2], F32)
        HT = [inner32[:, b, :] for b in range(2)]
        c2 = view(9152, CONST2_COLS)
        prm2 = view(11060, PRM2_COLS)
        sm2 = view(11160, 64)
        XX = parts(R2, 0, KT, T2)
        HH = parts(R2, 2 * KT * T2, FT, T2)
        WX2 = parts(R2, 2 * (KT + FT) * T2, 2, SLOT_COLS)
        ZS = view(11264, 4, T2)
        XR = view(12352, 6, T2 + 3)
        XV = view(14002, 6, T2)
        FQ = view(15634, 2, T2)
        FK = view(16178, 2, T2)
        CQ = view(16722, 3, T2)
        QM = view(17538, 4, T2)
        KM = view(18626, 4, T2)
        FV = view(19714, 3, 256)
        MV = view(20482, 3, 256)
        XD = view(21250, 3, 512)
        SP = view(22786, T2)
        AC = view(23058, T2)
        LN_ = view(23330, T2)
        TR = view(23602, 3, P)
        MX = view(23986, 8, T2)
        BI2 = view(26162, 4, T2)
        PB = [view(27250 + 1088 * b, 4, T2) for b in range(2)]
        PT = [view(29426 + 3264 * b, 3, 4, T2) for b in range(2)]
        EB = [view(35954 + 1088 * b, 4, T2) for b in range(2)]
        SE = [EB[0], EB[1], PB[1]]
        CSQ = view(38130, 3, T2)
        CRS = view(38946, 2, T2)
        KR = view(39490, 2, T2)
        YG = view(40034, 4, T2)
        maskq = c2[:, 0:3 * T2].rearrange("p (j t) -> p j t", j=3)
        maskt = c2[:, 3 * T2:6 * T2].rearrange("p (j t) -> p j t", j=3)
        rope_t = c2[:, 6 * T2:7 * T2]
        sign = c2[:, 7 * T2:7 * T2 + 1]
        coef = sm2[:, 0:1]
        eps2, eps2x4 = sm2[:, 1:2], sm2[:, 2:3]
        mxs = sm2[:, 8:16]
        sms = sm2[:, 16:24]

        def p2(name):
            a, b = PRM2[name]
            return prm2[:, a:b]

        def first_blocks(L, w):
            return (2 * PN + (N_GU + N_DN) * (2 * L + w),
                    (BASE2 + L * PER_LAYER + (AT_FFN2 if w else 0)) // SLOTS + 1)

        block = ctx.enter_context(nc.Block())

        TURNED = [1, 3, 6, 7, 9, 12]

        PER = dict(silu_done=44, hidden_done=44, y_parts=24, mean2=3, var2=3, squares2=6, centred2=6, deviation2=3,
                   normed2=3, h_ready=3)

        def peer_loads(sp):
            u, v, b0 = io["peer_u"], io["peer_v"], STREAM1 // SLOTS

            def group(m, turn, first=False, last=False):
                for b, src in enumerate((u[0] if first else v[2 * m - 1], u[2 * m + 1], v[2 * m],
                                         v[PN - 1] if last else u[2 * m + 2])):
                    sp.wait_ge(us[b], turn)
                    sp.dma_start(slot(b), src).then_inc(ld[b], 16)

            group(0, b0, first=True)
            with sp.Fori(1, PN // 2 - 1) as m:
                group(m, m + b0)
            group(PN // 2 - 1, b0 + PN // 2 - 1, last=True)

        def layer_loads(sp):
            sp.wait_ge(s("experts_out"), 4)
            sp.dma_start(c2, io["const2"]).then_inc(s("const2_loaded"), 16)
            sp.wait_ge(s("y2_ready"), 1)
            sp.dma_start(xT[:, :, 0:NMETA], io["metaT"]).then_inc(s("meta_loaded"), 16)
            for L in range(NL):
                t0 = L * (PER_LAYER // SLOTS) + BASE2 // SLOTS

                def blocks(pos, src, cols, turn=0):
                    for b in range(SLOTS):
                        sp.wait_ge(us[b], t0 + (pos // SLOTS) + turn)
                        n = cols[b] if isinstance(cols, list) else cols
                        sp.dma_start(slot(b, n), src(b)[:, 0:n]).then_inc(ld[b], 16)

                def ffn(pos, w):
                    with sp.Fori(0, N_GU // SLOTS) as i:
                        blocks(pos, lambda b: io["gu"][L * (2 * N_GU) + i * SLOTS + (w * N_GU + b)], 1024, i)
                    with sp.Fori(0, N_DN // SLOTS) as i:
                        blocks(pos + N_GU, lambda b: io["dn"][L * (2 * N_DN) + i * SLOTS + (w * N_DN + b)], DN_COLS, i)

                if L == 0:
                    sp.wait_ge(s("h_ready"), 1)
                ffn(0, 0)
                sp.wait_ge(s("h_ready"), L * 3 + 1)
                sp.dma_start(prm2, io["prm2"][L]).then_inc(s("prm2_loaded"), 16)
                for q in range(0, N_PROJ2, SLOTS):
                    blocks(AT_PROJ + q, lambda b: io["proj2"][L * N_PROJ2 + (q + b)], PROJ_COLS[q:q + SLOTS])
                for q in range(0, N_OUT2, SLOTS):
                    blocks(AT_OUT + q, lambda b: io["out2"][L * N_OUT2 + (q + b)], 1024)
                ffn(AT_FFN2, 1)

        @block.sync
        def _(sp):
            sp.dma_start(prm1[:, :], io["prm1"]).then_inc(s("small_loaded"), 16)
            sp.dma_start(X[:, :, 0:T1], io["xT"]).then_inc(s("x_loaded"), 16)
            sp.dma_start(X[:, :, T1:TC], io["ctxT"]).then_inc(s("x_loaded"), 16)
            sp.dma_start(const[:, :], io["const"]).then_inc(s("small_loaded"), 16)
            sp.dma_start(masks[:, :], io["masks"]).then_inc(s("small_loaded"), 16)
            sp.dma_start(wgk2[:, :], io["wgk2"]).then_inc(s("small_loaded"), 16)
            sp.dma_start(keysT[:, :], io["keysT"]).then_inc(s("small_loaded"), 16)
            for b in range(SLOTS):
                sp.dma_start(slot(b), io["stream1"][b]).then_inc(ld[b], 16)
            with sp.Fori(1, STREAM1 // SLOTS) as i:
                for b in range(SLOTS):
                    sp.wait_ge(us[b], i)
                    sp.dma_start(slot(b), io["stream1"][i * SLOTS + b]).then_inc(ld[b], 16)
            peer_loads(sp)
            layer_loads(sp)
            sp.wait_ge(s("h_ready"), 3 * NL + 1)
            sp.dma_start(io["out"], xT[:, :, NMETA:T2]).then_inc(s("out_stored"), 16)
            sp.wait_ge(s("out_stored"), 16)

        fills = [0] * 8

        def mm(pe, out, lhsT, rhs, start, stop):
            return pe.matmul(out, lhsT, rhs, start=start, stop=stop)

        def fill(pe, b):
            if fills[b]:
                pe.wait_ge(bank_read[b], fills[b])
            fills[b] += 1

        def norm_sums(pe, n, x, sq, T, banks, square_parts=2):
            fill(pe, banks[0])
            for k in range(KT):
                last = mm(pe, ps[:, banks[0], 0:T], ones, x[:, k, 0:T], k == 0, k == KT - 1)
            last.then_inc(s("mean_ready"), 1)
            yield
            fill(pe, banks[1])
            for h in range(2):
                pe.wait_ge(s("squares_ready"), 2 * n + h + 1)
                for k in range(4 * h, 4 * h + 4):
                    last = mm(pe, ps[:, banks[1], 0:T], ones, sq[:, k, 0:T], k == 0, k == KT - 1)
            last.then_inc(s("var_ready"), 1)

        def channel_tile(pe, n, bank, rhs, N):
            fill(pe, bank)
            pe.wait_ge(ld[n % SLOTS], 16 * (n // SLOTS + 1))
            for k in range(KT):
                last = mm(pe, ps[:, bank, 0:N], slot(n)[:, k * P:(k + 1) * P], rhs[:, k, 0:N], k == 0, k == KT - 1)
            last.then_inc(us[n % SLOTS], 1)

        def token_tiles(pe, n, bank0, rhs, tiles, signal):
            for t in range(tiles):
                fill(pe, bank0 + t)
                src = rhs(t)
                for k in range(KT):
                    if t == 0 and k % 2 == 0:
                        pe.wait_ge(ld[(n + k // 2) % SLOTS], 16 * ((n + k // 2) // SLOTS + 1))
                    w = slot(n + k // 2)[:, 512 * (k % 2):512 * (k % 2) + 512]
                    last = mm(pe, ps[:, bank0 + t, :], src(k), w, k == 0, k == KT - 1)
                    if t == tiles - 1 and k % 2 == 1:
                        last.then_inc(us[(n + k // 2) % SLOTS], 1)
                if t < tiles - 1:
                    last.then_inc(s(signal), 1)

        def modulation_tiles(pe, n, count, bank, row_banks, done):
            base = n // SLOTS
            for b in (bank, *row_banks):
                fill(pe, b)
            with pe.Fori(0, count // (2 * SLOTS)) as i:
                for u in range(2):
                    for b in range(SLOTS):
                        pe.wait_ge(ld[b], i * 32 + (base * 16 + 16 * u + 16))
                        for k in range(KT):
                            last = mm(pe, ps[0:2, row_banks[u], b * P:(b + 1) * P], silc2[:, k, :],
                                      slot(b)[:, k * P:(k + 1) * P], k == 0, k == KT - 1)
                        last.then_inc(us[b], 1)
                for u in range(2):
                    pe.wait_ge(s("mod_rows"), i * 2 + (done + u + 1))
                    pe.wait_ge(s("silu_c"), 1)
                    for b in range(SLOTS):
                        last = mm(pe, ps[:, bank, bass.ds(i * (4 * SLOTS) + 2 * (SLOTS * u + b), 2)],
                                  MR[0:2, u, b * P:(b + 1) * P], ident[0:2, 0:2], True, True)
                    last.then_inc(s("mod_turned"), 1)

        def tensor_mixer(pe):
            pe.wait_ge(s("small_loaded"), 80)
            pe.wait_ge(s("x_loaded"), 32)
            norm = norm_sums(pe, 0, X, SQ, TC, (4, 5))
            next(norm)
            pe.wait_ge(s("silu_c"), 1)
            modulation_tiles(pe, 0, N_ADA1, 0, (1, 2), 0)
            next(norm, None)
            n = N_ADA1
            pe.wait_ge(s("hT_ready"), 3)
            for j in range(8):
                channel_tile(pe, n + j, j % 4, hT, TC)
            n += 8
            wl = prm("w_glr").rearrange("p (k r) -> p k r", k=KT)
            for d in range(2):
                fill(pe, 4 + d)
                for k in range(KT):
                    last = mm(pe, ps[0:16, 4 + d, :], wl[:, k, 16 * d:16 * d + 16], hT[:, k, :], k == 0, k == KT - 1)
                last.then_inc(s("rank_rows"), 1)
            for j in range(4):
                channel_tile(pe, n + j, j, hT, TC if j < 2 else T1)
            n += 4
            pe.wait_ge(s("rank_rows_out"), 2)
            for d in range(2):
                for g in range(2):
                    fill(pe, 4 + 2 * d + g)
                    mm(pe, ps[:, 4 + 2 * d + g, :], wgk2[:, d * 256 + g * P:d * 256 + (g + 1) * P], RT[0:16, d, :],
                       True, True).then_inc(s("gla_rows"), 1)
            for j in range(12):
                channel_tile(pe, n + j, j % 4, hT, T1)
            n += 12
            token_tiles(pe, n, 0, lambda t: lambda k: hT[:, k, t * P:(t + 1) * P], 4, "v_tiles")
            n += 4

            def gla_tokens(t):
                return lambda k: hP[:, k, t * P:(t + 1) * P] if t < 2 else hT[:, k, t * P:(t + 1) * P]

            token_tiles(pe, n, 0, gla_tokens, 4, "v_tiles")
            n += 4
            modulation_tiles(pe, n, N_ADA2, 6, (4, 5), N_ADA1 // SLOTS)
            for d in range(2):
                for g in range(GROUPS):
                    j = d * GROUPS + g
                    if g % 2 == 0:
                        fill(pe, j // 2)
                    if g == 0:
                        pe.wait_ge(s("keys_decayed"), d + 1)
                    for c in range(2):
                        last = pe.transpose(ps[:, j // 2, (2 * (j % 2) + c) * P:(2 * (j % 2) + c + 1) * P],
                                            KE[:, d, g, c * P:(c + 1) * P], ident)
                    if g % 2 == 1:
                        last.then_inc(s("keys_turned"), 1)
            for d in range(2):
                fill(pe, 6 + d)
                pe.wait_ge(s("turned_out"), 3 * (d + 1))
                for h in range(4):
                    for c in range(2):
                        last = mm(pe, ps[:, 6 + d, h * P:(h + 1) * P], KE[:, d, h, c * P:(c + 1) * P],
                                  V[:, 2 + c, h * P:(h + 1) * P], c == 0, c == 1)
                last.then_inc(s("states_ready"), 1)
            fill(pe, 0)
            for d in range(2):
                for h in range(4):
                    p0 = 64 * (h % 2)
                    for c in range(2):
                        col = (d * 2 + h // 2) * P
                        last = mm(pe, ps[p0:p0 + 64, 0, col:col + P],
                                  KE[:, d, 4 + h // 2, c * P + p0:c * P + p0 + 64],
                                  V[:, 2 + c, 512 + h * P:512 + (h + 1) * P], c == 0, c == 1)
            last.then_inc(s("states_ready"), 1)
            for lev in range(LEVELS + 1):
                b0 = 4 * (lev % 2)
                for b in range(4):
                    fill(pe, b0 + b)
                pe.wait_ge(s("level_ready"), lev + 1)
                for hi, (g, p0, np_, _, _) in enumerate(HEAD_AT):
                    for c in range(2):
                        cs = 1 - c if lev == LEVELS - 1 else c
                        a = AB[lev % 2][p0:p0 + np_, 0, g, cs * P:(cs + 1) * P]
                        bb = AB[lev % 2][:, 1] if lev < LEVELS else Q
                        last = mm(pe, ps[:, b0 + hi // 2, ((hi % 2) * 2 + c) * P:((hi % 2) * 2 + c + 1) * P], a,
                                  bb[p0:p0 + np_, g, c * P:(c + 1) * P], True, True)
                last.then_inc(s("scores_ready"), 1)
            pe.wait_ge(s("scores_masked"), 1)
            pe.wait_ge(s("queries_decayed"), 2)
            pe.wait_ge(s("states_out"), 3)
            for hi, (g, p0, np_, vc, _) in enumerate(HEAD_AT):
                if hi % 2 == 0:
                    fill(pe, 4 + hi // 2)
                for c in range(2):
                    o = ps[:, 4 + hi // 2, ((hi % 2) * 2 + c) * P:((hi % 2) * 2 + c + 1) * P]
                    mm(pe, o, V[:, c, vc:vc + P], SCO[:, hi, c, :], True, False)
                    mm(pe, o, V[:, 1 - c, vc:vc + P], X8[:, hi, c, :], False, False)
                    for d in range(2):
                        sg = d * 4 + g if g < 4 else 8 + d * 2 + g - 4
                        last = mm(pe, o, ST[p0:p0 + np_, sg, :], QE[p0:p0 + np_, d, g, c * P:(c + 1) * P], False, d == 1)
            last.then_inc(s("outputs_ready"), 1)
            for b in range(4):
                fill(pe, b)
                pe.wait_ge(s("output_squares"), b + 1)
                mm(pe, ps[:, b, :], ones, OSQ[:, b * 512:(b + 1) * 512], True, True).then_inc(s("head_sums"), 1)
            pe.wait_ge(s("mix_ready"), 1)
            n = N_ADA1 + N_PROJ1 + N_ADA2
            for j in range(8):
                channel_tile(pe, n + j, j % 4, MIX, T1)
            pe.wait_ge(s("y1_ready"), 8)
            norm_products(pe, 1, Y1, SQ1, T1)

        def norm_products(pe, n, x, sq, T):
            norm = norm_sums(pe, n, x, sq, T, (4, 5))
            next(norm)
            next(norm, None)

        def tensor_peer(pe):
            pe.wait_ge(s("x1_ready"), 1)
            norm_products(pe, 2, xT, SQH, T1)
            pe.wait_ge(s("h2_ready"), 1)
            n = STREAM1 - N_WQ
            pe.wait_ge(s("h2_parts"), 2)
            for j in range(N_WQ):
                fill(pe, j % 4)
                o, w = ps[:, j % 4, 0:T1], [v[:, j % 2, :] for v in WX1]
                pe.wait_ge(s("query_hi"), j + 1)
                for k in range(KT):
                    mm(pe, o, w[0][:, k * P:(k + 1) * P], HX[0][:, k, :], k == 0, False)
                    last = mm(pe, o, w[0][:, k * P:(k + 1) * P], HX[1][:, k, :], False, False)
                last.then_inc(s("query_hi_used"), 1)
                used(pe, n + j)
                for k in range(KT):
                    last = mm(pe, o, w[1][:, k * P:(k + 1) * P], HX[0][:, k, :], False, k == KT - 1)
                last.then_inc(s("query_products"), 1)
            for tt in range(2):
                for b in range(4):
                    bank = 4 - 4 * tt + b
                    fill(pe, bank)
                    pe.wait_ge(s("queries_out"), 4 * b + 4)
                    for w in range(4):
                        hh = 4 * b + w
                        last = mm(pe, ps[:, bank, w * P:(w + 1) * P], QT[:, hh, tt * P:(tt + 1) * P],
                                  keysT[:, (hh % 2) * PN:(hh % 2 + 1) * PN], True, True)
                    last.then_inc(s("key_scores"), 1)
            for tt in range(2):
                fill(pe, 4 + tt)
                pe.wait_ge(s("choices_ready"), tt + 1)
                for w in range(3):
                    last = pe.transpose(ps[:, 4 + tt, w * P:(w + 1) * P], CH[:, tt, w, :], ident)
                last.then_inc(s("choices_turned"), 1)
            for b in range(2):
                fill(pe, b)

            def weights(i, first):
                for u in range(2):
                    if u == 0:
                        pe.wait_ge(s("first_onehots"), i + 1)
                    pe.wait_ge(s("onehots_ready"), i * 2 + (u + 1))
                    if not first:
                        pe.wait_ge(s("weights_copied"), i * 2 + (u - 1))
                    for w in range(4):
                        last = mm(pe, ps[:, u, w * P:(w + 1) * P], OH[u][:, 0, w, :],
                                  OH[u][:, 1, w, :], True, True)
                    last.then_inc(s("weights_built"), 1)

            weights(0, True)
            with pe.Fori(1, 32) as i:
                weights(i, False)

            fill(pe, 4)
            fill(pe, 5)
            t0 = STREAM1 // SLOTS

            def up(c, m, par, gelus):
                if gelus is not None:
                    pe.wait_ge(s("gelu_done"), gelus)
                pe.wait_ge(s("hi_ready"), m * 4 + (c + 1))
                o = ps[:, 4 + par, 0:T1]
                w, x = [v[:, c % 2, :] for v in WX1], HX
                for k in range(KT):
                    mm(pe, o, w[0][:, k * P:(k + 1) * P], x[0][:, k, :], k == 0, False)
                    last = mm(pe, o, w[0][:, k * P:(k + 1) * P], x[1][:, k, :], False, False)
                last.then_inc(s("hi_used"), 1)
                pe.wait_ge(us[c % SLOTS], m + (t0 + 1 + c // SLOTS))
                for k in range(KT):
                    last = mm(pe, o, w[1][:, k * P:(k + 1) * P], x[0][:, k, :], False, k == KT - 1)
                last.then_inc(s("split_products"), 1)

            def down(c, m, par, gated, start=False, stop=False):
                pe.wait_ge(s("gated"), gated)
                pe.wait_ge(s("hi_ready"), m * 4 + (c + 1))
                w = [v[:, c % 2, :] for v in WX1]

                def product(v, g, st, sp):
                    for th in range(2):
                        for dh in range(2):
                            last = mm(pe, ps[:, 2 * th + dh, :], GX[g][:, par, th * P:(th + 1) * P],
                                      w[v][:, dh * 512:(dh + 1) * 512], st, sp)
                    return last

                product(0, 0, start, False)
                product(0, 1, False, False).then_inc(s("hi_used"), 1)
                pe.wait_ge(us[c % SLOTS], m + (t0 + 1 + c // SLOTS))
                product(1, 0, False, stop).then_inc(s("split_products"), 1)

            pe.wait_ge(s("h2_parts"), 2)
            up(0, 0, 0, None)
            pe.wait_ge(s("weights_copied"), 64)

            def pair(m, first=False):
                up(1, m, 1, None if first else m * 2)
                down(2, m, 0, m * 2 + 1, start=first)
                up(3, m, 0, m * 2 + 1)
                down(4, m, 1, m * 2 + 2)

            pair(0, True)
            with pe.Fori(1, PN // 2 - 1) as m:
                pair(m)
            m = PN // 2 - 1
            up(1, m, 1, 2 * m)
            down(2, m, 0, 2 * m + 1)
            down(3, m, 1, 2 * m + 2, stop=True)
            for b in range(4):
                pe.wait_ge(s("experts_out"), 4)
                fill(pe, 4 + b)
                for w in range(2):
                    for tt in range(2):
                        k = 2 * b + w
                        last = pe.transpose(ps[:, 4 + b, (2 * w + tt) * P:(2 * w + tt + 1) * P],
                                            YS[:, tt, k * P:(k + 1) * P], ident)
                last.then_inc(s("experts_turned"), 1)
            pe.wait_ge(s("y2_ready"), 1)
            norm_products(pe, 3, Y2, SQ2, T1)

        def tensor_layers(pe):
            pe.wait_ge(s("h_ready"), 1)
            pe.wait_ge(s("meta_loaded"), 16)
            pe.wait_ge(s("const2_loaded"), 16)
            for L in range(NL):
                def fill2(b):
                    fill(pe, b)

                def at_layer(name, n):
                    return L * PER[name] + n

                def turn(pos):
                    return L * (PER_LAYER // SLOTS) + (BASE2 // SLOTS + pos // SLOTS + 1)

                def loaded(pos):
                    pe.wait_ge(ld[pos % SLOTS], 16 * turn(pos))

                def norm(i, first_part):
                    fill2(6)
                    for k in range(KT):
                        pe.wait_ge(s("y_parts"), at_layer("y_parts", first_part + k + 1))
                        last = mm(pe, ps[:, 6, 0:T2], ones, hY[:, k, :], k == 0, k == KT - 1)
                    last.then_inc(s("mean2"), 1)
                    fill2(7)
                    for h in range(2):
                        pe.wait_ge(s("squares2"), at_layer("squares2", 2 * i + h + 1))
                        for k in range(4 * h, 4 * h + 4):
                            last = mm(pe, ps[:, 7, 0:T2], ones, hSQ[:, k, :], k == 0, k == KT - 1)
                    last.then_inc(s("var2"), 1)
                    pe.wait_ge(s("h_ready"), at_layer("h_ready", i + 2))

                def ffn(w, pos):
                    for b in range(4):
                        fill2(b)

                    m0 = 2 * PN + (N_GU + N_DN) * (2 * L + w)

                    def three_pass(o, v, n_hi, n_raw, raw, x, tiles_, first=True, last_=True):
                        pe.wait_ge(s("hi_ready"), n_hi)
                        nt = len(tiles_)
                        for k, xk in enumerate(tiles_):
                            wk = WX2[0][:, v, k * P:(k + 1) * P]
                            mm(pe, o, wk, x[0][:, xk, :], first and k == 0, False)
                            last = mm(pe, o, wk, x[1][:, xk, :], False, False)
                        last.then_inc(s("hi_used"), 1)
                        pe.wait_ge(us[raw], n_raw)
                        for k, xk in enumerate(tiles_):
                            last = mm(pe, o, WX2[1][:, v, k * P:(k + 1) * P], x[0][:, xk, :], False, last_ and k == nt - 1)
                        last.then_inc(s("split_products"), 1)

                    pe.wait_ge(s("h_parts"), 4 * (2 * L + w) + 4)

                    def gate_up(i, first):
                        for u in range(2):
                            for v, name in ((0, "silu_done"), (1, "hidden_done")):
                                c = 2 * u + v
                                if not first:
                                    pe.wait_ge(s(name), i * 2 + at_layer(name, 22 * w + u - 1))
                                three_pass(ps[:, c, 0:T2], v, i * 4 + (m0 + c + 1), i + turn(pos), c, XX, range(KT))

                    gate_up(0, True)
                    with pe.Fori(1, FT // 2) as i:
                        gate_up(i, False)
                    pe.wait_ge(s("inner_parts"), FT * (2 * L + w + 1))
                    fill2(4)
                    fill2(5)

                    def down(i, first):
                        for u in range(2):
                            if not first:
                                pe.wait_ge(s("y_parts"), i * 2 + at_layer("y_parts", 16 * w + u - 1))
                            for v in range(2):
                                c = 2 * u + v
                                h = FT // 2
                                three_pass(ps[:, 4 + u, 0:T2], v, i * 4 + (m0 + N_GU + c + 1), i + turn(pos + N_GU), c,
                                           HH, range(v * h, v * h + h), v == 0, v == 1)

                    down(0, True)
                    with pe.Fori(1, 4) as i:
                        down(i, False)

                def chan(pos, bank):
                    fill2(bank)
                    loaded(pos)
                    for k in range(KT):
                        last = mm(pe, ps[:, bank, 0:T2], slot(pos, SLOT_COLS)[:, k * P:(k + 1) * P], xT[:, k, :], k == 0, k == KT - 1)
                    last.then_inc(us[pos % SLOTS], 1)

                ffn(0, 0)
                norm(0, 0)
                q0 = AT_PROJ
                for q in range(14):
                    chan(q0 + q, q % 4)
                for tt, (a, n) in enumerate(TILES):
                    fill2(4 + tt)
                    for k in range(KT):
                        pos = q0 + 14 + k // 4
                        if tt == 0 and k % 4 == 0:
                            loaded(pos)
                        last = mm(pe, ps[0:n, 4 + tt, 0:256], xT[:, k, a:a + n],
                                  slot(pos, SLOT_COLS)[:, 256 * (k % 4):256 * (k % 4) + 256], k == 0, k == KT - 1)
                        if tt == 2 and k % 4 == 3:
                            last.then_inc(us[pos % SLOTS], 1)
                    if tt < 2:
                        last.then_inc(s("fox_values"), 1)
                for j in range(2):
                    fill2(2 + j)
                    pe.wait_ge(s("latent_squares"), L * 2 + (j + 1))
                    ks = (0, 1) if j == 0 else (2,)
                    for k in ks:
                        last = mm(pe, ps[:, 2 + j, 0:T2], ones, CSQ[:, k, :], k == ks[0], k == ks[-1])
                    last.then_inc(s("latent_sums"), 1)
                pe.wait_ge(s("latents_normed"), L * 2 + 1)
                for h in range(4):
                    pos = q0 + 16 + h // 2
                    fill2(h)
                    if h % 2 == 0:
                        loaded(pos)
                    for k in range(2):
                        last = mm(pe, ps[:, h, 0:T2], slot(pos, SLOT_COLS)[:, k * 256 + (h % 2) * P:k * 256 + (h % 2 + 1) * P],
                                  CQ[:, k, :], k == 0, k == 1)
                    last.then_inc(us[pos % SLOTS] if h % 2 else s("mla_q"), 1)
                pe.wait_ge(s("latents_normed"), L * 2 + 2)
                pos = q0 + 18
                loaded(pos)
                for h in range(4):
                    fill2(4 + h)
                    last = mm(pe, ps[0:64, 4 + h, 0:T2], slot(pos, SLOT_COLS)[:, h * 64:(h + 1) * 64], CQ[:, 2, :], True, True)
                    last.then_inc(us[pos % SLOTS] if h == 3 else s("mla_k"), 1)
                pos = q0 + 19
                loaded(pos)
                for tt, (a, n) in enumerate(TILES):
                    fill2(tt)
                    last = mm(pe, ps[0:n, tt, 0:256], CQ[:, 2, a:a + n], slot(pos, SLOT_COLS)[:, 0:256], True, True)
                    last.then_inc(us[pos % SLOTS] if tt == 2 else s("mla_v"), 1)
                for j in range(4):
                    chan(q0 + 20 + j, 3 + j)
                pe.wait_ge(s("rows_ready"), L + 1)
                for tt, (a, n) in enumerate(TILES):
                    fill2(tt)
                    pe.transpose(ps[0:n, tt, 0:64], AC[0:64, a:a + n], ident[0:64, 0:64])
                    last = pe.transpose(ps[0:n, tt, 64:128], SP[0:64, a:a + n], ident[0:64, 0:64])
                    last.then_inc(s("rows_turned"), 1)
                pe.wait_ge(s("conv_ready"), L + 1)
                for tt, (a, n) in enumerate(TILES):
                    fill2(3 + tt)
                    for j in range(4):
                        last = pe.transpose(ps[0:n, 3 + tt, j * P:(j + 1) * P], XV[:, j, a:a + n], ident)
                    last.then_inc(s("x_turned"), 1)
                for h in range(4):
                    fill2(h)
                    mm(pe, ps[:, h, 0:T2], ident[0:64, 32 + h:33 + h].to_broadcast([64, P]), AC[0:64, :], True, True
                       ).then_inc(s("fox_rows"), 1)

                def logits(step):
                    a_, (a, n) = step // 3, TILES[step % 3]
                    nk = a + n
                    for h in range(4):
                        fill2(h)
                        if a_ == 0:
                            r = slice(64 * (h % 2), 64 * (h % 2) + 64)
                            last = mm(pe, ps[0:n, h, 0:nk], FQ[r, h // 2, a:a + n], FK[r, h // 2, 0:nk], True, True)
                        else:
                            last = mm(pe, ps[0:n, h, 0:nk], QM[0:96, h, a:a + n], KM[0:96, h, 0:nk], True, True)
                    last.then_inc(s("logits_ready"), 1)

                pe.wait_ge(s("attn_inputs"), L + 1)
                logits(0)
                logits(1)
                for step in range(6):
                    if step < 4:
                        logits(step + 2)
                    turn_probs(pe, L, fill2, step // 3, step % 3)

                def ssd_rows(g):
                    for h in range(4):
                        fill2(h)
                        hh = 4 * g + h
                        mm(pe, ps[:, h, 0:T2], ident[0:64, hh:hh + 1].to_broadcast([64, P]), AC[0:64, :], True, True)

                def ssd_product(g, kt):
                    a, n = TILES[kt]
                    fill2(4 + kt % 2)
                    r = slice(64 * g, 64 * g + 64)
                    mm(pe, ps[0:n, 4 + kt % 2, a:T2], XV[r, 4, a:a + n], XV[r, 5, a:T2], True, True
                       ).then_inc(s("ssd_products"), 1)

                ssd_rows(0)
                ssd_product(0, 0)
                ssd_product(0, 1)
                for a_ in range(2):
                    v = (FV, MV)[a_]
                    for pair in range(2):
                        b = 6 + pair
                        fill2(b)
                        pe.wait_ge(s("probs_out"), L * 12 + 6 * (a_ + 1))
                        for h in (2 * pair, 2 * pair + 1):
                            r = slice(64 * (h % 2), 64 * (h % 2) + 64)
                            for kt, (a, n) in enumerate(TILES):
                                last = mm(pe, ps[r, b, a:T2], v[0:n, kt, h * 64:(h + 1) * 64], PT[a_][0:n, kt, h, a:T2],
                                          kt == 0, kt == 2)
                        last.then_inc(s("attended"), 1)
                    if a_ == 0:
                        ssd_product(0, 2)
                for g in range(2):
                    if g:
                        ssd_product(1, 0)
                        ssd_product(1, 1)
                        ssd_product(1, 2)
                    fill2(6)
                    fill2(7)
                    for kt, (a, n) in enumerate(TILES):
                        if g == 0 and kt == 2:
                            ssd_rows(1)
                        pe.wait_ge(s("ssd_weights"), L * 6 + (3 * g + kt + 1))
                        for h in range(4):
                            hh = 4 * g + h
                            r = slice(64 * (h % 2), 64 * (h % 2) + 64)
                            last = pe.matmul(ps[r, 6 + h // 2, a:T2], XD[0:n, kt, hh * 64:(hh + 1) * 64],
                                             SE[kt][0:n, h, a:T2], start=kt == 0, stop=kt == 2)
                        last.then_inc(s("ssd_outputs"), 1)
                for g in range(2):
                    fill2(g)
                    pe.wait_ge(s("ssd_squares"), L * 2 + (g + 1))
                    for k in range(2):
                        last = mm(pe, ps[:, g, 0:T2], ones, hSQ[:, 2 * g + k, :], k == 0, k == 1)
                    last.then_inc(s("ssd_sums"), 1)
                pe.wait_ge(s("mixed"), L + 1)
                for j in range(8):
                    pos = AT_OUT + j
                    fill2(j % 4)
                    loaded(pos)
                    for k in range(KT):
                        last = mm(pe, ps[:, j % 4, 0:T2], slot(pos, SLOT_COLS)[:, k * P:(k + 1) * P], MX[:, k, :], k == 0, k == KT - 1)
                    last.then_inc(us[pos % SLOTS], 1)
                norm(1, 8)
                ffn(1, AT_FFN2)
                norm(2, 16)

        def turn_probs(pe, L, fill2, a_, qt):
            a, n = TILES[qt]
            pe.wait_ge(s("probs_ready"), L * 6 + (3 * a_ + qt + 1))
            for kt in range(qt + 1):
                ka, kn = TILES[kt]
                b = 4 + kt
                fill2(b)
                for h in range(4):
                    last = pe.transpose(ps[0:kn, b, h * P:h * P + n], PB[(3 * a_ + qt) % 2][0:n, h, ka:ka + kn], ident[0:n, 0:n])
                last.then_inc(s("probs_turned"), 1)

        def norm_vector(ve, dv, n, x, c, T, banks):
            ve.wait_ge(s("mean_ready"), n + 1)
            for h in range(2):
                k = slice(4 * h, 4 * h + 4)
                m = ps[:, banks[0], 0:T].unsqueeze(1).to_broadcast([P, 4, T])
                last = ve.scalar_tensor_tensor(out=c[:, k, 0:T], in0=m, scalar=-1.0 / D, in1=x[:, k, 0:T],
                                               op0=ALU.mult, op1=ALU.add)
                last.then_inc(s("centred"), 1)
            ve.wait_ge(s("centred"), 2 * n + 2)
            ve.wait_ge(s("deviation_ready"), n + 1)
            dv(ve.reciprocal(RS[:, 0:T], RS[:, 0:T]))
            dv.join()
            ve.tensor_tensor(c[:, :, 0:T], c[:, :, 0:T], RS[:, 0:T].unsqueeze(1).to_broadcast([P, KT, T]), ALU.mult
                             ).then_inc(s("normed"), 1)
            ve.wait_ge(s("normed"), n + 1)

        def vector_mixer(ve, dv):
            def bc(ap, n):
                return ap.unsqueeze(len(ap.shape)).to_broadcast([*ap.shape, n])

            dv(ve.memset(eps1, EPS1))
            dv(ve.memset(one1, 1.0))
            dv.join()
            ve.nop().then_inc(s("eps_ready"), 1)
            ve.wait_ge(s("small_loaded"), 80)
            ve.wait_ge(s("x_loaded"), 32)
            lbp = prm("lb")
            ve.tensor_tensor(lbt, lbp, lbp, ALU.subtract).then_inc(s("lb_steps"), 1)
            ve.wait_ge(s("lb_steps"), 2)
            dv(ve.reciprocal(lb1, lbt))
            dv.join()
            dv(ve.tensor_tensor(lbt, lbt, lb1, ALU.mult))
            dv.join()
            dv(ve.tensor_tensor(lb_, lbt, lbt, ALU.subtract))
            dv.join()
            dv(ve.tensor_scalar(lb_, lb_, 0.0, 1.0 - 1e-6, ALU.max, ALU.min))
            dv.join()
            dv(ve.tensor_scalar(lb1, lb_, -1.0, 1.0, ALU.mult, ALU.add))
            ve.tensor_scalar(lbA, lb_, LB_FLOOR, None, ALU.max).then_inc(s("lb_steps"), 1)
            norm_vector(ve, dv, 0, X, C, TC, (4, 5))
            ve.wait_ge(s("mod_turned"), N_ADA1 // SLOTS)
            ve.tensor_tensor(mod[:, 0:16, :], ps[:, 0, 0:32].rearrange("p (j w) -> p j w", w=2),
                             bc(prm("b_ada")[:, 0:16], 2), ALU.add).then_inc(bank_read[0], 1)
            ve.wait_ge(bank_read[0], 1)
            ve.tensor_scalar(sc1, mod[:, 8:16, :].rearrange("p k w -> p (k w)"), 1.0, None,
                             ALU.add).then_inc(s("scale_ready"), 1)
            ve.wait_ge(s("scale_ready"), 1)
            scw = sc1.rearrange("p (k w) -> p k w", w=2)
            for k in range(KT):
                last = ve.tensor_scalar(hT[:, k, 0:T1], C[:, k, 0:T1], scw[:, k, 0:1], mod[:, k, 0:1],
                                        ALU.mult, ALU.add)
            last.then_inc(s("hT_ready"), 1)
            for d in range(2):
                ve.wait_ge(s("rank_rows"), d + 1)
                ve.tensor_copy(RT[0:16, d, :], ps[0:16, 4 + d, :]).then_inc(s("rank_rows_out"), 1)
            ve.wait_ge(s("rank_rows_out"), 2)
            ve.nop().then_inc(bank_read[4], 1)
            ve.nop().then_inc(bank_read[5], 1)
            for j in range(4):
                d, g = j // 2, j % 2
                ve.wait_ge(s("gla_rows"), j + 1)
                b = prm("b_gk")[:, j:j + 1]
                ve.tensor_scalar(by_cols(Z[:, d, 4 + g, 0:T1]), to_cols(ps[:, 4 + j, 0:T1]), b, None, ALU.add)
                ve.tensor_scalar(Z[:, d, 4 + g, T1:TC], ps[:, 4 + j, T1:TC], b, None, ALU.add
                                 ).then_inc(bank_read[4 + j], 1)
            n0 = N_ADA1 + 8

            def flat(t, d, g0, g1):
                return t[:, d, g0:g1, :].rearrange("p g t -> p (g t)")

            def gate_logs(d):
                ve.wait_ge(s("gate_ln1p"), 2 * d + 1)
                ve.wait_ge(bank_read[5 + 2 * d], 1 + 2 * (d == 0))
                dv(ve.scalar_tensor_tensor(out=flat(LA, d, 0, 6), in0=flat(Z, d, 0, 6), scalar=0.0,
                                           in1=flat(LA, d, 0, 6), op0=ALU.min, op1=ALU.subtract))
                dv.join()
                dv(ve.tensor_tensor(KX[:, d, 0:4, :], LA[:, d, 0:4, :], Z[:, d, 0:4, :], ALU.subtract))
                dv(ve.tensor_tensor(LA[:, d, 0:4, :], LA[:, d, 0:4, :], bc(lbC[:, 4 * d:4 * d + 4], TC), ALU.add))
                dv(ve.tensor_scalar(flat(LA, d, 4, 6), flat(LA, d, 4, 6), 1.0 / 16.0, None, ALU.mult))
                dv.join()
                ve.tensor_tensor(Z[:, d, 0:4, :], LA[:, d, 0:4, :], bc(lbA[:, 4 * d:4 * d + 4], TC),
                                 ALU.subtract).then_inc(s("gate_diff"), 1)

            def gate_finish(d):
                ve.wait_ge(s("gate_ln1p"), 2 * d + 2)
                dv(ve.tensor_tensor(K[:, d, 0:4, :], K[:, d, 0:4, :], bc(lb1[:, 4 * d:4 * d + 4], TC), ALU.mult))
                dv(ve.tensor_tensor(LA[:, d, 0:4, :], LA[:, d, 0:4, :], bc(lbA[:, 4 * d:4 * d + 4], TC), ALU.max))
                dv.join()
                dv(ve.tensor_tensor(LA[:, d, 0:4, :], LA[:, d, 0:4, :], Z[:, d, 0:4, :], ALU.add))
                dv.join()

            ve.wait_ge(s("lb_steps"), 5)
            dv(ve.tensor_scalar(lbA, lbA, -LN_SHIFT * float(np.log(2.0)), None, ALU.add))
            dv.join()
            gate_logs(0)
            for g in range(2):
                used(ve, n0 + g)
                for d in range(2):
                    ve.tensor_copy(by_cols(K[:, d, 4 + g, 0:T1]), to_cols(ps[:, g, 0:T1]))
                    last = ve.tensor_copy(K[:, d, 4 + g, T1:TC], ps[:, g, T1:TC])
                last.then_inc(bank_read[g], 1)
            for g in range(2):
                used(ve, n0 + 2 + g)
                ve.tensor_scalar(by_cols(Q[:, 4 + g, :]), to_cols(ps[:, 2 + g, 0:T1]), 0.125, None, ALU.mult
                                 ).then_inc(bank_read[2 + g], 1)
            gate_logs(1)
            for g in range(4):
                used(ve, n0 + 4 + g)
                ve.tensor_copy(Q[:, g, :], ps[:, g, 0:T1]).then_inc(bank_read[g], 1)
            for g in range(8):
                used(ve, n0 + 8 + g)
                ve.tensor_copy(GT[:, g, :], ps[:, g % 4, 0:T1]).then_inc(bank_read[g % 4], 1)
            gate_finish(0)
            gate_finish(1)
            n1 = n0 + 16
            for w in range(2):
                for t in range(4):
                    if t < 3:
                        ve.wait_ge(s("v_tiles"), 3 * w + t + 1)
                    else:
                        used(ve, n1 + 4 * w + 3)
                    ve.tensor_copy(V[:, t, 512 * w:512 * (w + 1)], ps[:, t, :]).then_inc(bank_read[t], 1)
            dv(ve.memset(PP[:, :, :, :, 0:1].rearrange("p d g w o -> p (d g w) o"), 0.0))
            one_b = one1.to_broadcast([P, T1])
            for d in range(2):
                for g in range(GROUPS):
                    for w in range(2):
                        last = dv(ve.tensor_tensor_scan(PP[:, d, g, w, 1:T1 + 1], one_b, LA[:, d, g, w * T1:(w + 1) * T1],
                                                        0.0, ALU.mult, ALU.add))
            dv.join()
            ve.nop().then_inc(s("prefix_ready"), 1)

            end = [bc(PP[:, 0, :, 1, T1], T1), bc(PP[:, 1, :, 0, T1], T1)]
            ve.tensor_tensor(KE[:, 0], end[0], PP[:, 0, :, 1, 1:T1 + 1], ALU.subtract).then_inc(s("end_exponents"), 1)
            ve.tensor_tensor(QE[:, 1], end[1], PP[:, 1, :, 0, 0:T1], ALU.subtract).then_inc(s("end_exponents"), 1)
            for d in range(2):
                ve.wait_ge(s("end_decays"), d + 1)
                ve.tensor_tensor(KE[:, d], KE[:, d], K[:, d, :, T1:TC], ALU.mult).then_inc(s("keys_decayed"), 1)
            for d in range(2):
                ve.wait_ge(s("end_decays"), 4)
                ve.tensor_tensor(QE[:, d], QE[:, d], Q, ALU.mult).then_inc(s("queries_decayed"), 1)

            def split(ap, m):
                v = ap.rearrange("p g (b m) -> p g b m", m=2 * m)
                return v[:, :, :, 0:m], v[:, :, :, m:2 * m]

            Pf, Pb = PP[:, 0, :, 0, :], PP[:, 1, :, 0, :]

            def exponents(lev):
                m = 1 << lev
                buf = AB[lev % 2]
                if lev >= 2:
                    ve.wait_ge(s("scores_ready"), lev - 1)
                Pf1, Pb0 = split(Pf[:, :, 1:T1 + 1], m), split(Pb[:, :, 0:T1], m)

                def mid(p):
                    v = p[:, :, 0:T1].rearrange("p g (b m) -> p g b m", m=2 * m)[:, :, :, m:m + 1]
                    return v.to_broadcast([P, GROUPS, T1 // (2 * m), m])

                (k1, k2), (q1, q2) = split(buf[:, 0], m), split(buf[:, 1], m)
                ve.tensor_tensor(k1, mid(Pf), Pf1[0], ALU.subtract)
                ve.tensor_tensor(k2, Pb0[1], mid(Pb), ALU.subtract)
                ve.tensor_tensor(q1, mid(Pb), Pb0[0], ALU.subtract)
                ve.tensor_tensor(q2, Pf1[1], mid(Pf), ALU.subtract).then_inc(s("level_exponents"), 1)

            def decayed(lev):
                m = 1 << lev
                buf = AB[lev % 2]
                ve.wait_ge(s("level_decays"), lev + 1)
                (a1, a2) = split(buf[:, 0], m)
                ve.tensor_tensor(a1, a1, split(K[:, 0, :, 0:T1], m)[0], ALU.mult)
                ve.tensor_tensor(a2, a2, split(K[:, 1, :, 0:T1], m)[1], ALU.mult)
                ve.tensor_tensor(buf[:, 1], buf[:, 1], Q, ALU.mult).then_inc(s("level_ready"), 1)

            def masked(lev):
                ve.wait_ge(s("scores_ready"), lev + 1)
                b0 = 4 * (lev % 2)
                if lev == LEVELS - 1:
                    last = dv(ve.tensor_copy(X8.rearrange("p h c t -> p (h c t)"),
                                             ps[:, b0:b0 + 4, :].rearrange("p b n -> p (b n)")))
                else:
                    last = dv(ve.copy_predicated(SCO.rearrange("p h c t -> p (h c) t"),
                                                 mask[:, min(lev, 7), :].unsqueeze(1).to_broadcast([P, 16, P]),
                                                 ps[:, b0:b0 + 4, :].rearrange("p b (j t) -> p (b j) t", t=P)))
                dv.join()
                for b in range(4):
                    ve.nop().then_inc(bank_read[b0 + b], 1)

            exponents(0)
            exponents(1)
            for j in range(6):
                ve.wait_ge(s("keys_turned"), j + 1)
                d, g = j // 3, 2 * (j % 3)
                dv(ve.tensor_copy(KE[:, d, g:g + 2, :].rearrange("p g t -> p (g t)"), ps[:, j, :]))
                dv.join()
                ve.nop().then_inc(s("turned_out"), 1)
                ve.nop().then_inc(bank_read[j], 1)
            ve.wait_ge(s("mod_turned"), (N_ADA1 + N_ADA2) // SLOTS)
            ve.tensor_tensor(mod[:, 16:48, :], ps[:, 6, 0:64].rearrange("p (j w) -> p j w", w=2),
                             bc(prm("b_ada")[:, 16:48], 2), ALU.add).then_inc(bank_read[6], 1)
            for j, b in enumerate((6, 7, 0)):
                ve.wait_ge(s("states_ready"), j + 1)
                dv(ve.tensor_copy(ST[:, 4 * j:4 * j + 4, :].rearrange("p g v -> p (g v)"), ps[:, b, :]))
                dv.join()
                ve.nop().then_inc(s("states_out"), 1)
                ve.nop().then_inc(bank_read[b], 1)
            decayed(0)
            for lev in range(LEVELS):
                if lev + 1 < LEVELS:
                    decayed(lev + 1)
                masked(lev)
                if lev + 2 < LEVELS:
                    exponents(lev + 2)
            ve.wait_ge(s("scores_ready"), LEVELS - 1)
            ve.tensor_tensor(AB[0][:, 0], K[:, 0, :, 0:T1], K[:, 1, :, 0:T1], ALU.add).then_inc(s("level_ready"), 1)
            masked(LEVELS)
            ve.nop().then_inc(s("scores_masked"), 1)
            ve.wait_ge(s("keys_turned"), 6)
            for b in range(4):
                ve.wait_ge(s("head_deviation"), b + 1)
                r = ORS[:, b * 512:(b + 1) * 512]
                dv(ve.reciprocal(r, r))
                dv.join()
                dv(ve.tensor_tensor(ON[:, 2 * b:2 * b + 2, :].rearrange("p h t -> p (h t)"), ps[:, 4 + b, :], r, ALU.mult))
                dv.join()
                ve.nop().then_inc(bank_read[4 + b], 1)
            ve.wait_ge(s("gates_ready"), 1)
            for hi, (g, _, _, _, kt) in enumerate(HEAD_AT):
                o, src, gate = MIX[:, kt, :], ON[:, hi, :], GT[:, kt, :]
                gain = prm("hg_norm" if g < 4 else "gla_norm")
                if g >= 4:
                    o, gate = to_cols(o), to_cols(gate)
                    src = by_cols(src)
                last = ve.scalar_tensor_tensor(out=o, in0=src, scalar=gain, in1=gate, op0=ALU.mult, op1=ALU.mult)
            last.then_inc(s("mix_ready"), 1)
            n = N_ADA1 + N_PROJ1 + N_ADA2
            ve.wait_ge(s("ax_loaded"), 16)
            dv(ve.tensor_scalar(AXT, AXT, ALPHA1, None, ALU.mult))
            dv.join()
            for j in range(8):
                used(ve, n + j)
                dv(ve.scalar_tensor_tensor(out=Y1[:, j, :], in0=ps[:, j % 4, 0:T1], scalar=mod[:, 16 + j, 0:1],
                                           in1=AXT[:, j, :], op0=ALU.mult, op1=ALU.add))
                dv.join()
                ve.nop().then_inc(bank_read[j % 4], 1)
                ve.nop().then_inc(s("y1_ready"), 1)
            norm_vector(ve, dv, 1, Y1, C1, T1, (4, 5))
            for k in range(KT):
                last = ve.tensor_scalar(xT[:, k, 0:T1], C1[:, k, :], prm("gamma")[:, k:k + 1], prm("beta")[:, k:k + 1],
                                        ALU.mult, ALU.add)
            last.then_inc(s("x1_ready"), 1)

        def vector_peer(ve, dv):
            def bc(ap, n):
                return ap.unsqueeze(len(ap.shape)).to_broadcast([*ap.shape, n])

            dv(ve.tensor_scalar(sc2, mod[:, 32:40, 0], 1.0, None, ALU.add))
            norm_vector(ve, dv, 2, xT, H2, T1, (4, 5))
            dv.join()
            for k in range(KT):
                last = ve.tensor_scalar(H2[:, k, :], H2[:, k, :], sc2[:, k:k + 1], mod[:, 24 + k, 0:1], ALU.mult, ALU.add)
            last.then_inc(s("h2_ready"), 1)
            ve.wait_ge(s("h2_parts"), 1)
            ve.wait_ge(s("h2_ready"), 1)
            ve.tensor_tensor(HX[1], H2, HX[0], ALU.subtract).then_inc(s("h2_parts"), 1)
            for j in range(N_WQ):
                ve.wait_ge(s("query_hi"), j + 1)
                if j >= 2:
                    ve.wait_ge(s("query_products"), j - 1)
                b = STREAM1 - N_WQ + j
                ve.tensor_tensor(WX1[1][:, j % 2, :], slot(b), WX1[0][:, j % 2, :], ALU.subtract).then_inc(us[b % SLOTS], 1)

            def best16(tt, n, src, alt, vals, idx):
                for j in range(n):
                    dv(ve.max(vals[:, tt, j, 0:8], src[:, tt, j, :]))
                dv.join()
                for j in range(n):
                    dv(ve.match_replace(alt[:, tt, j, :], vals[:, tt, j, 0:8], src[:, tt, j, :], -3.0e38))
                for j in range(n):
                    dv(ve.max_index(idx[:, tt, j, 0:8], vals[:, tt, j, 0:8], src[:, tt, j, :]))
                dv.join()
                for j in range(n):
                    dv(ve.max(vals[:, tt, j, 8:16], alt[:, tt, j, :]))
                dv.join()
                for j in range(n):
                    dv(ve.max_index(idx[:, tt, j, 8:16], vals[:, tt, j, 8:16], alt[:, tt, j, :]))
                dv.join()

            for tt in range(2):
                ve.wait_ge(s("key_scores_out"), 4 * tt + 4)
                best16(tt, 16, S0, S1, TV, TI.bitcast(U32))
                dv(ve.tensor_copy(TF[:, tt], TI[:, tt].bitcast(U32)))
                tv = TV[:, tt].rearrange("p (h w) k -> p h w k", w=2)
                dv(ve.tensor_tensor(CA[:, tt].rearrange("p h (i j) -> p h i j", i=16), bc(tv[:, :, 0, :], 16),
                                    tv[:, :, 1, :].unsqueeze(2).to_broadcast([P, 8, 16, 16]), ALU.add))
                dv.join()
                best16(tt, 8, CA, CB, BV, BP.rearrange("p a (h k) -> p a h k", h=8).bitcast(U32))
                bp = BP[:, tt].bitcast(U32)
                dv(ve.tensor_scalar(BI[:, tt, 0].bitcast(U32), bp, 4, None, ALU.logical_shift_right))
                dv(ve.tensor_scalar(BI[:, tt, 1].bitcast(U32), bp, 15, None, ALU.bitwise_and))
                dv.join()
                dv(ve.tensor_copy(BF[:, tt], BI[:, tt].bitcast(U32)))
                dv.join()
                tf = TF[:, tt].rearrange("p (h w) k -> p h w k", w=2)
                for w in range(2):
                    dv(ve.tensor_tensor(EQ[:, w], bc(BF[:, tt, w], 16),
                                        row16.unsqueeze(1).to_broadcast([P, 128, 16]), ALU.is_equal))
                for w in range(2):
                    dv.join()
                    dv(ve.tensor_tensor(PR.rearrange("p (h k) i -> p h k i", h=8),
                                        EQ[:, w].rearrange("p (h k) i -> p h k i", h=8),
                                        tf[:, :, w, :].unsqueeze(2).to_broadcast([P, 8, 16, 16]), ALU.mult))
                    dv.join()
                    dv(ve.tensor_reduce(CH[:, tt, w], PR, AX.X, ALU.add))
                g = CH[:, tt, 2].rearrange("p (h k) -> p h k", h=8)
                ve.tensor_tensor(g, BV[:, tt], BV[:, tt, :, 0:1].to_broadcast([P, 8, 16]), ALU.subtract
                                 ).then_inc(s("pair_exponents"), 1)
                ve.wait_ge(s("pair_exps"), tt + 1)
                dv(ve.tensor_reduce(SM[:, tt], g, AX.X, ALU.add))
                dv.join()
                dv(ve.reciprocal(SM[:, tt], SM[:, tt]))
                dv.join()
                ve.tensor_tensor(g, g, bc(SM[:, tt], 16), ALU.mult).then_inc(s("choices_ready"), 1)
            for tt in range(2):
                ve.wait_ge(s("choices_turned"), tt + 1)
                ve.tensor_copy(TT[:, :, tt * P:(tt + 1) * P], ps[:, 4 + tt, 0:384].rearrange("p (w t) -> p w t", w=3)
                               ).then_inc(s("choices_out"), 1)
            ve.wait_ge(s("choices_out"), 2)
            for tt in range(2):
                ve.nop().then_inc(bank_read[4 + tt], 1)

            def onehots(i, first):
                for u in range(2):
                    if not first:
                        ve.wait_ge(s("weights_built"), i * 2 + (u - 1))
                    if u == 1:
                        ve.tensor_tensor(OH[1][:, 0, :, :], row.unsqueeze(1).to_broadcast([P, 4, PN]),
                                         TT[:, 0, bass.ds(i * 8 + 4, 4)].unsqueeze(2).to_broadcast([P, 4, PN]), ALU.is_equal)
                    for w in range(4):
                        t = i * 8 + (4 * u + w)
                        last = ve.tensor_scalar(OH[u][:, 1, w, :], row, TT[:, 1, bass.ds(t, 1)], TT[:, 2, bass.ds(t, 1)],
                                                ALU.is_equal, ALU.mult)
                    last.then_inc(s("onehots_ready"), 1)

            onehots(0, True)
            with ve.Fori(1, 32) as i:
                onehots(i, False)

            ve.wait_ge(s("weights_copied"), 64)
            def low(c, m, wait=True):
                ve.wait_ge(s("hi_ready"), m * 4 + (c + 1))
                if wait:
                    ve.wait_ge(s("split_products"), m * 4 + (c - 1))
                ve.tensor_tensor(WX1[1][:, c % 2, :], slot(c), WX1[0][:, c % 2, :], ALU.subtract).then_inc(us[c % SLOTS], 1)

            def gate(u, m):
                ve.wait_ge(s("gelu_done"), m * 2 + (u + 1))
                ve.tensor_tensor(G32[u], GEL[u], W[:, :, bass.ds(m * 2 + u, 1)].rearrange("p t o -> p (t o)"), ALU.mult
                                 ).then_inc(s("gate_product"), 1)
                ve.wait_ge(s("gated_hi"), m * 2 + (u + 1))
                ve.tensor_tensor(GX[1][:, u, :], G32[u], GX[0][:, u, :], ALU.subtract).then_inc(s("gated"), 1)

            low(0, 0, False)
            low(1, 0, False)

            def tile_pair(m):
                for u in range(2):
                    gate(u, m)
                    low(2 * u + 2, m)
                    low(2 * u + 3, m)

            with ve.Fori(0, PN // 2 - 1) as m:
                tile_pair(m)
            m = PN // 2 - 1
            gate(0, m)
            low(2, m)
            low(3, m)
            gate(1, m)
            ve.wait_ge(s("split_products"), 2 * PN)
            dv(ve.tensor_scalar(AX2, xT[:, :, 0:T1], ALPHA1, None, ALU.mult))
            for b in range(2):
                ve.tensor_copy(YS[:, b, :].rearrange("p (h n) -> p h n", h=2)[:, 0, :], ps[:, 2 * b, :]
                               ).then_inc(s("experts_out"), 1)
            dv.join()
            for b in range(4):
                ve.wait_ge(s("experts_turned"), b + 1)
                for w in range(2):
                    k = 2 * b + w
                    dv(ve.scalar_tensor_tensor(out=Y2[:, k, :], in0=ps[:, 4 + b, w * T1:(w + 1) * T1],
                                               scalar=mod[:, 40 + k, 0:1], in1=AX2[:, k, :], op0=ALU.mult, op1=ALU.add))
                dv.join()
                ve.nop().then_inc(bank_read[4 + b], 1)
            ve.nop().then_inc(s("y2_ready"), 1)
            norm_vector(ve, dv, 3, Y2, C2, T1, (4, 5))
            for k in range(KT):
                last = ve.tensor_scalar(xT[:, k, 16:16 + T1], C2[:, k, :], prm("gamma")[:, 8 + k:9 + k],
                                        prm("beta")[:, 8 + k:9 + k], ALU.mult, ALU.add)
            last.then_inc(s("h_ready"), 1)

        def vector_layers(ve, dv):
            def low_ahead(L, w):
                m0, _ = first_blocks(L, w)
                for c in range(2):
                    ve.wait_ge(s("hi_ready"), m0 + c + 1)
                    ve.wait_ge(s("split_products"), m0 + c - 1)
                    ve.tensor_tensor(WX2[1][:, c, 0:D], slot(c, D), WX2[0][:, c, 0:D], ALU.subtract).then_inc(us[c], 1)

            def bc(ap, n):
                return ap.unsqueeze(len(ap.shape)).to_broadcast([*ap.shape, n])

            ve.wait_ge(s("h_ready"), 1)
            dv(ve.memset(coef, -1.0))
            dv(ve.memset(eps2, EPS2))
            dv(ve.memset(eps2x4, 4 * EPS2))
            dv.join()
            ve.nop().then_inc(s("eps2_ready"), 1)
            ve.wait_ge(s("const2_loaded"), 16)
            for L in range(NL):
                def read(*banks):
                    dv.join()
                    for b in banks:
                        ve.nop().then_inc(bank_read[b], 1)

                def at_layer(name, n):
                    return L * PER[name] + n

                def turn(pos):
                    return L * (PER_LAYER // SLOTS) + (BASE2 // SLOTS + pos // SLOTS + 1)

                def done(pos):
                    ve.wait_ge(us[pos % SLOTS], turn(pos))

                def norm(i):
                    ve.wait_ge(s("mean2"), L * 3 + (i + 1))
                    for h in range(2):
                        k = slice(4 * h, 4 * h + 4)
                        ve.scalar_tensor_tensor(out=hC[:, k, :], in0=ps[:, 6, 0:T2].unsqueeze(1).to_broadcast([P, 4, T2]),
                                                scalar=-1.0 / D, in1=hY[:, k, :], op0=ALU.mult, op1=ALU.add
                                                ).then_inc(s("centred2"), 1)
                    ve.wait_ge(s("centred2"), L * 6 + (2 * i + 2))
                    ve.nop().then_inc(bank_read[6], 1)
                    ve.wait_ge(s("deviation2"), L * 3 + (i + 1))
                    dv(ve.reciprocal(RS[:, 0:T2], RS[:, 0:T2]))
                    dv.join()
                    ve.tensor_tensor(hC, hC, RS[:, 0:T2].unsqueeze(1).to_broadcast([P, KT, T2]), ALU.mult
                                     ).then_inc(s("normed2"), 1)
                    ve.wait_ge(s("normed2"), L * 3 + (i + 1))
                    for k in range(KT):
                        last = ve.tensor_scalar(xT[:, k, :], hC[:, k, :], p2("ln_g")[:, 8 * i + k:8 * i + k + 1],
                                                p2("ln_b")[:, 8 * i + k:8 * i + k + 1], ALU.mult, ALU.add)
                    last.then_inc(s("h_ready"), 1)

                def ffn(w, pos):
                    n_ffn = 2 * L + w
                    m0 = 2 * PN + (N_GU + N_DN) * n_ffn
                    for h in range(2):
                        ve.wait_ge(s("h_hi"), 2 * n_ffn + h + 1)
                        k = slice(4 * h, 4 * h + 4)
                        ve.tensor_tensor(XX[1][:, k, :], xT[:, k, :], XX[0][:, k, :], ALU.subtract
                                         ).then_inc(s("h_parts"), 2)

                    def low(c, i, at_=0, cols=D):
                        ve.wait_ge(s("hi_ready"), i * 4 + (m0 + at_ + c + 1))
                        ve.wait_ge(s("split_products"), i * 4 + (m0 + at_ + c - 1))
                        ve.tensor_tensor(WX2[1][:, c % 2, 0:cols], slot(c, cols), WX2[0][:, c % 2, 0:cols], ALU.subtract
                                         ).then_inc(us[c % SLOTS], 1)

                    def hidden(u, i):
                        ve.wait_ge(s("silu_done"), i * 2 + at_layer("silu_done", 22 * w + u + 1))
                        ve.wait_ge(s("split_products"), i * 4 + (m0 + 2 * u + 2))
                        ve.tensor_tensor(HT[u], SG[u], ps[:, 2 * u + 1, 0:T2], ALU.mult).then_inc(s("hidden_done"), 1)

                    def hidden_low(u, i):
                        ve.wait_ge(s("inner_hi"), i * 2 + (FT * n_ffn + u + 1))
                        ve.tensor_tensor(HH[1][:, bass.ds(i * 2 + u, 1), :].rearrange("p o t -> p (o t)"), HT[u],
                                         HH[0][:, bass.ds(i * 2 + u, 1), :].rearrange("p o t -> p (o t)"), ALU.subtract
                                         ).then_inc(s("inner_parts"), 1)

                    def inner_tile(u, i, cols=D):
                        low(2 * u + 2, i, cols=cols)
                        hidden(u, i)
                        low(2 * u + 3, i, cols=cols)
                        hidden_low(u, i)

                    if L == 0 and w == 0:
                        low_ahead(0, 0)
                    with ve.Fori(0, FT // 2 - 1) as i:
                        inner_tile(0, i)
                        inner_tile(1, i)
                    inner_tile(0, FT // 2 - 1)
                    inner_tile(1, FT // 2 - 1, DN_COLS)
                    for b in (1, 3):
                        ve.nop().then_inc(bank_read[b], 1)

                    def out_tile(u, i, more=True):
                        if more:
                            low(2 * u + 2, i, N_GU, DN_COLS)
                        ve.wait_ge(s("split_products"), i * 4 + (m0 + N_GU + 2 * u + 2))
                        ve.scalar_tensor_tensor(out=hY[:, bass.ds(i * 2 + u, 1), :].rearrange("p o t -> p (o t)"),
                                                in0=xT[:, bass.ds(i * 2 + u, 1), :].rearrange("p o t -> p (o t)"),
                                                scalar=2.0 * ALPHA2, in1=ps[:, 4 + u, 0:T2], op0=ALU.mult, op1=ALU.add
                                                ).then_inc(s("y_parts"), 1)
                        if more:
                            low(2 * u + 3, i, N_GU, DN_COLS)

                    with ve.Fori(0, 3) as i:
                        out_tile(0, i)
                        out_tile(1, i)
                    out_tile(0, 3)
                    out_tile(1, 3, False)
                    ve.wait_ge(s("y_parts"), at_layer("y_parts", 16 * w + 8))
                    for b in (4, 5):
                        ve.nop().then_inc(bank_read[b], 1)

                ffn(0, 0)
                ve.wait_ge(s("prm2_loaded"), L * 16 + 16)
                norm(0)
                dv(ve.memset(XR[:, :, 0:3], 0.0))
                q0 = AT_PROJ
                done(q0)
                dv(ve.tensor_scalar(SP[0:64, :], ps[0:64, 0, 0:T2], p2("row_bias")[0:64, :], sign[0:64, :], ALU.add, ALU.mult))
                dv(ve.tensor_tensor(KR[64:96, 0, :], ps[64:96, 0, 0:T2], rope_t[64:96, :], ALU.mult))
                dv(ve.tensor_tensor(KR[64:96, 1, :], ps[96:128, 0, 0:T2], rope_t[96:128, :], ALU.mult))
                read(0)
                ve.nop().then_inc(s("rows_in"), 1)
                dv(ve.tensor_tensor(KM[64:96, :, :], KR[64:96, 0:1, :].to_broadcast([32, 4, T2]),
                                    KR[64:96, 1:2, :].to_broadcast([32, 4, T2]), ALU.add))
                for j in range(2):
                    ve.wait_ge(s("latent_deviation"), L * 2 + (j + 1))
                    dv(ve.reciprocal(CRS[:, j, :], CRS[:, j, :]))
                    dv.join()
                    for k in ((0, 1) if j == 0 else (2,)):
                        g = p2("q_g")[:, k:k + 1] if j == 0 else p2("kv_g")
                        last = ve.scalar_tensor_tensor(out=CQ[:, k, :], in0=CQ[:, k, :], scalar=g, in1=CRS[:, j, :],
                                                       op0=ALU.mult, op1=ALU.mult)
                    last.then_inc(s("latents_normed"), 1)
                ve.wait_ge(s("rows_ln"), L + 1)
                dv(ve.scalar_tensor_tensor(out=SP[0:64, :], in0=SP[0:64, :], scalar=0.0, in1=LN_[0:64, :],
                                           op0=ALU.max, op1=ALU.add))
                dv(ve.tensor_scalar(coef[0:8, :], coef[0:8, :], -1.0, None, ALU.mult))
                dv.join()
                dv(ve.tensor_scalar(LN_[0:64, :], SP[0:64, :], coef[0:64, :], None, ALU.mult))
                dv.join()
                ve.tensor_tensor_scan(AC[0:64, :], one1[0:64, :].to_broadcast([64, T2]), LN_[0:64, :], 0.0,
                                      ALU.mult, ALU.add).then_inc(s("rows_ready"), 1)
                for tt, (a, n) in enumerate(TILES):
                    if tt < 2:
                        ve.wait_ge(s("fox_values"), L * 2 + (tt + 1))
                    else:
                        done(q0 + 15)
                    dv(ve.tensor_copy(FV[0:n, tt, :], ps[0:n, 4 + tt, 0:256]))
                read(4, 5, 6)
                for j in range(6):
                    ve.wait_ge(s("conv_rows"), L * 6 + (j + 1))
                    w = p2("conv_w")
                    dv(ve.tensor_scalar(XV[:, j, :], XR[:, j, 3:3 + T2], w[:, 18 + j:19 + j], p2("conv_b")[:, j:j + 1],
                                        ALU.mult, ALU.add))
                for i in range(3):
                    dv.join()
                    for j in range(6):
                        dv(ve.scalar_tensor_tensor(out=XV[:, j, :], in0=XR[:, j, i:i + T2],
                                                   scalar=p2("conv_w")[:, 6 * i + j:6 * i + j + 1],
                                                   in1=XV[:, j, :], op0=ALU.mult, op1=ALU.add))
                dv.join()
                ve.nop().then_inc(s("conv_sums"), 1)
                for h in range(4):
                    if h % 2 == 0:
                        ve.wait_ge(s("mla_q"), L * 2 + (h // 2 + 1))
                    else:
                        done(q0 + 16 + h // 2)
                    dv(ve.tensor_copy(QM[0:64, h, :], ps[0:64, h, 0:T2]))
                    dv(ve.tensor_tensor(QM[64:96, h, :], ps[64:96, h, 0:T2], rope_t[64:96, :], ALU.mult))
                    dv(ve.tensor_tensor(KR[64:96, h % 2, :], ps[96:128, h, 0:T2], rope_t[96:128, :], ALU.mult))
                    read(h)
                    dv(ve.tensor_tensor(QM[64:96, h, :], QM[64:96, h, :], KR[64:96, h % 2, :], ALU.add))
                for h in range(4):
                    if h < 3:
                        ve.wait_ge(s("mla_k"), L * 3 + (h + 1))
                    else:
                        done(q0 + 18)
                    dv(ve.tensor_copy(KM[0:64, h, :], ps[0:64, 4 + h, 0:T2]))
                read(4, 5, 6, 7)
                for tt, (a, n) in enumerate(TILES):
                    if tt < 2:
                        ve.wait_ge(s("mla_v"), L * 2 + (tt + 1))
                    else:
                        done(q0 + 19)
                    dv(ve.tensor_copy(MV[0:n, tt, :], ps[0:n, tt, 0:256]))
                read(0, 1, 2)
                for tt, (a, n) in enumerate(TILES):
                    ve.wait_ge(s("rows_turned"), L * 3 + (tt + 1))
                    dv(ve.tensor_copy(TR[0:n, tt, :], ps[0:n, tt, 0:P]))
                read(0, 1, 2)
                for tt, (a, n) in enumerate(TILES):
                    ve.wait_ge(s("x_turned"), L * 3 + (tt + 1))
                    dv(ve.tensor_tensor(XD[0:n, tt, :].rearrange("p (h d) -> p h d", h=8),
                                        ps[0:n, 3 + tt, :].rearrange("p (h d) -> p h d", h=8),
                                        bc(TR[0:n, tt, 64:72], 64), ALU.mult))
                read(3, 4, 5)
                def exponents(step):
                    a_, qt = step // 3, step % 3
                    a, n = TILES[qt]
                    if step == 0:
                        ve.wait_ge(s("fox_rows"), L * 4 + 4)
                        dv(ve.tensor_copy(BI2[:, :, :], ps[:, 0:4, 0:T2]))
                        read(0, 1, 2, 3)
                        ve.nop().then_inc(s("attn_inputs"), 1)
                    nk, pb = a + n, PB[step % 2]
                    b3 = [n, 4, nk]
                    m_ = maskq[0:n, qt, 0:nk].unsqueeze(1).to_broadcast(b3)
                    if a_ == 0:
                        dv(ve.tensor_tensor(EB[1][0:n, :, 0:nk], m_, BI2[0:n, :, 0:nk], ALU.subtract))
                        dv.join()
                        dv(ve.tensor_tensor(EB[0][0:n, :, 0:nk], EB[1][0:n, :, 0:nk], bc(TR[0:n, qt, 32:36], nk), ALU.add))
                        m_, scale = EB[0][0:n, :, 0:nk], 64.0 ** -0.5
                    else:
                        scale = 96.0 ** -0.5
                    dv.join()
                    ve.wait_ge(s("logits_ready"), L * 6 + (step + 1))
                    if step >= 2:
                        ve.wait_ge(s("probs_turned"), L * 12 + TURNED[step - 2])
                    dv(ve.scalar_tensor_tensor(out=pb[0:n, :, 0:nk], in0=ps[0:n, 0:4, 0:nk], scalar=scale,
                                               in1=m_, op0=ALU.mult, op1=ALU.add))
                    read(0, 1, 2, 3)
                    if step:
                        ve.wait_ge(s("attn_exponents"), L * 6 + step)
                    dv(ve.tensor_reduce(mxs[0:n, 0:4], pb[0:n, :, 0:nk], AX.X, ALU.max))
                    dv.join()
                    ve.tensor_tensor(pb[0:n, :, 0:nk], pb[0:n, :, 0:nk], bc(mxs[0:n, 0:4], nk), ALU.subtract
                                     ).then_inc(s("attn_exponents"), 1)

                def normalise(step):
                    a, n = TILES[step % 3]
                    nk, pb = a + n, PB[step % 2]
                    ve.wait_ge(s("attn_exps"), L * 6 + (step + 1))
                    if step:
                        ve.wait_ge(s("probs_ready"), L * 6 + step)
                    dv(ve.tensor_reduce(sms[0:n, 0:4], pb[0:n, :, 0:nk], AX.X, ALU.add))
                    dv.join()
                    dv(ve.reciprocal(sms[0:n, 0:4], sms[0:n, 0:4]))
                    dv.join()
                    ve.tensor_tensor(pb[0:n, :, 0:nk], pb[0:n, :, 0:nk], bc(sms[0:n, 0:4], nk), ALU.mult
                                     ).then_inc(s("probs_ready"), 1)

                exponents(0)
                for step in range(1, 6):
                    exponents(step)
                    normalise(step - 1)
                normalise(5)
                for g in range(2):
                    def decays(kt):
                        a, n = TILES[kt]
                        e = SE[kt]
                        ve.wait_ge(s("ssd_products"), L * 6 + (3 * g + kt + 1))
                        if g:
                            ve.wait_ge(s("ssd_outputs"), L * 6 + (kt + 1))
                        else:
                            ve.wait_ge(s("probs_ready"), L * 6 + 6)
                            ve.wait_ge(s("probs_turned"), L * 12 + 12)
                        for h in range(4):
                            dv(ve.scalar_tensor_tensor(out=e[0:n, h, a:T2], in0=ps[0:n, h, a:T2],
                                                       scalar=TR[0:n, kt, 4 * g + h:4 * g + h + 1],
                                                       in1=maskt[0:n, kt, a:T2], op0=ALU.subtract, op1=ALU.add))
                        dv.join()
                        ve.nop().then_inc(s("ssd_exponents"), 1)
                        if kt == 2:
                            read(0, 1, 2, 3)

                    def weigh(kt):
                        a, n = TILES[kt]
                        e = SE[kt]
                        ve.wait_ge(s("ssd_exps"), L * 6 + (3 * g + kt + 1))
                        dv(ve.tensor_tensor(e[0:n, :, a:T2], e[0:n, :, a:T2],
                                            ps[0:n, 4 + kt % 2, a:T2].unsqueeze(1).to_broadcast([n, 4, T2 - a]), ALU.mult))
                        read(4 + kt % 2)
                        ve.nop().then_inc(s("ssd_weights"), 1)

                    decays(0)
                    decays(1)
                    weigh(0)
                    decays(2)
                    weigh(1)
                    weigh(2)
                    ve.wait_ge(s("ssd_outputs"), L * 6 + (3 * g + 3))
                    for j in range(2):
                        k = 2 * g + j
                        dv(ve.scalar_tensor_tensor(out=YG[:, k, :], in0=XV[:, k, :], scalar=p2("d_skip")[:, k:k + 1],
                                                   in1=ps[:, 6 + j, 0:T2], op0=ALU.mult, op1=ALU.add))
                    read(6, 7)
                    ve.wait_ge(s("z_gates"), L + 1)
                    ve.tensor_tensor(YG[:, 2 * g:2 * g + 2, :], YG[:, 2 * g:2 * g + 2, :], ZS[:, 2 * g:2 * g + 2, :],
                                     ALU.mult).then_inc(s("ssd_gated"), 1)
                for g in range(2):
                    ve.wait_ge(s("ssd_deviation"), L * 2 + (g + 1))
                    dv(ve.reciprocal(CRS[:, g, :], CRS[:, g, :]))
                    dv.join()
                    for j in range(2):
                        k = 2 * g + j
                        dv(ve.scalar_tensor_tensor(out=MX[:, k, :], in0=YG[:, k, :], scalar=p2("ssd_g")[:, k:k + 1],
                                                   in1=CRS[:, g, :], op0=ALU.mult, op1=ALU.mult))
                dv.join()
                ve.wait_ge(s("attended_out"), L * 4 + 4)
                ve.nop().then_inc(s("mixed"), 1)
                for j in range(8):
                    done(AT_OUT + j)
                    dv(ve.scalar_tensor_tensor(out=hY[:, j, :], in0=xT[:, j, :], scalar=ALPHA2, in1=ps[:, j % 4, 0:T2],
                                               op0=ALU.mult, op1=ALU.add))
                    read(j % 4)
                    ve.nop().then_inc(s("y_parts"), 1)
                low_ahead(L, 1)
                norm(1)
                ffn(1, AT_FFN2)
                if L + 1 < NL:
                    low_ahead(L + 1, 0)
                norm(2)

        def modulation_rows(act, n, groups, total, row_banks):
            for i in groups:
                used(act, n + SLOTS * i + SLOTS - 1)
                act.copy(MR[0:2, i % 2, :], ps[0:2, row_banks[i % 2], :]).then_inc(s("mod_rows"), 1)
            if groups[-1] == total - 1:
                act.wait_ge(s("mod_rows"), total + (N_ADA1 // SLOTS if n else 0))
                for b in row_banks:
                    act.nop().then_inc(bank_read[b], 1)

        def norm_scalar(act, n, c, sq, T, banks, eps, scale=1.0 / D):
            for h in range(2):
                act.wait_ge(s("centred"), 2 * n + h + 1)
                if n:
                    act.wait_ge(s("var_ready"), n)
                act.activation(sq[:, 4 * h:4 * h + 4, 0:T], c[:, 4 * h:4 * h + 4, 0:T], ACT.Square
                               ).then_inc(s("squares_ready"), 1)
            if n == 0:
                modulation_rows(act, 0, range(N_ADA1 // SLOTS), N_ADA1 // SLOTS, (1, 2))
            act.wait_ge(s("var_ready"), n + 1)
            act.activation(RS[:, 0:T], ps[:, banks[1], 0:T], ACT.Sqrt, bias=eps, scale=scale
                           ).then_inc(s("deviation_ready"), 1)
            act.wait_ge(s("deviation_ready"), n + 1)
            act.nop().then_inc(bank_read[banks[0]], 1)
            act.nop().then_inc(bank_read[banks[1]], 1)

        def scalar_mixer(act, ac):
            act.wait_ge(s("small_loaded"), 80)
            act.wait_ge(s("x_loaded"), 32)
            act.wait_ge(s("eps_ready"), 1)
            act.activation(silc, prm("c"), ACT.Silu).then_inc(s("silu_c"), 1)
            act.wait_ge(s("lb_steps"), 1)
            act.activation(lbt, lbt, ACT.Exp).then_inc(s("lb_steps"), 1)
            act.wait_ge(s("lb_steps"), 3)
            act.activation(lbA, lbA, ACT.Ln, scale=2.0 ** LN_SHIFT).then_inc(s("lb_steps"), 1)
            act.activation(lbC, lb1, ACT.Ln).then_inc(s("lb_steps"), 1)
            norm_scalar(act, 0, C, SQ, TC, (4, 5), eps1)
            act.wait_ge(s("scale_ready"), 1)
            act.wait_ge(s("normed"), 1)
            scw = sc1.rearrange("p (k w) -> p k w", w=2)
            for k in range(KT):
                last = act.activation(hT[:, k, T1:TC], C[:, k, T1:TC], ACT.Identity, bias=mod[:, k, 1:2],
                                      scale=scw[:, k, 1:2])
            last.then_inc(s("hT_ready"), 1)
            for j in range(8):
                used(act, N_ADA1 + j)
                act.copy(Z[:, j // 4, j % 4, :], ps[:, j % 4, :]).then_inc(bank_read[j % 4], 1)
            act.wait_ge(bank_read[3], 2)

            def flat(t, d, g0, g1):
                return t[:, d, g0:g1, :].rearrange("p g t -> p (g t)")

            def step(*a, **k):
                ac(act.activation(*a, **k))
                ac.join()

            for d in range(2):
                act.wait_ge(bank_read[5 + 2 * d], 1 + 2 * (d == 0))
                step(flat(LA, d, 0, 6), flat(Z, d, 0, 6), ACT.Abs)
                step(flat(LA, d, 0, 6), flat(LA, d, 0, 6), ACT.Exp, scale=-1.0)
                act.activation(flat(LA, d, 0, 6), flat(LA, d, 0, 6), ACT.Ln, bias=1.0).then_inc(s("gate_ln1p"), 1)
                act.wait_ge(s("gate_diff"), d + 1)
                step(flat(K, d, 0, 4), flat(KX, d, 0, 4), ACT.Exp)
                step(flat(Z, d, 0, 4), flat(Z, d, 0, 4), ACT.Abs)
                step(flat(Z, d, 0, 4), flat(Z, d, 0, 4), ACT.Exp, scale=-1.0)
                act.activation(flat(Z, d, 0, 4), flat(Z, d, 0, 4), ACT.Ln, bias=1.0).then_inc(s("gate_ln1p"), 1)
            n, total = N_ADA1 + N_PROJ1, N_ADA2 // SLOTS
            modulation_rows(act, n, [0], total, (4, 5))
            act.wait_ge(s("prefix_ready"), 1)
            act.wait_ge(s("end_exponents"), 1)
            ef = s("end_decays")
            act.activation(KE[:, 0], KE[:, 0], ACT.Exp).then_inc(ef, 1)
            act.activation(KE[:, 1], PP[:, 1, :, 1, 0:T1], ACT.Exp).then_inc(ef, 1)
            act.activation(QE[:, 0], PP[:, 0, :, 0, 1:T1 + 1], ACT.Exp).then_inc(ef, 1)
            act.wait_ge(s("end_exponents"), 2)
            act.activation(QE[:, 1], QE[:, 1], ACT.Exp).then_inc(ef, 1)
            modulation_rows(act, n, [1], total, (4, 5))
            for lev in range(LEVELS):
                if lev == 2:
                    modulation_rows(act, n, range(2, total), total, (4, 5))
                act.wait_ge(s("level_exponents"), lev + 1)
                buf = AB[lev % 2].rearrange("p a g t -> p (a g t)")
                act.activation(buf, buf, ACT.Exp).then_inc(s("level_decays"), 1)
            gt = GT.rearrange("p k t -> p (k t)")
            act.wait_ge(s("prefix_ready"), 1)
            act.activation(gt, gt, ACT.Silu).then_inc(s("gates_ready"), 1)
            act.wait_ge(s("outputs_ready"), 1)
            for b in range(4):
                act.activation(OSQ[:, b * 512:(b + 1) * 512], ps[:, 4 + b, :], ACT.Square).then_inc(s("output_squares"), 1)
            for b in range(4):
                act.wait_ge(s("head_sums"), b + 1)
                act.activation(ORS[:, b * 512:(b + 1) * 512], ps[:, b, :], ACT.Sqrt, bias=eps1, scale=1.0 / P
                               ).then_inc(s("head_deviation"), 1)
                act.wait_ge(s("head_deviation"), b + 1)
                act.nop().then_inc(bank_read[b], 1)
            norm_scalar(act, 1, C1, SQ1, T1, (4, 5), eps1)

        def scalar_peer(act, ac):
            norm_scalar(act, 2, H2, SQH, T1, (4, 5), eps1)
            act.wait_ge(s("h2_ready"), 1)
            act.copy(HX[0], H2).then_inc(s("h2_parts"), 1)
            n = STREAM1 - N_WQ

            def query_high(j):
                act.wait_ge(ld[(n + j) % SLOTS], 16 * ((n + j) // SLOTS + 1))
                if j >= 2:
                    act.wait_ge(s("query_hi_used"), j - 1)
                    used(act, n + j - 2)
                act.copy(WX1[0][:, j % 2, :], slot(n + j)).then_inc(s("query_hi"), 1)

            query_high(0)
            query_high(1)
            for j in range(N_WQ):
                if j + 2 < N_WQ:
                    query_high(j + 2)
                act.wait_ge(s("query_products"), j + 1)
                act.copy(QT[:, j, :], ps[:, j % 4, 0:T1]).then_inc(s("queries_out"), 1)
                act.wait_ge(s("queries_out"), j + 1)
                act.nop().then_inc(bank_read[j % 4], 1)
            for tt in range(2):
                for b in range(4):
                    act.wait_ge(s("key_scores"), 4 * tt + b + 1)
                    act.copy(S0[:, tt, 4 * b:4 * b + 4, :].rearrange("p a n -> p (a n)"), ps[:, 4 - 4 * tt + b, :]
                             ).then_inc(s("key_scores_out"), 1)
            act.wait_ge(s("key_scores_out"), 8)
            for b in range(8):
                act.nop().then_inc(bank_read[b], 1)
            for tt in range(2):
                act.wait_ge(s("pair_exponents"), tt + 1)
                act.activation(CH[:, tt, 2], CH[:, tt, 2], ACT.Exp).then_inc(s("pair_exps"), 1)
            act.wait_ge(s("choices_turned"), 2)

            def copy(i, u):
                act.wait_ge(s("weights_built"), i * 2 + (u + 1))
                act.copy(W[:, bass.ds(i * 8 + 4 * u, 4), :].rearrange("p t n -> p (t n)"), ps[:, u, :]
                         ).then_inc(s("weights_copied"), 1)

            def distance(i, v):
                act.wait_ge(s("distances"), i * 2 + (v + 1))
                act.activation(OH[0][:, 0, :, :], DIF[v], ACT.Relu, bias=1.0, scale=-1.0
                               ).then_inc(s("first_onehots"), 1)

            distance(0, 0)

            def batches(i):
                copy(2 * i, 0)
                distance(i, 1)
                copy(2 * i, 1)
                copy(2 * i + 1, 0)

            with act.Fori(0, 15) as i:
                batches(i)
                distance(i + 1, 0)
                copy(2 * i + 1, 1)
            batches(15)
            copy(31, 1)
            t0 = 16 * (STREAM1 // SLOTS)

            def high(c, m, wait=True):
                act.wait_ge(ld[c % SLOTS], m * 16 + (t0 + 16 * (1 + c // SLOTS)))
                if wait:
                    act.wait_ge(s("hi_used"), m * 4 + (c - 1))
                    act.wait_ge(us[(c - 2) % SLOTS], m + (t0 // 16 + 1 + (c - 2) // SLOTS))
                act.copy(WX1[0][:, c % 2, :], slot(c)).then_inc(s("hi_ready"), 1)

            def gelu(u, m, n_up):
                act.wait_ge(s("split_products"), n_up)
                act.activation(GEL[u], ps[:, 4 + u, 0:T1], ACT.Gelu_apprx_tanh).then_inc(s("gelu_done"), 1)
                act.wait_ge(s("gate_product"), m * 2 + (u + 1))
                act.copy(GX[0][:, u, :], G32[u]).then_inc(s("gated_hi"), 1)

            high(0, 0, False)
            high(1, 0, False)

            def tile_pair(m, first=False):
                gelu(0, m, 1 if first else m * 4)
                high(2, m)
                high(3, m)
                gelu(1, m, m * 4 + 2)
                high(4, m)
                high(5, m)

            tile_pair(0, True)
            with act.Fori(1, PN // 2 - 1) as m:
                tile_pair(m)
            m = PN // 2 - 1
            gelu(0, m, 4 * m)
            high(2, m)
            high(3, m)
            gelu(1, m, 4 * m + 2)
            act.wait_ge(s("split_products"), 2 * PN)
            for b in range(2):
                act.copy(YS[:, b, :].rearrange("p (h n) -> p h n", h=2)[:, 1, :], ps[:, 2 * b + 1, :]
                         ).then_inc(s("experts_out"), 1)
            act.wait_ge(s("experts_out"), 4)
            for b in (0, 1, 4, 5):
                act.nop().then_inc(bank_read[b], 1)
            norm_scalar(act, 3, C2, SQ2, T1, (4, 5), eps1)

        def scalar_layers(act, ac):
            def high_ahead(L, w):
                m0, turn0 = first_blocks(L, w)
                for c in range(2):
                    act.wait_ge(ld[c], 16 * turn0)
                    act.wait_ge(s("hi_used"), m0 + c - 1)
                    act.wait_ge(us[c + 2], turn0 - 1)
                    act.copy(WX2[0][:, c, 0:D], slot(c, D)).then_inc(s("hi_ready"), 1)

            act.wait_ge(s("eps2_ready"), 1)
            for L in range(NL):
                def read(*banks):
                    ac.join()
                    for b in banks:
                        act.nop().then_inc(bank_read[b], 1)

                def at_layer(name, n):
                    return L * PER[name] + n

                def turn(pos):
                    return L * (PER_LAYER // SLOTS) + (BASE2 // SLOTS + pos // SLOTS + 1)

                def done(pos):
                    act.wait_ge(us[pos % SLOTS], turn(pos))

                def norm(i):
                    for h in range(2):
                        act.wait_ge(s("centred2"), L * 6 + (2 * i + h + 1))
                        act.activation(hSQ[:, 4 * h:4 * h + 4, :], hC[:, 4 * h:4 * h + 4, :], ACT.Square
                                       ).then_inc(s("squares2"), 1)
                    act.wait_ge(s("var2"), L * 3 + (i + 1))
                    act.activation(RS[:, 0:T2], ps[:, 7, 0:T2], ACT.Sqrt, bias=eps2 if i == 1 else eps2x4, scale=1.0 / D
                                   ).then_inc(s("deviation2"), 1)
                    act.wait_ge(s("deviation2"), L * 3 + (i + 1))
                    act.nop().then_inc(bank_read[7], 1)

                def ffn(w, pos):
                    n_ffn = 2 * L + w
                    m0 = 2 * PN + (N_GU + N_DN) * n_ffn
                    act.wait_ge(s("h_ready"), 3 * L + 1 + 2 * w)
                    act.wait_ge(s("meta_loaded"), 16)
                    for h in range(2):
                        k = slice(4 * h, 4 * h + 4)
                        act.copy(XX[0][:, k, :], xT[:, k, :]).then_inc(s("h_hi"), 1)

                    def high(c, i, at_=0, cols=D):
                        act.wait_ge(ld[c % SLOTS], i * 16 + (16 * (turn(pos + at_) + c // SLOTS)))
                        act.wait_ge(s("hi_used"), i * 4 + (m0 + at_ + c - 1))
                        if c >= 2:
                            act.wait_ge(us[(c - 2) % SLOTS], i + (turn(pos + at_) + (c - 2) // SLOTS))
                        act.copy(WX2[0][:, c % 2, 0:cols], slot(c, cols)).then_inc(s("hi_ready"), 1)

                    def inner_tile(u, i, cols=D):
                        act.wait_ge(s("split_products"), i * 4 + (m0 + 2 * u + 1))
                        act.activation(SG[u], ps[:, 2 * u, 0:T2], ACT.Silu).then_inc(s("silu_done"), 1)
                        high(2 * u + 2, i, cols=cols)
                        high(2 * u + 3, i, cols=cols)
                        act.wait_ge(s("hidden_done"), i * 2 + at_layer("hidden_done", 22 * w + u + 1))
                        act.copy(HH[0][:, bass.ds(i * 2 + u, 1), :].rearrange("p o t -> p (o t)"), HT[u]
                                 ).then_inc(s("inner_hi"), 1)

                    if L == 0 and w == 0:
                        high_ahead(0, 0)
                    with act.Fori(0, FT // 2 - 1) as i:
                        inner_tile(0, i)
                        inner_tile(1, i)
                    inner_tile(0, FT // 2 - 1)
                    inner_tile(1, FT // 2 - 1, DN_COLS)
                    for b in (0, 2):
                        act.nop().then_inc(bank_read[b], 1)
                    with act.Fori(0, 3) as i:
                        for c in range(2, 6):
                            high(c, i, N_GU, DN_COLS)
                    high(2, 3, N_GU, DN_COLS)
                    high(3, 3, N_GU, DN_COLS)

                ffn(0, 0)
                norm(0)
                act.wait_ge(s("prm2_loaded"), L * 16 + 16)
                q0 = AT_PROJ
                for j in range(3):
                    done(q0 + 1 + j)
                    ac(act.copy(CQ[:, j, :], ps[:, 1 + j, 0:T2]))
                    last = act.activation(CSQ[:, j, :], ps[:, 1 + j, 0:T2], ACT.Square)
                    if j:
                        last.then_inc(s("latent_squares"), 1)
                        act.wait_ge(s("latent_squares"), L * 2 + j)
                    else:
                        ac(last)
                    read(1 + j)
                for j in range(6):
                    done(q0 + 4 + j)
                    act.copy(XR[:, j, 3:3 + T2], ps[:, j % 4, 0:T2]).then_inc(s("conv_rows"), 1)
                    act.wait_ge(s("conv_rows"), L * 6 + (j + 1))
                    read(j % 4)
                for j in range(4):
                    done(q0 + 10 + j)
                    ac(act.copy((FQ, FK)[j // 2][:, j % 2, :], ps[:, (10 + j) % 4, 0:T2]))
                    read((10 + j) % 4)
                for j in range(2):
                    act.wait_ge(s("latent_sums"), L * 2 + (j + 1))
                    act.activation(CRS[:, j, :], ps[:, 2 + j, 0:T2], ACT.Sqrt, bias=eps2, scale=1.0 / (256 - 128 * j)
                                   ).then_inc(s("latent_deviation"), 1)
                    act.wait_ge(s("latent_deviation"), L * 2 + (j + 1))
                    read(2 + j)
                act.wait_ge(s("rows_in"), L + 1)
                ac(act.activation(LN_[0:64, :], SP[0:64, :], ACT.Abs))
                ac.join()
                ac(act.activation(LN_[0:64, :], LN_[0:64, :], ACT.Exp, scale=-1.0))
                ac(act.activation(coef[0:8, :], p2("a_log")[0:8, :], ACT.Exp))
                ac.join()
                act.activation(LN_[0:64, :], LN_[0:64, :], ACT.Ln, bias=1.0).then_inc(s("rows_ln"), 1)
                act.wait_ge(s("conv_sums"), L + 1)
                act.activation(XV.rearrange("p j t -> p (j t)"), XV.rearrange("p j t -> p (j t)"), ACT.Silu
                               ).then_inc(s("conv_ready"), 1)
                for j in range(4):
                    done(q0 + 20 + j)
                    last = ac(act.activation(ZS[:, j, :], ps[:, 3 + j, 0:T2], ACT.Silu))
                    read(3 + j)
                act.nop().then_inc(s("z_gates"), 1)
                n_out = 0
                for a_ in range(2):
                    for qt, (a, n) in enumerate(TILES):
                        nk, pb = a + n, PB[(3 * a_ + qt) % 2]
                        act.wait_ge(s("attn_exponents"), L * 6 + (3 * a_ + qt + 1))
                        act.activation(pb[0:n, :, 0:nk], pb[0:n, :, 0:nk], ACT.Exp).then_inc(s("attn_exps"), 1)
                        if qt or a_:
                            n_out = probs_out(act, L, a_ if qt else 0, qt - 1 if qt else 2, n_out)
                n_out = probs_out(act, L, 1, 2, n_out)
                def attended(j):
                    act.wait_ge(s("attended"), L * 4 + (j + 1))
                    act.copy(MX[:, 4 + j, :], ps[:, 6 + j % 2, 0:T2]).then_inc(s("attended_out"), 1)
                    act.wait_ge(s("attended_out"), L * 4 + (j + 1))
                    read(6 + j % 2)

                for g in range(2):
                    for kt, (a, n) in enumerate(TILES):
                        act.wait_ge(s("ssd_exponents"), L * 6 + (3 * g + kt + 1))
                        e = SE[kt][0:n, :, a:T2]
                        act.activation(e, e, ACT.Exp).then_inc(s("ssd_exps"), 1)
                        if g == 0 and kt > 0:
                            attended(2 * kt - 2)
                            attended(2 * kt - 1)
                    act.wait_ge(s("ssd_gated"), L * 2 + (g + 1))
                    act.activation(hSQ[:, 2 * g:2 * g + 2, :], YG[:, 2 * g:2 * g + 2, :], ACT.Square
                                   ).then_inc(s("ssd_squares"), 1)
                for g in range(2):
                    act.wait_ge(s("ssd_sums"), L * 2 + (g + 1))
                    act.activation(CRS[:, g, :], ps[:, g, 0:T2], ACT.Sqrt, bias=eps2, scale=1.0 / 256
                                   ).then_inc(s("ssd_deviation"), 1)
                    act.wait_ge(s("ssd_deviation"), L * 2 + (g + 1))
                    read(g)
                high_ahead(L, 1)
                norm(1)
                ffn(1, AT_FFN2)
                if L + 1 < NL:
                    high_ahead(L + 1, 0)
                norm(2)

        def probs_out(act, L, a_, qt, n_out):
            a, n = TILES[qt]
            for kt in range(qt + 1):
                kn = TILES[kt][1]
                n_out += 1
                act.wait_ge(s("probs_turned"), L * 12 + n_out)
                act.copy(PT[a_][0:kn, kt, :, a:a + n], ps[0:kn, 4 + kt, :].rearrange("p (h q) -> p h q", h=4)[:, :, 0:n]
                         ).then_inc(s("probs_out"), 1)
                act.wait_ge(s("probs_out"), L * 12 + n_out)
                act.nop().then_inc(bank_read[4 + kt], 1)
            return n_out

        def pool_mixer(pool):
            pool.wait_ge(s("hT_ready"), 2)
            for k in range(KT):
                last = pool.tensor_copy(by_cols(hP[:, k, :]), to_cols(hT[:, k, 0:T1]))
            last.then_inc(s("hT_ready"), 1)
            pool.wait_ge(s("queries_decayed"), 2)
            pool.wait_ge(s("states_ready"), 3)
            pool.wait_ge(s("outputs_ready"), 1)
            pool.dma_start(AXT, io["xT"]).then_inc(s("ax_loaded"), 16)
            pool.wait_ge(s("ax_loaded"), 16)

        def pool_peer(pool):
            pool.wait_ge(s("choices_out"), 2)

            def squares(i, v, wait=True):
                if wait:
                    pool.wait_ge(s("first_onehots"), i * 2 + (v - 1))
                d = DIF[v]
                pool.tensor_tensor(d, row.unsqueeze(1).to_broadcast([P, 4, PN]),
                                   TT[:, 0, bass.ds(i * 16 + 8 * v, 4)].unsqueeze(2).to_broadcast([P, 4, PN]),
                                   ALU.subtract).then_inc(s("differences"), 1)
                pool.wait_ge(s("differences"), i * 2 + (v + 1))
                pool.tensor_tensor(d, d, d, ALU.mult).then_inc(s("distances"), 1)

            squares(0, 0, False)
            squares(0, 1, False)
            with pool.Fori(1, 16) as i:
                squares(i, 0)
                squares(i, 1)

        @block.tensor
        def _(pe):
            tensor_mixer(pe)
            tensor_peer(pe)
            tensor_layers(pe)

        @block.vector
        def _(ve):
            dv = Chain(ve, s("vector_steps"))
            vector_mixer(ve, dv)
            vector_peer(ve, dv)
            vector_layers(ve, dv)

        @block.scalar
        def _(act):
            ac = Chain(act, s("scalar_steps"))
            scalar_mixer(act, ac)
            scalar_peer(act, ac)
            scalar_layers(act, ac)

        @block.gpsimd
        def _(pool):
            pool_mixer(pool)
            pool_peer(pool)


ARENA = 44992


def host_layout(i):
    def chan(a):
        a = np.asarray(a).reshape(-1, a.shape[-1] // P, P)
        return np.ascontiguousarray(a.transpose(2, 1, 0))

    def tiles(w):
        k, n = w.shape
        return w.reshape(k // P, P, n // P, P).transpose(2, 1, 0, 3).reshape(n // P, P, k)

    def moving(w):
        k = w.shape[0]
        return w.reshape(k // (2 * P), 2, P, 512).transpose(0, 2, 1, 3).reshape(k // (2 * P), P, 1024)

    w_in, ada = i["w_in"][0], i["w_ada"][0]
    parts = [tiles(ada[:, 0:2048])]
    for kind, a, b in (("t", 512, 1536), ("t", 2816, 3072), ("t", 2560, 2816), ("t", 0, 512), ("t", 2048, 2560),
                       ("t", 3584, 4096), ("m", 1536, 2048), ("m", 3072, 3584)):
        parts.append((tiles if kind == "t" else moving)(w_in[:, a:b]))
    parts += [tiles(ada[:, 2048:]), tiles(i["w_out"][0]), tiles(i["peer_w_query"][0])]
    out = {"stream1": np.concatenate(parts, 0), "xT": chan(i["x"][0]), "ctxT": chan(i["ctx"][0])}
    assert out["stream1"].shape[0] == STREAM1

    prm = np.zeros((P, PRM1_COLS), np.float32)

    def put(name, a):
        lo, hi = PRM1[name]
        prm[:, lo:hi] = np.asarray(a).reshape(P, hi - lo)

    put("b_ada", i["b_ada"][0].reshape(48, P).T)
    put("w_glr", w_in[:, 4096:4128].reshape(KT, P, 32).transpose(1, 0, 2))
    put("lb", i["hg_lower_bounds"][:, 0].reshape(8, P).T)
    put("b_gk", i["b_gk"][0].reshape(4, P).T)
    put("hg_norm", i["hg_norm"][0])
    put("gla_norm", i["gla_norm"][0])
    put("gamma", i["ln_gamma"][0].reshape(16, P).T)
    put("beta", i["ln_beta"][0].reshape(16, P).T)
    put("c", np.stack([i["c"][0], i["c_ctx"]], -1).reshape(KT, P, 2).transpose(1, 0, 2))
    out["prm1"] = prm
    out["wgk2"] = i["w_gk2"][0].transpose(1, 0, 2).reshape(16, 512)
    out["keysT"] = i["peer_sub_keys"][0].transpose(2, 0, 1).reshape(P, 2 * P)
    u, v = i["peer_u"][0].reshape(PN, PN, KT, P), i["peer_v"][0].reshape(PN, PN, D)
    out["peer_u"] = u.transpose(1, 3, 2, 0).reshape(PN, P, KT * PN)
    out["peer_v"] = v.transpose(1, 0, 2)
    def gate_up(g, u):
        return np.stack([tiles(g), tiles(u)], 1).reshape(N_GU, P, D)

    def down(w):
        return w.reshape(2, FT // 2, P, KT, P).transpose(3, 0, 2, 1, 4).reshape(N_DN, P, DN_COLS)

    gu, dn, proj, w_o, prms = [], [], [], [], []
    for l in range(NL):
        for w in ("ffn1", "ffn2"):
            gu.append(gate_up(i[w + "_w_gate_2"][l], i[w + "_w_up_2"][l]))
            dn.append(down(i[w + "_w_down_2"][l]))
        w = i["w_in_2"][l]
        at_ = np.cumsum([0, 512, 768, 8, 256, 256, 256, 4, 256, 128, 32])
        z, xbc, dt, fq, fk, fv, fr, cq, ckv, kr = (w[:, at_[j]:at_[j + 1]] for j in range(10))
        swap = np.r_[16:32, 0:16]
        rows = np.zeros((D, P), np.float32)
        rows[:, 0:8], rows[:, 32:36], rows[:, 64:96], rows[:, 96:128] = dt, fr, kr, kr[:, swap]
        b = np.zeros((N_PROJ2, P, 1024), np.float32)
        b[0:14] = np.concatenate([tiles(a) for a in (rows, cq, ckv, xbc, fq, fk)])
        b[14:16] = fv.reshape(2, 4, P, 256).transpose(0, 2, 1, 3).reshape(2, P, 1024)
        uq = i["mla_w_uq_2"][l].reshape(256, 4, 96)
        uq = np.concatenate([uq, uq[:, :, 64:][:, :, swap]], 2)
        b[16:18, :, 0:512] = uq.reshape(2, P, 2, 256).transpose(2, 1, 0, 3).reshape(2, P, 512)
        ukv = i["mla_w_ukv_2"][l].reshape(P, 4, 128)
        b[18, :, 0:256] = ukv[:, :, 0:64].reshape(P, 256)
        b[19, :, 0:256] = ukv[:, :, 64:].reshape(P, 256)
        b[20:24] = tiles(z)
        proj.append(b)
        w_o.append(tiles(i["w_out_2"][l]))
        pr = np.zeros((P, PRM2_COLS), np.float32)

        def put2(name, a, rows=slice(0, P)):
            lo, hi = PRM2[name]
            pr[rows, lo:hi] = a

        for nm, part in (("ln_g", "g"), ("ln_b", "b")):
            put2(nm, np.concatenate([i[f"ln{j}_{part}_2"][l].reshape(KT, P).T for j in (1, 2, 3)], 1))
        put2("conv_w", i["conv_w_2"][l].reshape(24, P).T)
        put2("conv_b", i["conv_b_2"][l].reshape(6, P).T)
        put2("d_skip", np.repeat(i["d_skip_2"][l], 64).reshape(4, P).T)
        put2("ssd_g", i["ssd_norm_g_2"][l].reshape(4, P).T)
        put2("row_bias", i["dt_bias_2"][l][:, None], slice(0, 8))
        put2("row_bias", i["fox_f_b_2"][l][:, None], slice(32, 36))
        put2("a_log", i["a_log_2"][l][:, None], slice(0, 8))
        put2("q_g", i["mla_q_norm_g_2"][l].reshape(2, P).T)
        put2("kv_g", i["mla_kv_norm_g_2"][l][:, None])
        prms.append(pr)
    out.update(gu=np.concatenate(gu), dn=np.concatenate(dn), proj2=np.concatenate(proj), out2=np.concatenate(w_o),
               prm2=np.stack(prms), metaT=chan(i["meta_2"]), const2=np.concatenate(list(constants2().values()), 1))
    tables, out["masks"] = constants()
    out["const"] = np.concatenate(list(tables.values()), 1)
    return {k: np.ascontiguousarray(v) for k, v in out.items()}


def kernel(**inputs):
    import concourse.bacc as bacc
    from concourse.bass_utils import run_bass_kernel_spmd

    nc = bacc.Bacc("TRN2", target_bir_lowering=False, num_devices=1)
    arrays = host_layout({k: np.asarray(v) for k, v in inputs.items()})
    io = {name: nc.dram_tensor("in_" + name, a.shape, mybir.dt.from_np(a.dtype), kind="ExternalInput").ap()
          for name, a in arrays.items()}
    io["out"] = nc.dram_tensor("out", (P, KT, T1), F32, kind="ExternalOutput").ap()
    build(nc, io)
    r = run_bass_kernel_spmd(nc, [{"in_" + k: v for k, v in arrays.items()}], core_ids=[0])
    return r.results[0]["out"].transpose(2, 1, 0).reshape(1, T1, D)
```
